# Optimizing a Trainium2 kernel written in Bass

```python
import math
import jax
import jax.numpy as jnp
from jax import lax
import numpy as np

D_MODEL = 1024
BATCH = 1
SEQ = 128
DEPTH = 4
DEC_BATCH = 1
DEC_SEQ = 256
PAST_LEN = 128

GRID_W = 64
N_MIXERS = 3
N_GDN = (DEPTH + 2) // 3
N_GQA = (DEPTH + 1) // 3
N_MLA = DEPTH // 3

GDN_HEADS = 8
GDN_DK = 128
GDN_DV = 128
GDN_CONV = 5
GDN_CHUNK = 64
GDN_QKV = GDN_HEADS * (2 * GDN_DK + GDN_DV)
GDN_IN = GDN_QKV + GDN_HEADS * GDN_DV + 4 * GDN_HEADS
DT_MIN = 0.001
DT_MAX = 0.1

GQA_HEADS = 8
GQA_KV_HEADS = 2
GQA_GROUP = GQA_HEADS // GQA_KV_HEADS
GQA_HEAD_DIM = 128
GQA_IN = (GQA_HEADS + 2 * GQA_KV_HEADS) * GQA_HEAD_DIM

MLA_HEADS = 8
MLA_Q_LORA = 512
MLA_KV_LORA = 256
MLA_NOPE = 128
MLA_ROPE = 64
MLA_V = 128
MLA_IN = MLA_Q_LORA + MLA_KV_LORA + MLA_ROPE

N_EXPERTS = 16
N_GROUPS = 4
EXPERTS_PER_GROUP = N_EXPERTS // N_GROUPS
GROUP_SCORE_TOPK = 2
TOP_K = 2
D_EXPERT = 256

ROPE_THETA = 10000.0
Q_BLOCK = 128
ALPHA = (2 * DEPTH) ** 0.25
BETA_INIT = (8 * DEPTH) ** -0.25
NORM_EPS = 1e-6

kernel_name = "hybrid_flow_trunk_ctx_prefix_step"

def _layer_norm(x, g, b):
    xf = x.astype(jnp.float32)
    mu = jnp.mean(xf, axis=-1, keepdims=True)
    var = jnp.mean(jnp.square(xf - mu), axis=-1, keepdims=True)
    return ((xf - mu) * lax.rsqrt(var + NORM_EPS)).astype(x.dtype) * g + b

def _rms_norm(x, g):
    xf = x.astype(jnp.float32)
    y = xf * lax.rsqrt(jnp.mean(jnp.square(xf), axis=-1, keepdims=True) + NORM_EPS)
    return y.astype(x.dtype) * g

def _l2_normalize(x):
    return x * lax.rsqrt(jnp.sum(jnp.square(x), axis=-1, keepdims=True) + NORM_EPS)

def _modulate(x, shift, scale):
    return x * (1 + scale[:, None]) + shift[:, None]

def _grid_angles(n_tokens, rot_dim):
    n_rows = n_tokens // GRID_W
    row = jnp.repeat(jnp.arange(n_rows, dtype=jnp.float32), GRID_W)
    col = jnp.tile(jnp.arange(GRID_W, dtype=jnp.float32), n_rows)
    n_freq = rot_dim // 4
    inv_freq = ROPE_THETA ** (-jnp.arange(n_freq, dtype=jnp.float32) / n_freq)
    return row[:, None] * inv_freq, col[:, None] * inv_freq

def _rope_half(x, ang):
    ang = ang.reshape(ang.shape[0], *([1] * (x.ndim - 3)), ang.shape[1])
    cos, sin = jnp.cos(ang).astype(x.dtype), jnp.sin(ang).astype(x.dtype)
    x1, x2 = jnp.split(x, 2, axis=-1)
    return jnp.concatenate([x1 * cos - x2 * sin, x2 * cos + x1 * sin], axis=-1)

def _axial_rope(x, row_ang, col_ang):
    half = x.shape[-1] // 2
    return jnp.concatenate([_rope_half(x[..., :half], row_ang), _rope_half(x[..., half:], col_ang)], axis=-1)

def _short_conv(x, w):
    pad = GDN_CONV // 2
    return lax.conv_general_dilated(
        x, w[:, None, :].astype(x.dtype), window_strides=(1,), padding=[(pad, pad)],
        dimension_numbers=("NWC", "WIO", "NWC"), feature_group_count=x.shape[-1])

def _chunk_gated_delta(q, k, v, g, beta, s0):
    B, N, H, _ = q.shape
    dv = v.shape[-1]
    C = GDN_CHUNK
    nc = N // C

    def to_chunks(t):
        t = t.reshape(B, nc, C, H, *t.shape[3:])
        return jnp.moveaxis(jnp.swapaxes(t, 2, 3), 1, 0)

    q, k, v, g, beta = (to_chunks(t) for t in (q, k, v, g, beta))
    g = jnp.cumsum(g, axis=-1)
    idx = jnp.arange(C)
    causal = idx[:, None] >= idx[None, :]
    strict = idx[:, None] > idx[None, :]
    decay = jnp.exp(jnp.where(causal, g[..., :, None] - g[..., None, :], -jnp.inf))
    kb = k * beta[..., None]
    a = jnp.where(strict, jnp.einsum("nbhid,nbhjd->nbhij", kb, k) * decay, 0.0)
    lower = a + jnp.eye(C, dtype=a.dtype)
    rhs = jnp.concatenate([v * beta[..., None], kb * jnp.exp(g)[..., None]], axis=-1)
    sol = lax.linalg.triangular_solve(lower, rhs, left_side=True, lower=True, unit_diagonal=True)
    u, w = sol[..., :dv], sol[..., dv:]
    qk = jnp.einsum("nbhid,nbhjd->nbhij", q, k) * decay

    def step(state, xs):
        q_c, k_c, u_c, w_c, g_c, qk_c = xs
        v_new = u_c - jnp.einsum("bhcd,bhde->bhce", w_c, state)
        o_c = (jnp.einsum("bhcd,bhde->bhce", q_c * jnp.exp(g_c)[..., None], state)
               + jnp.einsum("bhij,bhje->bhie", qk_c, v_new))
        g_last = g_c[..., -1:]
        state = (state * jnp.exp(g_last)[..., None]
                 + jnp.einsum("bhcd,bhce->bhde", k_c * jnp.exp(g_last - g_c)[..., None], v_new))
        return state, o_c

    s_final, o = lax.scan(step, s0, (q, k, u, w, g, qk))
    o = jnp.moveaxis(o, 0, 1)
    return jnp.swapaxes(o, 2, 3).reshape(B, N, H, dv), s_final

def _blocked_attention(q, k, v, scale):
    B, Nq = q.shape[:2]
    nb = Nq // Q_BLOCK
    qb = jnp.moveaxis(q.reshape(B, nb, Q_BLOCK, *q.shape[2:]), 1, 0)

    def attend(qi):
        s = jnp.einsum("bqhgd,bkhd->bhgqk", qi, k).astype(jnp.float32) * scale
        p = jax.nn.softmax(s, axis=-1).astype(v.dtype)
        return jnp.einsum("bhgqk,bkhe->bqhge", p, v)

    o = lax.map(attend, qb)
    return jnp.moveaxis(o, 0, 1).reshape(B, Nq, *o.shape[3:])

def _gdn_mixer(h, s0, w_in, conv_w, a_log, dt_bias, norm_g, w_out):
    B, N, _ = h.shape
    proj = h @ w_in
    qkv = jax.nn.silu(_short_conv(proj[..., :GDN_QKV], conv_w))
    nqk = GDN_HEADS * GDN_DK
    q = qkv[..., :nqk].reshape(B, N, GDN_HEADS, GDN_DK)
    k = qkv[..., nqk:2 * nqk].reshape(B, N, GDN_HEADS, GDN_DK)
    v = qkv[..., 2 * nqk:].reshape(B, N, GDN_HEADS, GDN_DV)
    z = proj[..., GDN_QKV:GDN_QKV + GDN_HEADS * GDN_DV].reshape(B, N, GDN_HEADS, GDN_DV)
    ab = proj[..., GDN_QKV + GDN_HEADS * GDN_DV:].astype(jnp.float32).reshape(B, N, 2, 2, GDN_HEADS)
    g = -jnp.exp(a_log.astype(jnp.float32)) * jax.nn.softplus(ab[:, :, 0] + dt_bias.astype(jnp.float32))
    beta = jax.nn.sigmoid(ab[:, :, 1])
    qf = _l2_normalize(q.astype(jnp.float32)) * GDN_DK ** -0.5
    kf = _l2_normalize(k.astype(jnp.float32))
    vf = v.astype(jnp.float32)
    s0f = s0.astype(jnp.float32)
    o_f, s_f = _chunk_gated_delta(qf, kf, vf, g[:, :, 0], beta[:, :, 0], s0f[:, 0])
    rev = lambda t: jnp.flip(t, axis=1)
    o_b, s_b = _chunk_gated_delta(rev(qf), rev(kf), rev(vf), rev(g[:, :, 1]), rev(beta[:, :, 1]), s0f[:, 1])
    o = (o_f + rev(o_b)).astype(h.dtype)
    o = _rms_norm(o, norm_g) * jax.nn.silu(z)
    out = o.reshape(B, N, GDN_HEADS * GDN_DV) @ w_out
    return out, jnp.stack([s_f, s_b], axis=1).astype(h.dtype)

def _gqa_mixer(h, angles, ctx_k, ctx_v, w_in, q_norm, k_norm, w_out):
    B, N, _ = h.shape
    proj = h @ w_in
    nq = GQA_HEADS * GQA_HEAD_DIM
    nkv = GQA_KV_HEADS * GQA_HEAD_DIM
    q = _rms_norm(proj[..., :nq].reshape(B, N, GQA_KV_HEADS, GQA_GROUP, GQA_HEAD_DIM), q_norm)
    k = _rms_norm(proj[..., nq:nq + nkv].reshape(B, N, GQA_KV_HEADS, GQA_HEAD_DIM), k_norm)
    v = proj[..., nq + nkv:].reshape(B, N, GQA_KV_HEADS, GQA_HEAD_DIM)
    if angles is None:
        k_all, v_all = k, v
    else:
        q = _axial_rope(q, *angles)
        k_all = jnp.concatenate([ctx_k, _axial_rope(k, *angles)], axis=1)
        v_all = jnp.concatenate([ctx_v, v], axis=1)
    o = _blocked_attention(q, k_all, v_all, GQA_HEAD_DIM ** -0.5)
    return o.reshape(B, N, nq) @ w_out, k, v

def _mla_mixer(h, angles, ctx_ckv, ctx_krope, w_in, q_norm, kv_norm, w_q_up, w_kv_up, w_out):
    B, N, _ = h.shape
    proj = h @ w_in
    cq = _rms_norm(proj[..., :MLA_Q_LORA], q_norm)
    ckv = _rms_norm(proj[..., MLA_Q_LORA:MLA_Q_LORA + MLA_KV_LORA], kv_norm)
    krope = proj[..., MLA_Q_LORA + MLA_KV_LORA:]
    q = (cq @ w_q_up).reshape(B, N, MLA_HEADS, MLA_NOPE + MLA_ROPE)
    if angles is None:
        ckv_all, krope_all = ckv, krope
    else:
        q = jnp.concatenate([q[..., :MLA_NOPE], _axial_rope(q[..., MLA_NOPE:], *angles)], axis=-1)
        ckv_all = jnp.concatenate([ctx_ckv, ckv], axis=1)
        krope_all = jnp.concatenate([ctx_krope, _axial_rope(krope, *angles)], axis=1)
    nk = ckv_all.shape[1]
    kv = (ckv_all @ w_kv_up).reshape(B, nk, MLA_HEADS, MLA_NOPE + MLA_V)
    k = jnp.concatenate(
        [kv[..., :MLA_NOPE], jnp.broadcast_to(krope_all[:, :, None, :], (B, nk, MLA_HEADS, MLA_ROPE))], axis=-1)
    o = _blocked_attention(q[:, :, :, None, :], k, kv[..., MLA_NOPE:], (MLA_NOPE + MLA_ROPE) ** -0.5)
    return o.reshape(B, N, MLA_HEADS * MLA_V) @ w_out, ckv, krope

def _moe(h, router_w, router_b, w_gate, w_up, w_down):
    B, N, D = h.shape
    t = h.reshape(B * N, D)
    scores = jax.nn.sigmoid((t @ router_w).astype(jnp.float32))
    sel = scores + router_b.astype(jnp.float32)
    group_score = lax.top_k(sel.reshape(-1, N_GROUPS, EXPERTS_PER_GROUP), GROUP_SCORE_TOPK)[0].sum(-1)
    best_group = jnp.argmax(group_score, axis=-1)
    in_group = (jnp.arange(N_EXPERTS) // EXPERTS_PER_GROUP)[None, :] == best_group[:, None]
    _, e_idx = lax.top_k(jnp.where(in_group, sel, -jnp.inf), TOP_K)
    w = jnp.take_along_axis(scores, e_idx, axis=-1)
    w = w / jnp.sum(w, axis=-1, keepdims=True)
    combine = jnp.einsum("tk,tke->te", w, jax.nn.one_hot(e_idx, N_EXPERTS, dtype=jnp.float32)).astype(h.dtype)
    hid = jax.nn.silu(jnp.einsum("td,edf->tef", t, w_gate)) * jnp.einsum("td,edf->tef", t, w_up)
    out = jnp.einsum("tef,efd->td", hid * combine[..., None], w_down)
    return out.reshape(B, N, D)

def setup_inputs(seed: int = 0) -> dict:
    key = jax.random.key(seed)
    ks = iter(jax.random.split(key, 40))
    D = D_MODEL

    def nrm(shape, scale=1.0):
        return jax.random.normal(next(ks), shape, jnp.float32) * scale

    def gain(shape):
        return 1.0 + nrm(shape, 0.01)

    x_prompt = nrm((BATCH, SEQ, D))
    x_sample = nrm((DEC_BATCH, DEC_SEQ, D))
    state_gdn = nrm((DEC_BATCH, N_GDN, 2, GDN_HEADS, GDN_DK, GDN_DV), 0.1)
    cache_gqa_k = nrm((DEC_BATCH, N_GQA, PAST_LEN, GQA_KV_HEADS, GQA_HEAD_DIM))
    cache_gqa_v = nrm((DEC_BATCH, N_GQA, PAST_LEN, GQA_KV_HEADS, GQA_HEAD_DIM))
    cache_mla_ckv = nrm((DEC_BATCH, N_MLA, PAST_LEN, MLA_KV_LORA))
    cache_mla_krope = nrm((DEC_BATCH, N_MLA, PAST_LEN, MLA_ROPE))
    c = nrm((DEC_BATCH, D))
    c_ctx = nrm((D,))
    w_ada = nrm((DEPTH, D, 6 * D), 0.3 * D ** -0.5)
    b_ada = nrm((DEPTH, 6 * D), 0.01)
    ln_mix_g = gain((DEPTH, D))
    ln_mix_b = nrm((DEPTH, D), 0.01)
    ln_ffn_g = gain((DEPTH, D))
    ln_ffn_b = nrm((DEPTH, D), 0.01)
    gdn_w_in = nrm((N_GDN, D, GDN_IN), D ** -0.5)
    gdn_conv = nrm((N_GDN, GDN_CONV, GDN_QKV), GDN_CONV ** -0.5)
    gdn_a_log = jnp.log(jax.random.uniform(next(ks), (N_GDN, 2, GDN_HEADS), jnp.float32, 1.0, 16.0))
    u = jax.random.uniform(next(ks), (N_GDN, 2, GDN_HEADS), jnp.float32)
    dt = jnp.exp(math.log(DT_MIN) + u * (math.log(DT_MAX) - math.log(DT_MIN)))
    gdn_dt_bias = dt + jnp.log(-jnp.expm1(-dt))
    gdn_norm_g = gain((N_GDN, GDN_DV))
    gdn_w_out = nrm((N_GDN, GDN_HEADS * GDN_DV, D), BETA_INIT * (GDN_HEADS * GDN_DV) ** -0.5)
    gqa_w_in = nrm((N_GQA, D, GQA_IN), D ** -0.5)
    gqa_q_norm = gain((N_GQA, GQA_HEAD_DIM))
    gqa_k_norm = gain((N_GQA, GQA_HEAD_DIM))
    gqa_w_out = nrm((N_GQA, GQA_HEADS * GQA_HEAD_DIM, D), BETA_INIT * (GQA_HEADS * GQA_HEAD_DIM) ** -0.5)
    mla_w_in = nrm((N_MLA, D, MLA_IN), D ** -0.5)
    mla_q_norm = gain((N_MLA, MLA_Q_LORA))
    mla_kv_norm = gain((N_MLA, MLA_KV_LORA))
    mla_w_q_up = nrm((N_MLA, MLA_Q_LORA, MLA_HEADS * (MLA_NOPE + MLA_ROPE)), MLA_Q_LORA ** -0.5)
    mla_w_kv_up = nrm((N_MLA, MLA_KV_LORA, MLA_HEADS * (MLA_NOPE + MLA_V)), MLA_KV_LORA ** -0.5)
    mla_w_out = nrm((N_MLA, MLA_HEADS * MLA_V, D), BETA_INIT * (MLA_HEADS * MLA_V) ** -0.5)
    router_w = nrm((D, N_EXPERTS), D ** -0.5)
    router_b = nrm((N_EXPERTS,), 0.01)
    moe_w_gate = nrm((DEPTH, N_EXPERTS, D, D_EXPERT), D ** -0.5)
    moe_w_up = nrm((DEPTH, N_EXPERTS, D, D_EXPERT), D ** -0.5)
    moe_w_down = nrm((DEPTH, N_EXPERTS, D_EXPERT, D), BETA_INIT * D_EXPERT ** -0.5)
    return {
        "x_prompt": x_prompt, "x_sample": x_sample,
        "state_gdn": state_gdn, "cache_gqa_k": cache_gqa_k, "cache_gqa_v": cache_gqa_v,
        "cache_mla_ckv": cache_mla_ckv, "cache_mla_krope": cache_mla_krope,
        "c": c, "c_ctx": c_ctx,
        "w_ada": w_ada, "b_ada": b_ada,
        "ln_mix_g": ln_mix_g, "ln_mix_b": ln_mix_b, "ln_ffn_g": ln_ffn_g, "ln_ffn_b": ln_ffn_b,
        "gdn_w_in": gdn_w_in, "gdn_conv": gdn_conv, "gdn_a_log": gdn_a_log, "gdn_dt_bias": gdn_dt_bias,
        "gdn_norm_g": gdn_norm_g, "gdn_w_out": gdn_w_out,
        "gqa_w_in": gqa_w_in, "gqa_q_norm": gqa_q_norm, "gqa_k_norm": gqa_k_norm, "gqa_w_out": gqa_w_out,
        "mla_w_in": mla_w_in, "mla_q_norm": mla_q_norm, "mla_kv_norm": mla_kv_norm,
        "mla_w_q_up": mla_w_q_up, "mla_w_kv_up": mla_w_kv_up, "mla_w_out": mla_w_out,
        "router_w": router_w, "router_b": router_b,
        "moe_w_gate": moe_w_gate, "moe_w_up": moe_w_up, "moe_w_down": moe_w_down,
    }

def reference(x_prompt, x_sample, state_gdn, cache_gqa_k, cache_gqa_v, cache_mla_ckv, cache_mla_krope,
              c, c_ctx, w_ada, b_ada, ln_mix_g, ln_mix_b, ln_ffn_g, ln_ffn_b,
              gdn_w_in, gdn_conv, gdn_a_log, gdn_dt_bias, gdn_norm_g, gdn_w_out,
              gqa_w_in, gqa_q_norm, gqa_k_norm, gqa_w_out,
              mla_w_in, mla_q_norm, mla_kv_norm, mla_w_q_up, mla_w_kv_up, mla_w_out,
              router_w, router_b, moe_w_gate, moe_w_up, moe_w_down):
    n_lat = x_sample.shape[1]
    angles_gqa = _grid_angles(n_lat, GQA_HEAD_DIM)
    angles_mla = _grid_angles(n_lat, MLA_ROPE)
    cond_ctx = jax.nn.silu(c_ctx)[None]
    cond_lat = jax.nn.silu(c)
    xp, xs = x_prompt, x_sample
    st_gdn, st_k, st_v, st_ckv, st_krope = [], [], [], [], []
    for l in range(DEPTH):
        kind, li = l % N_MIXERS, l // N_MIXERS
        m_p = jnp.split(cond_ctx @ w_ada[l] + b_ada[l], 6, axis=-1)
        m_s = jnp.split(cond_lat @ w_ada[l] + b_ada[l], 6, axis=-1)
        hp = _modulate(xp, m_p[0], m_p[1])
        hs = _modulate(xs, m_s[0], m_s[1])
        if kind == 0:
            w = (gdn_w_in[li], gdn_conv[li], gdn_a_log[li], gdn_dt_bias[li], gdn_norm_g[li], gdn_w_out[li])
            zero_state = jnp.zeros((xp.shape[0], 2, GDN_HEADS, GDN_DK, GDN_DV), xp.dtype)
            op, s_ctx = _gdn_mixer(hp, zero_state, *w)
            os_, _ = _gdn_mixer(hs, state_gdn[:, li], *w)
            st_gdn.append(s_ctx)
        elif kind == 1:
            w = (gqa_w_in[li], gqa_q_norm[li], gqa_k_norm[li], gqa_w_out[li])
            op, k_ctx, v_ctx = _gqa_mixer(hp, None, None, None, *w)
            os_, _, _ = _gqa_mixer(hs, angles_gqa, cache_gqa_k[:, li], cache_gqa_v[:, li], *w)
            st_k.append(k_ctx)
            st_v.append(v_ctx)
        else:
            w = (mla_w_in[li], mla_q_norm[li], mla_kv_norm[li], mla_w_q_up[li], mla_w_kv_up[li], mla_w_out[li])
            op, ckv_ctx, krope_ctx = _mla_mixer(hp, None, None, None, *w)
            os_, _, _ = _mla_mixer(hs, angles_mla, cache_mla_ckv[:, li], cache_mla_krope[:, li], *w)
            st_ckv.append(ckv_ctx)
            st_krope.append(krope_ctx)
        xp = _layer_norm(ALPHA * xp + (1 + m_p[2])[:, None] * op, ln_mix_g[l], ln_mix_b[l])
        xs = _layer_norm(ALPHA * xs + (1 + m_s[2])[:, None] * os_, ln_mix_g[l], ln_mix_b[l])
        moe_w = (router_w, router_b, moe_w_gate[l], moe_w_up[l], moe_w_down[l])
        fp = _moe(_modulate(xp, m_p[3], m_p[4]), *moe_w)
        fs = _moe(_modulate(xs, m_s[3], m_s[4]), *moe_w)
        xp = _layer_norm(ALPHA * xp + (1 + m_p[5])[:, None] * fp, ln_ffn_g[l], ln_ffn_b[l])
        xs = _layer_norm(ALPHA * xs + (1 + m_s[5])[:, None] * fs, ln_ffn_g[l], ln_ffn_b[l])
    new_state_gdn = jnp.stack(st_gdn, axis=1)
    new_cache_gqa_k = jnp.stack(st_k, axis=1)
    new_cache_gqa_v = jnp.stack(st_v, axis=1)
    new_cache_mla_ckv = jnp.stack(st_ckv, axis=1)
    new_cache_mla_krope = jnp.stack(st_krope, axis=1)
    return (xp, xs, new_state_gdn, new_cache_gqa_k, new_cache_gqa_v, new_cache_mla_ckv, new_cache_mla_krope)


_drawn_inputs = setup_inputs


def setup_inputs(seed=0):
    import zlib

    import numpy as np

    out = dict(_drawn_inputs(seed))
    spreads = {}
    factors = {'cache_gqa_k': 2.787,
     'cache_mla_krope': 24.16,
     'gqa_q_norm': 8.0,
     'gqa_k_norm': 3.843,
     'mla_q_norm': 8.0,
     'mla_kv_norm': 5.359,
     'cache_mla_ckv': 8.0}
    for name, (base, spread) in spreads.items():
        noise = np.random.default_rng([zlib.crc32(name.encode()), seed]).standard_normal(out[name].shape)
        drawn = base * np.exp(spread * noise) if base else spread * noise
        out[name] = jnp.asarray(drawn.astype(out[name].dtype))
    for name, factor in factors.items():
        out[name] = (out[name] * factor).astype(out[name].dtype)
    return out
```

```python
from contextlib import ExitStack

import numpy as np

import concourse.bass as bass
from concourse import mybir

F32 = mybir.dt.float32
F32R = mybir.dt.float32r
I32 = mybir.dt.int32
ALU = mybir.AluOpType
ACT = mybir.ActivationFunctionType
AX = mybir.AxisListType

P = 128
D = 1024
KT = D // P
CTX, LAT = 128, 256
T = CTX + LAT
TT = T // P
PAST = 128
NK = T + PAST
DEPTH = 4
KINDS = ["gdn", "gqa", "mla", "gdn"]
H = 8
CHUNK = 64
TAPS = 5
PADW = 2 + CTX + 2 + LAT + 2
CONVW = PADW - (TAPS - 1)
NE, NG, EPG = 16, 4, 4
DE = 256
GRID_W = 64
THETA = 10000.0
ALPHA = (2 * DEPTH) ** 0.25
EPS = 1e-6
BIG = 1e30
RING = 8
UNIT = 2 * KT * P
ADA_UNITS = 6 * D * KT // UNIT
EXPERT = 3 * KT * DE
PARTS = EXPERT // UNIT
HEADS_PER_ITER = RING // 2
CTXS, LATS = slice(0, CTX), slice(CTX, T)
QK_SCALE = P ** -0.5
MLA_SCALE = (P + P // 2) ** -0.5

OUT_UNITS = [UNIT] * 4
MIX_UNITS = {
    "gdn": [UNIT] * (2 * H) + OUT_UNITS,
    "gqa": [UNIT] * 6 + OUT_UNITS,
    "mla": [UNIT] * 3 + [KT * 64] + [4 * 2 * 192] * 4 + [UNIT] * 2 + OUT_UNITS,
}

MOE_STEPS = [("G", 0, 0), ("U", 0, 0), ("U", 0, 1), ("T", 0, 0), ("U", 0, 2), ("D", 0, 0), ("T", 0, 1),
             ("U", 0, 3), ("D", 0, 1), ("T", 0, 2), ("G", 1, 0), ("D", 0, 2), ("T", 0, 3), ("U", 1, 0),
             ("D", 0, 3), ("U", 1, 1), ("S", 0, 0), ("T", 1, 0), ("U", 1, 2), ("D", 1, 0), ("T", 1, 1),
             ("U", 1, 3), ("D", 1, 1), ("T", 1, 2), ("D", 1, 2), ("T", 1, 3), ("D", 1, 3), ("S", 1, 0)]
MOE_UNITS = [(j, e, part) for kind, j, e in MOE_STEPS if kind in "UD" for part in ((0, 1) if kind == "U" else (2,))]
MOE_UNIT_OF = {key: n for n, key in enumerate(MOE_UNITS)}


def unit_plan():
    at, u = {}, 0
    for l, kind in enumerate(KINDS):
        for stage, n in (("ada", ADA_UNITS), ("mix", len(MIX_UNITS[kind])), ("moe", PARTS * NE)):
            at[stage, l] = u
            u += n
    return at, u


CONSTS = {}
CONST_COLS = 0
for _name, _n in [("ident", P), ("ones", P), ("le0", P), ("le1", P), ("lt0", P), ("lt1", P), ("inv0", P), ("inv1", P),
                  ("diag16", P), ("off32", P), ("off64", P), ("before", P), ("rot128", P), ("rot64", P),
                  ("cos128", LAT), ("sin128", LAT), ("cos64", LAT), ("sin64", LAT), ("iota", P),
                  ("block_base", 12), ("block_slot", 12), ("first4", 4), ("first16", 16), ("group_off", 4), ("eps", 1)]:
    CONSTS[_name] = (CONST_COLS, _n)
    CONST_COLS += _n

PARAMS = {}
PARAM_COLS = 0
for _name, _n in [("cond", KT * 2), ("b_ada", DEPTH * 48), ("ln_g", DEPTH * 2 * KT), ("ln_b", DEPTH * 2 * KT),
                  ("conv", 2 * H * 3 * TAPS), ("gdn_g", 2), ("gqa_q", 1), ("gqa_k", 1), ("mla_q", 4), ("mla_kv", 2),
                  ("router_w", KT * NE), ("router_b", NE), ("a_log", 2 * 16), ("dt_bias", 2 * 16),
                  ("w_ab", 2 * KT * 32)]:
    PARAMS[_name] = (PARAM_COLS, _n)
    PARAM_COLS += _n


def const_table():
    c = np.zeros((P, CONST_COLS), np.float32)

    def put(name, a):
        o, n = CONSTS[name]
        c[:a.shape[0], o:o + n] = a

    j, i = np.arange(P)[:, None], np.arange(P)[None, :]
    same = (j // CHUNK) == (i // CHUNK)
    put("ident", np.eye(P))
    put("ones", np.ones((P, P)))
    for d, (le, lt) in enumerate([(j <= i, j < i), (j >= i, j > i)]):
        put(f"le{d}", (same & le) * 1.0)
        put(f"lt{d}", (same & lt) * 1.0)
        put(f"inv{d}", (1.0 - (same & le)) * BIG)
    put("diag16", (j // 16 == i // 16) * 1.0)
    put("off32", ((j // 32 == i // 32) & (j // 16 != i // 16)) * 1.0)
    put("off64", ((j // 64 == i // 64) & (j // 32 != i // 32)) * 1.0)
    put("before", (j < i) * 1.0)
    for n in (P, P // 2):
        rot, q = np.zeros((n, n), np.float32), n // 4
        for o in (0, 2 * q):
            for m in range(q):
                rot[o + q + m, o + m] = -1.0
                rot[o + m, o + q + m] = 1.0
        full = np.zeros((n, P), np.float32)
        full[:, :n] = rot
        put(f"rot{n}", full)
        inv = (np.float32(THETA) ** (-np.arange(q, dtype=np.float32) / np.float32(q))).astype(np.float32)
        t = np.arange(LAT)
        row = (t // GRID_W).astype(np.float32)[None, :] * inv[:, None]
        col = (t % GRID_W).astype(np.float32)[None, :] * inv[:, None]
        ang = np.concatenate([row, row, col, col], axis=0)
        put(f"cos{n}", np.cos(ang))
        put(f"sin{n}", np.sin(ang))
    put("iota", np.broadcast_to(i.astype(np.float32), (P, P)))
    base = np.array([T * g for g in range(NG)] + [T * g + P * b for g in range(NG) for b in (1, 2)], np.float32)[None]
    put("block_base", np.broadcast_to(base, (P, 12)))
    put("block_slot", base + np.arange(P)[:, None])
    put("first4", np.broadcast_to(np.arange(4, 0, -1.0)[None, :], (P, 4)))
    put("first16", np.broadcast_to(np.arange(16, 0, -1.0)[None, :], (P, 16)))
    put("group_off", np.broadcast_to(T * np.arange(NG, dtype=np.float32)[None, :], (P, NG)))
    put("eps", np.full((P, 1), EPS))
    return c

def scan_plan():
    rounds, prev, last, n = [], {}, {}, 0
    for k in range(LAT // CHUNK):
        steps = []
        for ch, (base, size) in enumerate([(CTX, LAT), (CTX, LAT), (0, CTX), (0, CTX)]):
            if k < size // CHUNK:
                d = ch % 2
                c0 = base + CHUNK * (k if d == 0 else size // CHUNK - 1 - k)
                steps.append((n, (ch, d, c0 // P, c0 % P // CHUNK, c0, k == 0)))
                prev[n] = last.get(ch)
                last[ch] = n
                n += 1
        rounds.append(steps)
    return rounds, prev


SCAN_ROUNDS, SCAN_PREV = scan_plan()


class Chain:

    def __init__(self, eng, sem):
        self.eng, self.sem, self.base, self.n = eng, sem, 0, 0

    def step(self, ins):
        ins.then_inc(self.sem, 1)
        self.n += 1

    def wait(self):
        self.eng.wait_ge(self.sem, self.base + self.n)

    def enter(self, i, per_turn):
        self.outer = (self.base, self.n)
        self.per_turn = per_turn
        self.base, self.n = i * per_turn + self.base + self.n, 0

    def leave(self, turns):
        assert self.n == self.per_turn, (self.n, self.per_turn)
        self.base, self.n = self.outer[0], self.outer[1] + turns * self.per_turn


def trunk(nc, I, O):
    unit_at, n_units = unit_plan()
    with ExitStack() as ctx:
        def sb(name, shape, dt=F32):
            return ctx.enter_context(nc.sbuf_tensor(name, shape, dt))

        def sem(name):
            return ctx.enter_context(nc.semaphore(name))

        def sems(names):
            return [sem(n) for n in names.split()]

        ring = sb("ring", [P, RING, UNIT])
        bufx = sb("bufx", [P, KT, T])
        bufh = sb("bufh", [P, KT, T])
        bufo = sb("bufo", [P, KT, T])
        con = sb("con", [P, CONST_COLS])
        par = sb("par", [P, PARAM_COLS])
        silc = sb("silc", [P, KT, 2])
        mod = sb("mod", [P, DEPTH, 6 * KT, 2])
        lnt = sb("lnt", [P, 2, T])
        flags = sb("flags", [P, NG, 2], I32)
        SCRATCH = 20100
        with nc.sbuf_tensor("scratch", [P, SCRATCH], F32) as scratch:
            pass
        ps = ctx.enter_context(nc.psum_tensor("ps", [P, 8, 512], F32))

        def C(name, rows=P):
            o, n = CONSTS[name]
            return con[0:rows, o:o + n]

        def R(name):
            o, n = PARAMS[name]
            return par[:, o:o + n]

        def spread(ap, n):
            return ap.rearrange("p (o m) -> p o m", o=1).to_broadcast([ap.shape[0], n, ap.shape[1]])

        def wide(ap, n):
            return ap.rearrange("p (m o) -> p m o", o=1).to_broadcast([ap.shape[0], ap.shape[1], n])

        class Carve:

            def __init__(self):
                self.at = 0

            def __call__(self, *dims):
                n = int(np.prod(dims))
                v = scratch[:, self.at:self.at + n]
                self.at += n
                assert self.at <= SCRATCH, self.at
                if len(dims) == 1:
                    return v
                names = "abcd"[:len(dims)]
                return v.rearrange(f"p ({' '.join(names)}) -> p {' '.join(names)}", **dict(zip(names, dims)))

        ones, ident = C("ones"), C("ident")
        cond = R("cond").rearrange("p (k s) -> p k s", s=2)
        b_ada = R("b_ada").rearrange("p (l m) -> p l m", l=DEPTH)
        ln_g = R("ln_g").rearrange("p (l k) -> p l k", k=KT)
        ln_b = R("ln_b").rearrange("p (l k) -> p l k", k=KT)
        conv = R("conv").rearrange("p (n m) -> p n m", m=3 * TAPS)
        router_w = R("router_w").rearrange("p (k e) -> p k e", k=KT)
        w_ab = R("w_ab").rearrange("p (l k c) -> p l k c", l=2, k=KT)

        def mrow(l, s, k, seg):
            return mod[:, l, s * KT + k, seg:seg + 1]

        c = Carve()
        g_all = c(6, TT, 16)
        g_tmp = c(6, TT, 16)
        g_head = c(6, TT, 2)
        g_taps = c(3, TAPS)
        g_cin = c(3, PADW)
        g_acc = c(3, CONVW)
        g_z = c(2, T)
        g_sq = c(2, T)
        g_rs = c(2, T)
        g_qkv = c(3, T)
        g_kt = c(TT, P)
        g_vt = c(TT, P)
        g_kd = c(2, TT, P)
        g_w = c(2, TT, P)
        g_eq = c(2, T)
        g_last = c(2, T // CHUNK)
        g_n, g_nd, g_ndt, g_t32, g_t64, g_pa, g_pb, g_x = ([c(TT, P), c(TT, P)] for _ in range(8))
        g_s0 = c(2, 2, P)
        g_zero = c(P)
        g_state = c(4, P)
        g_y = c(4, P)
        g_v = c(4, P)
        g_o = c(T)
        g_osq = c(T)
        c = Carve()
        a_p = c(2, T)
        a_pt = c(2, 3, P)
        a_st = c(2, 4)
        a_tmp = c(2, LAT)
        shared = c.at
        q_qkv = c(12, T)
        q_sq = c(10, T)
        q_kall = c(2, NK)
        q_vall = c(2, NK // P, P)
        c = Carve()
        c(shared)
        m_c = c(6, T)
        m_sq = c(6, T)
        m_kr = c(T)
        m_ckv = c(2, NK)
        m_krall = c(NK)
        m_qn = c(4, T)
        m_qr = c(4, T)
        m_kn = c(4, NK)
        m_v = c(NK // P, 4 * P)
        e_hi, e_lo = sb("e_hi", [P, TT, D], F32R), sb("e_lo", [P, TT, D], F32R)
        e_pick = sb("e_pick", [P, 2, TT, P], F32R)
        e_put = sb("e_put", [P, 2, T], F32R)
        e_yhi, e_ylo = sb("e_yhi", [P, D], F32R), sb("e_ylo", [P, D], F32R)
        e_hs = sb("e_hs", [P, 2, KT, P])
        e_sg = sb("e_sg", [P, 2, DE])
        e_hid = sb("e_hid", [P, 2, DE])
        e_hidT = sb("e_hidT", [P, 2, 2, P])
        e_cs = sb("e_cs", [P, 2, EPG])
        e_sidrow = sb("e_sidrow", [P, T])
        e_rt = sb("e_rt", [P, 10, TT * NE])
        e_sid = sb("e_sid", [P, 3, TT])
        e_cnt = sb("e_cnt", [P, NG])

        params_in, consts_in, x_in = sems("params_in consts_in x_in")
        ring_full = [sem(f"ring_full{i}") for i in range(RING)]
        ring_free = sem("ring_free")
        cond_ready, mod_ready, h_ready, ax_ready = sems("cond_ready mod_ready h_ready ax_ready")
        (r_ready, mean_mm, mean_ready, centred, squared, var_mm, dev_ready, normed, x_ready) = sems(
            "r_ready mean_mm mean_ready centred squared var_mm dev_ready normed x_ready")
        tile_mm, y_out = sems("tile_mm y_out")
        chain_v, chain_a = sems("chain_v chain_a")
        (ab_mm, sp_in, sp_exp, sp_ln, g_ready, cum_mm, cum_ready) = sems(
            "ab_mm sp_in sp_exp sp_ln g_ready cum_mm cum_ready")
        pad_zero, s0_in, st_out = sems("pad_zero s0_in st_out")
        (raw_in, z_in, conv_done, head_cols, silu_done, qk_sq, nrm_mm, nrm_dev, qk_ready, kv_tr, kv_tok,
         kd_done, gram_mm, row_mm, row_masked, decay_done, strict_done, n_done, w_done, nd_done, x1_done,
         qe_done) = sems(
            "raw_in z_in conv_done head_cols silu_done qk_sq nrm_mm nrm_dev qk_ready kv_tr kv_tok kd_done "
            "gram_mm row_mm row_masked decay_done strict_done n_done w_done nd_done x1_done qe_done")
        inv_mm, inv_cp, inv_x = ([sem(f"{n}{d}") for d in range(2)] for n in ("inv_mm", "inv_cp", "inv_x"))
        (ks_mm, y_done, vn_mm, v_done, os_mm, s_done, o_done, o_sum, o_sq, o_nrm_mm, o_dev, head_done) = sems(
            "ks_mm y_done vn_mm v_done os_mm s_done o_done o_sum o_sq o_nrm_mm o_dev head_done")
        (raw_ev, at_sq, at_nmm, at_dev, at_normed, rot_mm, rot_done, own_ready, vt_mm, vt_ev, cache_in, cache_out,
         up_mm, up_ev) = sems(
            "raw_ev at_sq at_nmm at_dev at_normed rot_mm rot_done own_ready vt_mm vt_ev cache_in cache_out "
            "up_mm up_ev")
        (sc_mm, max_done, exp_done, p_done, pt_mm, pt_ev, pv_mm, oh_ev) = sems(
            "sc_mm max_done exp_done p_done pt_mm pt_ev pv_mm oh_ev")
        (o_zero, rt_mm, score_ready, oh_ready, rk_mm, sid_ready, row2_mm, row2_ready, tk_mm, tk_hi, tk_lo,
         flags_ready) = sems(
            "o_zero rt_mm score_ready oh_ready rk_mm sid_ready row2_mm row2_ready tk_mm tk_hi tk_lo flags_ready")

        def moe_sems(pre):
            return dict(zip("pick ga ga_ev cs sg hid tr trv yhi ylo sc sc_ev".split(), sems(" ".join(
                pre + n for n in "pick ga ga_ev cs sg hid tr trv yhi ylo sc sc_ev".split()))))

        F = moe_sems("f_")
        X = moe_sems("x_")
        x_w, x_piece = sems("x_w x_piece")

        tiles_at, n_tiles = {}, 0
        for l, kind in enumerate(KINDS):
            tiles_at["in", l] = n_tiles
            n_tiles += {"gdn": 2 * H, "gqa": 6, "mla": 3}[kind]
            tiles_at["out", l] = n_tiles
            n_tiles += 4
        att_at = {1: 0, 2: H * TT}
        li_of = {0: 0, 3: 1}

        def unit(u):
            return ring[:, u % RING, :]

        def landed(eng, u, turn=0):
            eng.wait_ge(ring_full[u % RING], turn * 16 + 16 * (u // RING + 1))

        def used(eng, u, shift=0):
            eng.wait_ge(ring_free, shift + (u + 1))

        def tile_done(eng, stage, l, n, turn=0, per_turn=0):
            if n % 2 == 0:
                eng.wait_ge(tile_mm, turn * per_turn + (tiles_at[stage, l] + n // 2 + 1))
            else:
                u0 = unit_at["mix", l] if stage == "in" else unit_at["moe", l] - len(OUT_UNITS)
                used(eng, u0 + n // 2, turn * per_turn)

        def scan_state(ch, d, first, j):
            if not first:
                return g_state[:, ch, :]
            return g_s0[:, j % 2, d, :] if ch < 2 else g_zero

        def piece_buf(part):
            return bufh[:, :, :].rearrange("p k t -> p (k t)")[:, 0:UNIT]

        block = ctx.enter_context(nc.Block())

        @block.sync
        def _(sp):
            sp.dma_start(par[:, :], I["params"]).then_inc(params_in, 16)

            def load(src, u, cols=UNIT, turn=0):
                if isinstance(turn, int) and u < RING:
                    pass
                else:
                    used(sp, u - RING, turn * RING)
                sp.dma_start(unit(u)[:, 0:cols], src).then_inc(ring_full[u % RING], 16)

            def stream(first, n, src):
                for k in range(RING):
                    load(src(k), first + k)
                turns = n // RING
                if turns > 1:
                    with sp.Fori(1, turns) as i:
                        for k in range(RING):
                            load(src(i * RING + k), first + k, turn=i)

            for l, kind in enumerate(KINDS):
                stream(unit_at["ada", l], ADA_UNITS, lambda k: I["w_ada"][k + l * ADA_UNITS])
                u0 = unit_at["mix", l]
                if kind == "gdn":
                    stream(u0, 2 * H, lambda k: I["gdn_w_in"][k + li_of[l] * 2 * H])
                    for k in range(4):
                        load(I["gdn_w_out"][4 * li_of[l] + k], u0 + 2 * H + k)
                elif kind == "gqa":
                    for k in range(6):
                        load(I["gqa_w_in"][k], u0 + k)
                    for k in range(4):
                        load(I["gqa_w_out"][k], u0 + 6 + k)
                else:
                    for k in range(3):
                        load(I["mla_w_in"][k], u0 + k)
                    load(I["mla_w_kr"], u0 + 3, KT * 64)
                    for half in range(2):
                        for k in range(2):
                            load(I["mla_w_q_up"][2 * half + k], u0 + 4 + 3 * half + k, 4 * 2 * 192)
                        load(I["mla_w_kv_up"][half], u0 + 6 + 3 * half)
                    for k in range(4):
                        load(I["mla_w_out"][k], u0 + 10 + k)
                u0, per = unit_at["moe", l], len(MOE_UNITS)

                def expert_part(turn, n):
                    j, e, part = MOE_UNITS[n]
                    return I["moe"][turn * (2 * EPG) + (l * NE + j * EPG + e), :, part * UNIT:(part + 1) * UNIT]

                with sp.Fori(0, NG // 2) as i:
                    for n in range(per):
                        used(sp, u0 + n - RING, i * per)
                        sp.dma_start(unit(u0 + n), expert_part(i, n)).then_inc(ring_full[(u0 + n) % RING], 16)
            sp.wait_ge(x_ready, KT * 2 * DEPTH)
            sp.dma_start(O["y"], bufx[:, :, :]).then_inc(y_out, 16)
            sp.wait_ge(y_out, 16)
            sp.wait_ge(st_out, 16 * 2 * H)
            sp.wait_ge(cache_out, 16 * 4)

        @block.tensor
        def _(pe):
            mm = nc.tensor.matmul

            def ada(l):
                u0 = unit_at["ada", l]
                if l == 0:
                    pe.wait_ge(cond_ready, 1)
                else:
                    pe.wait_ge(mod_ready, 3 * l)
                with pe.Fori(0, ADA_UNITS // RING) as i:
                    for k in range(RING):
                        landed(pe, u0 + k, i)
                        w = unit(u0 + k).rearrange("p (m k c) -> p m k c", m=2, k=KT)
                        for m in range(2):
                            out = ps[:, 7, bass.ds(i * (4 * RING) + (4 * k + 2 * m), 2)]
                            for kt in range(KT):
                                last = mm(out, w[:, m, kt, :], silc[:, kt, :], start=(kt == 0), stop=(kt == KT - 1))
                        last.then_inc(ring_free, 1)

            def project(l, stage, first, n, rhs, banks, wait_bank, tiles=None):
                u0 = unit_at["mix", l] if stage == "in" else unit_at["moe", l] - len(OUT_UNITS)
                for t in range(first, first + n):
                    if t % 2 == 0:
                        landed(pe, u0 + t // 2)
                    w = unit(u0 + t // 2).rearrange("p (m k c) -> p m k c", m=2, k=KT)
                    wait_bank(t)
                    for kt in range(KT):
                        last = mm(ps[:, banks[t % len(banks)], 0:T], w[:, t % 2, kt, :], rhs[:, kt, :],
                                  start=(kt == 0), stop=(kt == KT - 1))
                    last.then_inc(tile_mm if t % 2 == 0 else ring_free, 1)

            def project_out(l, ready, n_ready):
                pe.wait_ge(ready, n_ready)
                project(l, "out", 0, KT, bufo, (0, 1),
                        lambda t: pe.wait_ge(r_ready, KT * 2 * l + t - 1) if t >= 2 else None)

            def layer_norm(n, rbuf, sqbuf):
                for k in range(KT):
                    pe.wait_ge(r_ready, KT * n + k + 1)
                    last = mm(ps[:, 5, 0:T], ones, rbuf[:, k, :], start=(k == 0), stop=(k == KT - 1))
                last.then_inc(mean_mm, 1)
                for k in range(KT):
                    if k % 2 == 0:
                        pe.wait_ge(squared, 4 * n + k // 2 + 1)
                    last = mm(ps[:, 6, 0:T], ones, sqbuf[:, k, :], start=(k == 0), stop=(k == KT - 1))
                last.then_inc(var_mm, 1)

            def head_proj_unit(l, j, m, part, i):
                u0 = unit_at["mix", l]
                u = u0 + 2 * j + m // 2
                hh = i * HEADS_PER_ITER + (li_of[l] * H + j)
                if part != 1:
                    landed(pe, u, i)
                    if m >= 2:
                        pe.wait_ge(raw_in, hh * 3 + (m - 1))
                w = unit(u).rearrange("p (m k c) -> p m k c", m=2, k=KT)
                for kt in range(KT) if part is None else range(4 * part, 4 * part + 4):
                    last = mm(ps[:, 6 + m % 2, 0:T], w[:, m % 2, kt, :], bufh[:, kt, :],
                              start=(kt == 0), stop=(kt == KT - 1))
                if part != 0:
                    last.then_inc(tile_mm if m % 2 == 0 else ring_free, 1)

            def gdn(l):
                li = li_of[l]
                for kt in range(KT):
                    pe.wait_ge(h_ready, KT * 2 * l + kt + 1)
                for t in range(TT):
                    for kt in range(KT):
                        last = mm(ps[:, 2, 32 * t:32 * t + 32], bufh[:, kt, P * t:P * t + P], w_ab[:, li, kt, :],
                                  start=(kt == 0), stop=(kt == KT - 1))
                last.then_inc(ab_mm, 1)
                pe.wait_ge(g_ready, li + 1)
                for what, mats in enumerate((("le0", "le1"), ("lt1", "lt0"))):
                    for t in range(TT):
                        for d in range(2):
                            o = 48 * what + 16 * t + 8 * d
                            last = mm(ps[:, 3, o:o + 8], C(mats[d]), g_all[:, 0, t, 8 * d:8 * d + 8],
                                      start=True, stop=True)
                last.then_inc(cum_mm, 1)
                pe.wait_ge(cum_ready, 2 * (li + 1))
                with pe.Fori(0, H // HEADS_PER_ITER) as i:
                    for j in range(HEADS_PER_ITER):
                        gdn_head(l, i, j)
                project_out(l, head_done, H * (li + 1))

            def gdn_head(l, i, j):
                hh = i * HEADS_PER_ITER + (li_of[l] * H + j)
                if j == 0:
                    for m in range(4):
                        head_proj_unit(l, j, m, None, i)
                pe.wait_ge(head_cols, hh + 1)
                for d in range(2):
                    for t in range(TT):
                        last = mm(ps[:, 4 + d, P * t:P * t + P], g_head[:, 0, t, d:d + 1].to_broadcast([P, P]),
                                  C(f"le{d}"), start=True, stop=True)
                    last.then_inc(row_mm, 1)
                pe.wait_ge(qk_sq, hh + 1)
                for m in range(2):
                    last = mm(ps[:, 2 + m, 0:T], ones, g_sq[:, m, :], start=True, stop=True)
                last.then_inc(nrm_mm, 1)
                pe.wait_ge(silu_done, hh * 3 + 3)
                for t in range(TT):
                    last = nc.tensor.transpose(ps[:, 0, P * t:P * t + P], g_qkv[:, 2, P * t:P * t + P], ident)
                last.then_inc(kv_tr, 1)
                pe.wait_ge(qk_ready, hh * 2 + 2)
                for t in range(TT):
                    last = nc.tensor.transpose(ps[:, 1, P * t:P * t + P], g_qkv[:, 1, P * t:P * t + P], ident)
                last.then_inc(kv_tr, 1)
                for m, rhs in ((0, 1), (1, 0)):
                    for t in range(TT):
                        cols = slice(P * t, P * t + P)
                        last = mm(ps[:, 2 + m, cols], g_qkv[:, 1, cols], g_qkv[:, rhs, cols], start=True, stop=True)
                    last.then_inc(gram_mm, 1)
                inverse(hh)
                scan(l, i, j, hh)

            def inverse(hh):
                jobs = [
                    ("T", g_n, None, 0, 0, 0), ("M", g_ndt, g_nd, 1, 0, 1), ("M", g_nd, g_ndt, 0, 0, 1),
                    ("M", g_pb, g_x, 1, 2, 1), ("M", g_pb, g_pa, 0, 2, 1), ("M", g_pa, g_pb, 1, 2, 2),
                    ("M", g_ndt, g_x, 0, 4, 2), ("M", g_nd, g_ndt, 1, 4, 2), ("M", g_pa, g_x, 0, 5, 3),
                    ("T", g_x, None, 1, 5, 4), ("M", g_t32, g_x, 0, 5, 4), ("M", g_pb, g_nd, 1, 7, 4),
                    ("T", g_x, None, 0, 7, 5), ("M", g_t64, g_x, 1, 7, 5), ("M", g_pb, g_nd, 0, 9, 5)]
                for n, (kind, a, b, bank, copies, sums) in enumerate(jobs):
                    for d in range(2):
                        if n == 0:
                            pe.wait_ge(n_done, hh * 2 + d + 1)
                            pe.wait_ge(decay_done, hh * 2 + d + 1)
                        if n == 1:
                            pe.wait_ge(nd_done, hh * 2 + d + 1)
                        if n == 3:
                            pe.wait_ge(x1_done, hh * 2 + d + 1)
                        if copies:
                            pe.wait_ge(inv_cp[d], hh * 9 + copies)
                        if sums:
                            pe.wait_ge(inv_x[d], hh * 6 + sums)
                        for t in range(TT):
                            out = ps[:, 4 + d + 2 * bank, P * t:P * t + P]
                            if kind == "T":
                                last = nc.tensor.transpose(out, a[d][:, t, :], ident)
                            else:
                                last = mm(out, a[d][:, t, :], b[d][:, t, :], start=True, stop=True)
                        last.then_inc(inv_mm[d], 1)

            def scan(l, i, j, hh):
                pe.wait_ge(kd_done, hh + 1)
                pe.wait_ge(qe_done, hh * 2 + 2)
                pe.wait_ge(w_done, hh * 2 + 2)
                for d in range(2):
                    pe.wait_ge(inv_x[d], hh * 6 + 6)
                pe.wait_ge(s0_in, hh * 16 + 16)
                for k, steps in enumerate(SCAN_ROUNDS):
                    for n, (ch, d, t, half, c0, first) in steps:
                        if k == 0:
                            if n == 0:
                                pe.wait_ge(kv_tok, hh * 2 + 2)
                        else:
                            pe.wait_ge(s_done, hh * 12 + SCAN_PREV[n] + 1)
                        rows = slice(64 * half, 64 * half + 64)
                        mm(ps[rows, ch, 0:P], g_qkv[:, 1, c0:c0 + CHUNK], scan_state(ch, d, first, j),
                           start=True, stop=True).then_inc(ks_mm, 1)
                    if j + 1 < HEADS_PER_ITER:
                        head_proj_unit(l, j + 1, k, 0, i)
                    for n, (ch, d, t, half, c0, first) in steps:
                        rows = slice(64 * half, 64 * half + 64)
                        pe.wait_ge(y_done, hh * 12 + n + 1)
                        mm(ps[rows, ch, P:2 * P], g_x[d][:, t, rows], g_y[:, ch, :],
                           start=True, stop=True).then_inc(vn_mm, 1)
                    if j + 1 < HEADS_PER_ITER:
                        head_proj_unit(l, j + 1, k, 1, i)
                    for n, (ch, d, t, half, c0, first) in steps:
                        rows = slice(64 * half, 64 * half + 64)
                        pe.wait_ge(v_done, hh * 12 + n + 1)
                        out = ps[:, 4 + d, c0:c0 + CHUNK]
                        mm(out, scan_state(ch, d, first, j), g_eq[:, d, c0:c0 + CHUNK], start=True, stop=False)
                        mm(out, g_v[rows, ch, :], g_w[rows, d, t, rows], start=False, stop=True)
                        mm(ps[:, ch, 3 * P:4 * P], g_kd[rows, d, t, :], g_v[rows, ch, :],
                           start=True, stop=True).then_inc(os_mm, 1)
                pe.wait_ge(o_sq, hh + 1)
                mm(ps[:, 0, 0:T], ones, g_osq[:, :], start=True, stop=True).then_inc(o_nrm_mm, 1)

            def attention(l, heads, first_head, scores, values):
                a0 = att_at[l] + TT * first_head
                units = [(h, qt) for h in heads for qt in range(TT)]

                def score(n):
                    h, qt = units[n]
                    nk = P if qt == 0 else T
                    k0 = 0 if qt == 0 else P
                    if a0 + n >= 2:
                        pe.wait_ge(exp_done, a0 + n - 1)
                    scores(ps[:, n % 2, 0:nk], h, slice(P * qt, P * qt + P), slice(k0, k0 + nk)).then_inc(sc_mm, 1)

                score(0)
                for n, (h, qt) in enumerate(units):
                    if n + 1 < len(units):
                        score(n + 1)
                    tiles = [0] if qt == 0 else [1, 2, 3]
                    pe.wait_ge(p_done, a0 + n + 1)
                    if a0 + n >= 2:
                        pe.wait_ge(pt_ev, a0 + n - 1)
                    for m in range(len(tiles)):
                        last = nc.tensor.transpose(ps[:, 2 + n % 2, P * m:P * m + P], a_p[:, n % 2, P * m:P * m + P],
                                                   ident)
                    last.then_inc(pt_mm, 1)
                    pe.wait_ge(pt_ev, a0 + n + 1)
                    hn = a0 // TT + n // TT
                    if qt == 0 and hn >= 2:
                        pe.wait_ge(oh_ev, hn - 1)
                    for m, kt in enumerate(tiles):
                        last = mm(ps[:, 4 + (n // TT) % 2, P * qt:P * qt + P], values(h, kt), a_pt[:, n % 2, m, :],
                                  start=(m == 0), stop=(m == len(tiles) - 1))
                    last.then_inc(pv_mm, 1)

            def gqa(l):
                for kt in range(KT):
                    pe.wait_ge(h_ready, KT * 2 * l + kt + 1)
                project(l, "in", 0, 12, bufh, (0, 1), lambda t: pe.wait_ge(raw_ev, t - 1) if t >= 2 else None)
                for n in range(10):
                    pe.wait_ge(at_sq, n + 1)
                    if n >= 2:
                        pe.wait_ge(at_dev, n - 1)
                    mm(ps[:, 2 + n % 2, 0:T], ones, q_sq[:, n, :], start=True, stop=True).then_inc(at_nmm, 1)
                pe.wait_ge(raw_ev, 12)
                for kv in range(2):
                    for t in range(TT):
                        last = nc.tensor.transpose(ps[:, kv, P * t:P * t + P], q_qkv[:, 10 + kv, P * t:P * t + P], ident)
                    last.then_inc(vt_mm, 1)
                for n in range(5):
                    pe.wait_ge(at_normed, 2 * n + 2)
                    if n >= 2:
                        pe.wait_ge(rot_done, n - 1)
                    for m in range(2):
                        last = mm(ps[:, 4 + n % 2, LAT * m:LAT * m + LAT], C("rot128"), q_qkv[:, 2 * n + m, LATS],
                                  start=True, stop=True)
                    last.then_inc(rot_mm, 1)
                pe.wait_ge(rot_done, 5)
                pe.wait_ge(own_ready, 2)
                pe.wait_ge(vt_ev, 2)
                pe.wait_ge(cache_in, 16 * 2)

                def scores(out, h, q, keys):
                    return mm(out, q_qkv[:, h, q], q_kall[:, h // 4, keys], start=True, stop=True)

                attention(l, range(H), 0, scores, lambda h, kt: q_vall[:, h // 4, kt, :])
                project_out(l, oh_ev, H)

            def mla(l):
                for kt in range(KT):
                    pe.wait_ge(h_ready, KT * 2 * l + kt + 1)
                project(l, "in", 0, 6, bufh, (0, 1), lambda t: pe.wait_ge(raw_ev, 12 + t - 1) if t >= 2 else None)
                u = unit_at["mix", l] + 3
                landed(pe, u)
                w = unit(u)[:, 0:KT * 64].rearrange("p (k c) -> p k c", k=KT)
                pe.wait_ge(raw_ev, 12 + 5)
                for kt in range(KT):
                    last = mm(ps[0:64, 0, 0:T], w[:, kt, :], bufh[:, kt, :], start=(kt == 0), stop=(kt == KT - 1))
                last.then_inc(ring_free, 1)
                for m, tiles in enumerate((range(4), range(4, 6))):
                    for n in tiles:
                        pe.wait_ge(at_sq, 10 + n + 1)
                        last = mm(ps[:, 2 + m, 0:T], ones, m_sq[:, n, :], start=(n == tiles[0]), stop=(n == tiles[-1]))
                    last.then_inc(at_nmm, 1)
                pe.wait_ge(raw_ev, 12 + 7)
                mm(ps[0:64, 4, 0:LAT], C("rot64", 64)[:, 0:64], m_kr[0:64, LATS],
                   start=True, stop=True).then_inc(rot_mm, 1)
                pe.wait_ge(at_normed, 10 + 6)
                pe.wait_ge(cache_in, 16 * 4)
                pe.wait_ge(own_ready, 2 + 4)
                pe.wait_ge(rot_done, 6)
                for half in range(2):
                    mla_half(l, half)
                project_out(l, oh_ev, 2 * H)

            def mla_half(l, half):
                n_up = 16 * half
                job = [n_up]

                def free_bank():
                    if job[0] - n_up >= 2:
                        pe.wait_ge(up_ev, job[0] - 1)
                    elif half:
                        pe.wait_ge(up_ev, n_up)
                    job[0] += 1
                    return job[0] % 2

                if half:
                    pe.wait_ge(oh_ev, H + 4)
                for k in range(2):
                    u = unit_at["mix", l] + 4 + 3 * half + k
                    landed(pe, u)
                    w = unit(u)[:, 0:4 * 2 * 192].rearrange("p (h k c) -> p h k c", h=2, k=4)
                    for hd in range(2):
                        for cols in (slice(0, P), slice(P, 192)):
                            rows = cols.stop - cols.start
                            b = free_bank()
                            for kt in range(4):
                                last = mm(ps[0:rows, b, 0:T], w[:, hd, kt, cols], m_c[:, kt, :],
                                          start=(kt == 0), stop=(kt == 3))
                            if hd == 1 and rows == 64:
                                last.then_inc(ring_free, 1)
                            else:
                                last.then_inc(up_mm, 1)
                u = unit_at["mix", l] + 6 + 3 * half
                landed(pe, u)
                w = unit(u).rearrange("p (k c) -> p k c", k=2)
                for hd in range(4):
                    b = free_bank()
                    for kt in range(2):
                        last = mm(ps[:, b, 0:NK], w[:, kt, P * hd:P * hd + P], m_ckv[:, kt, :],
                                  start=(kt == 0), stop=(kt == 1))
                    last.then_inc(up_mm, 1)
                for tile in range(NK // P):
                    b = free_bank()
                    for kt in range(2):
                        last = mm(ps[:, b, 0:512], m_ckv[:, kt, P * tile:P * tile + P], w[:, kt, 512:1024],
                                  start=(kt == 0), stop=(kt == 1))
                    last.then_inc(up_mm if tile < 3 else ring_free, 1)
                pe.wait_ge(up_ev, 16 * half + 16)
                for m in range(2):
                    for hd in range(2):
                        last = mm(ps[0:64, 4 + m, LAT * hd:LAT * hd + LAT], C("rot64", 64)[:, 0:64],
                                  m_qr[0:64, 2 * m + hd, LATS], start=True, stop=True)
                    last.then_inc(rot_mm, 1)
                pe.wait_ge(rot_done, 6 + 2 * half + 2)

                def scores(out, h, q, keys):
                    mm(out, m_qn[:, h % 4, q], m_kn[:, h % 4, keys], start=True, stop=False)
                    return mm(out, m_qr[0:64, h % 4, q], m_krall[0:64, keys], start=False, stop=True)

                attention(l, range(4 * half, 4 * half + 4), 4 * half, scores,
                          lambda h, kt: m_v[:, kt, P * (h % 4):P * (h % 4) + P])

            def gather(S, n, j, comb_cols):
                pe.wait_ge(S["pick"], n + 1)
                for q in range(2):
                    for ft in range(4 * q, 4 * q + 4):
                        k = 0
                        for t in range(TT):
                            for half in (e_hi, e_lo):
                                last = mm(ps[:, 5 + q, P * (ft % 4):P * (ft % 4) + P],
                                          half[:, t, P * ft:P * ft + P], e_pick[:, j, t, :],
                                          start=(k == 0), stop=(k == 2 * TT - 1))
                                k += 1
                    last.then_inc(S["ga"], 1)
                for t in range(TT):
                    last = mm(ps[:, 7, 96 + 4 * j:100 + 4 * j], e_pick[:, j, t, :].bitcast(F32), comb_cols(t),
                              start=(t == 0), stop=(t == TT - 1))
                last.then_inc(S["ga"], 1)

            def transpose_hidden(S, n, b):
                pe.wait_ge(S["hid"], n + 1)
                for m in range(2):
                    last = nc.tensor.transpose(ps[:, 2, 256 * b + P * m:256 * b + P * m + P],
                                               e_hid[:, b, P * m:P * m + P], ident)
                last.then_inc(S["tr"], 1)

            def down(e, w):
                w = w.rearrange("p (f c) -> p f c", f=2)
                for f in range(2):
                    for y in range(2):
                        last = mm(ps[:, 3 + y, :], e_hidT[:, e % 2, f, :], w[:, f, 512 * y:512 * y + 512],
                                  start=(e == 0 and f == 0), stop=(e == EPG - 1 and f == 1))
                return last

            def scatter(S, n, j):
                pe.wait_ge(S["yhi"], n + 1)
                pe.wait_ge(S["ylo"], n + 1)
                for ft in range(KT):
                    if ft >= 2:
                        pe.wait_ge(S["sc_ev"], n * KT + (ft - 1))
                    b = 5 + ft % 2
                    mm(ps[:, b, 0:T], e_yhi[:, P * ft:P * ft + P], e_put[:, j, :], start=True, stop=False)
                    mm(ps[:, b, 0:T], e_ylo[:, P * ft:P * ft + P], e_put[:, j, :],
                       start=False, stop=True).then_inc(S["sc"], 1)

            def gate_up(b, part, e, w):
                w = w.rearrange("p (k c) -> p k c", k=4)
                for k in range(4):
                    kt = 4 * part + k
                    last = mm(ps[:, e % 2, :], e_hs[:, b, kt, :], w[:, k, :], start=(kt == 0), stop=(kt == KT - 1))
                return last

            def moe(l):
                for kt in range(KT):
                    pe.wait_ge(h_ready, KT * (2 * l + 1) + kt + 1)
                for t in range(TT):
                    for kt in range(KT):
                        last = mm(ps[:, 2, NE * t:NE * t + NE], bufh[:, kt, P * t:P * t + P], router_w[:, kt, :],
                                  start=(kt == 0), stop=(kt == KT - 1))
                last.then_inc(rt_mm, 1)
                pe.wait_ge(o_zero, l + 1)
                for n in range(2 * TT):
                    if n >= 2:
                        pe.wait_ge(tk_hi, 2 * TT * l + n - 1)
                        pe.wait_ge(tk_lo, 2 * TT * l + n - 1)
                    for m in range(4):
                        last = nc.tensor.transpose(ps[:, 5 + n % 2, P * m:P * m + P],
                                                   bufh[:, 4 * (n % 2) + m, P * (n // 2):P * (n // 2) + P], ident)
                    last.then_inc(tk_mm, 1)
                oh = e_rt[:, 8, 0:TT * NG].rearrange("p (t g) -> p t g", t=TT)
                pe.wait_ge(oh_ready, l + 1)
                for t in range(TT):
                    for t2 in range(t + 1):
                        mm(ps[:, 2, 64 + 4 * t:68 + 4 * t], C("before") if t2 == t else ones, oh[:, t2, :],
                           start=(t2 == 0), stop=(t2 == t))
                for t in range(TT):
                    last = mm(ps[:, 2, 80:84], ones, oh[:, t, :], start=(t == 0), stop=(t == TT - 1))
                last.then_inc(rk_mm, 1)
                pe.wait_ge(sid_ready, l + 1)
                for t in range(TT):
                    last = mm(ps[:, 2, P + P * t:2 * P + P * t], e_sid[:, 0, t:t + 1].to_broadcast([P, P]), ident,
                              start=True, stop=True)
                last.then_inc(row2_mm, 1)
                pe.wait_ge(row2_ready, l + 1)
                pe.wait_ge(tk_hi, 2 * TT * (l + 1))
                pe.wait_ge(tk_lo, 2 * TT * (l + 1))

                u0, per = unit_at["moe", l], len(MOE_UNITS)
                comb = e_rt[:, 9, :].rearrange("p (t e) -> p t e", t=TT)
                with pe.Fori(0, NG // 2) as i:
                    for kind, j, e in MOE_STEPS:
                        gg = i * 2 + (NG * l + j)
                        n = i * (2 * EPG) + (NE * l + EPG * j + e)
                        if kind == "G":
                            gather(F, gg, j, lambda t: comb[:, t, bass.ds(i * (2 * EPG) + EPG * j, EPG)])
                        elif kind == "U":
                            if e == 0:
                                pe.wait_ge(F["ga_ev"], gg * 2 + 2)
                            for part in range(2):
                                m = MOE_UNIT_OF[j, e, part]
                                landed(pe, u0 + m, i * (per // RING))
                                gate_up(j, part, e, unit(u0 + m)).then_inc(ring_free, 1)
                        elif kind == "T":
                            transpose_hidden(F, n, e % 2)
                        elif kind == "D":
                            m = MOE_UNIT_OF[j, e, 2]
                            landed(pe, u0 + m, i * (per // RING))
                            pe.wait_ge(F["trv"], n + 1)
                            down(e, unit(u0 + m)).then_inc(ring_free, 1)
                        else:
                            scatter(F, gg, j)
                pe.wait_ge(F["sc_ev"], KT * NG * (l + 1))
                pe.wait_ge(flags_ready, l + 1)
                with pe.Fori(0, NG) as g:
                    for b in range(2):
                        n = g * 2 + (2 * NG * l + b)
                        more = pe.value_load(flags[0:1, g, b:b + 1], min_val=0, max_val=1)
                        with pe.If(more > 0):
                            gather(X, n, 0, lambda t: comb[:, t, bass.ds(g * EPG, EPG)])
                            pe.wait_ge(X["ga_ev"], n * 2 + 2)
                            for e in range(EPG):
                                for part in range(PARTS):
                                    pe.wait_ge(x_w, (n * (EPG * PARTS) + (PARTS * e + part + 1)) * 16)
                                    w = piece_buf(part)
                                    if part < 2:
                                        last = gate_up(0, part, e, w)
                                    else:
                                        transpose_hidden(X, n * EPG + e, e % 2)
                                        pe.wait_ge(X["trv"], n * EPG + (e + 1))
                                        last = down(e, w)
                                    last.then_inc(x_piece, 1)
                            scatter(X, n, 0)
                            pe.wait_ge(X["sc_ev"], n * KT + KT)
                            pe.nop()
                        with pe.Else():
                            pe.sem_inc(X["ga"], 3)
                            pe.sem_inc(X["tr"], EPG)
                            pe.sem_inc(x_piece, EPG * PARTS)
                            pe.sem_inc(X["sc"], KT)

            pe.wait_ge(consts_in, 16)
            pe.wait_ge(params_in, 16)
            ada(0)
            for l, kind in enumerate(KINDS):
                {"gdn": gdn, "gqa": gqa, "mla": mla}[kind](l)
                layer_norm(2 * l, bufh, bufo)
                moe(l)
                layer_norm(2 * l + 1, bufo, bufh)
                if l + 1 < DEPTH:
                    ada(l + 1)

        @block.scalar
        def _(act):
            op = nc.scalar.activation
            a = Chain(act, chain_a)

            def copy(out, in_, **kw):
                return op(out, in_, ACT.Copy, **kw)

            def layer_norm(n, l, which, rbuf, sqbuf):
                act.wait_ge(mean_mm, n + 1)
                copy(lnt[:, 0, :], ps[:, 5, 0:T], scale=1.0 / D).then_inc(mean_ready, 1)
                for q in range(4):
                    act.wait_ge(centred, 4 * n + q + 1)
                    op(sqbuf[:, 2 * q:2 * q + 2, :], rbuf[:, 2 * q:2 * q + 2, :], ACT.Square).then_inc(squared, 1)
                act.wait_ge(var_mm, n + 1)
                op(lnt[:, 1, :], ps[:, 6, 0:T], ACT.Sqrt, bias=C("eps"), scale=1.0 / D).then_inc(dev_ready, 1)
                for k in range(KT):
                    act.wait_ge(normed, KT * n + k + 1)
                    op(bufx[:, k, :], rbuf[:, k, :], ACT.Identity,
                       bias=ln_b[:, 2 * l + which, k:k + 1]).then_inc(x_ready, 1)

            def head_raw(l, i, j, m):
                tile_done(act, "in", l, 4 * j + m, i, 2 * HEADS_PER_ITER)
                b = 6 + m % 2
                if m < 3:
                    copy(g_cin[:, m, 2:2 + CTX], ps[:, b, CTXS])
                    copy(g_cin[:, m, 4 + CTX:4 + T], ps[:, b, LATS]).then_inc(raw_in, 1)
                else:
                    op(g_z[:, j % 2, :], ps[:, b, 0:T], ACT.Silu).then_inc(z_in, 1)

            def gdn(l):
                li = li_of[l]
                act.wait_ge(sp_in, li + 1)
                op(g_tmp[:, 4, 0, :], R("a_log")[:, 16 * li:16 * li + 16], ACT.Exp)
                raw = ps[:, 2, 0:96].rearrange("p (t c) -> p t c", t=TT)
                op(g_tmp[:, 3, :, :], raw[:, :, 16:32], ACT.Exp, scale=-1.0)
                op(g_tmp[:, 2, :, :], g_tmp[:, 2, :, :], ACT.Exp).then_inc(sp_exp, 1)
                act.wait_ge(sp_exp, li + 1)
                op(g_tmp[:, 5, :, :], g_tmp[:, 2, :, :], ACT.Ln, bias=1.0).then_inc(sp_ln, 1)
                act.wait_ge(cum_mm, li + 1)
                cum = ps[:, 3, 0:96].rearrange("p (w t c) -> p w t c", w=2, t=TT)
                a.step(op(g_tmp[:, 0, :, :], cum[:, 0, :, :], ACT.Exp))
                op(g_all[:, 3, :, :], cum[:, 1, :, :], ACT.Exp).then_inc(cum_ready, 1)
                act.wait_ge(pad_zero, li + 1)
                with act.Fori(0, H // HEADS_PER_ITER) as i:
                    for j in range(HEADS_PER_ITER):
                        gdn_head(l, i, j)

            def gdn_head(l, i, j):
                hh = i * HEADS_PER_ITER + (li_of[l] * H + j)
                act.dma_start(g_s0[:, j % 2, :, :], I["state"][hh]).then_inc(s0_in, 16)
                if j == 0:
                    for m in range(4):
                        head_raw(l, i, j, m)
                for m in range(3):
                    act.wait_ge(conv_done, hh * 3 + m + 1)
                    op(g_qkv[:, m, CTXS], g_acc[:, m, 0:CTX], ACT.Silu)
                    op(g_qkv[:, m, LATS], g_acc[:, m, 2 + CTX:CONVW], ACT.Silu).then_inc(silu_done, 1)
                act.wait_ge(silu_done, hh * 3 + 2)
                op(g_sq, g_qkv[:, 0:2, :], ACT.Square).then_inc(qk_sq, 1)
                act.wait_ge(nrm_mm, hh + 1)
                op(g_rs, ps[:, 2:4, 0:T], ACT.Sqrt, bias=C("eps")).then_inc(nrm_dev, 1)
                for m, dst in ((0, g_vt), (1, g_kt)):
                    act.wait_ge(kv_tr, hh * 2 + m + 1)
                    copy(dst.rearrange("p t c -> p (t c)"), ps[:, m, 0:T]).then_inc(kv_tok, 1)
                for d in range(2):
                    act.wait_ge(row_mm, hh * 2 + d + 1)
                    op(g_eq[:, d, :], ps[:, 4 + d, 0:T], ACT.Exp)
                    at = CHUNK - 1 if d == 0 else 0
                    rows = ps[:, 4 + d, 0:T].rearrange("p (n c) -> p n c", c=CHUNK)
                    op(g_last[:, d, :], rows[:, :, at], ACT.Exp)
                    act.wait_ge(row_masked, hh * 2 + d + 1)
                    for t in range(TT):
                        last = op(g_w[:, d, t, :], g_w[:, d, t, :], ACT.Exp, bias=g_head[:, 1, t, d:d + 1])
                    last.then_inc(decay_done, 1)
                for n, dst, bank in ((1, g_pa, 1), (2, g_pb, 0), (4, g_nd, 0), (5, g_ndt, 1), (7, g_pa, 1),
                                     (9, g_pb, 1), (10, g_nd, 0), (12, g_pb, 0), (13, g_nd, 1)):
                    for d in range(2):
                        act.wait_ge(inv_mm[d], hh * 15 + n + 1)
                        copy(dst[d].rearrange("p t c -> p (t c)"), ps[:, 4 + d + 2 * bank, 0:T]).then_inc(inv_cp[d], 1)
                for k, steps in enumerate(SCAN_ROUNDS):
                    for n, (ch, d, t, half, c0, first) in steps:
                        rows = slice(64 * half, 64 * half + 64)
                        act.wait_ge(vn_mm, hh * 12 + n + 1)
                        copy(g_v[rows, ch, :], ps[rows, ch, P:2 * P],
                             scale=g_head[rows, 4, t, d:d + 1]).then_inc(v_done, 1)
                    if j + 1 < HEADS_PER_ITER:
                        head_raw(l, i, j + 1, k)
                act.wait_ge(s_done, hh * 12 + 8)
                act.dma_start(O["state"][hh], g_state[:, 2:4, :]).then_inc(st_out, 16)
                act.wait_ge(os_mm, hh * 12 + 12)
                copy(g_o, ps[:, 4, 0:T]).then_inc(o_done, 1)
                act.wait_ge(o_sum, hh + 1)
                op(g_osq, g_o, ACT.Square).then_inc(o_sq, 1)
                act.wait_ge(o_nrm_mm, hh + 1)
                op(g_rs[:, 0, :], ps[:, 0, 0:T], ACT.Sqrt, bias=C("eps"), scale=1.0 / P).then_inc(o_dev, 1)

            def attention(l, heads, first_head, scale):
                a0 = att_at[l] + TT * first_head
                units = [(h, qt) for h in heads for qt in range(TT)]

                def exps(n):
                    nk = P if units[n][1] == 0 else T
                    act.wait_ge(max_done, a0 + n + 1)
                    if a0 + n >= 2:
                        act.wait_ge(pt_mm, a0 + n - 1)
                    op(a_p[:, n % 2, 0:nk], ps[:, n % 2, 0:nk], ACT.Exp, scale=scale, bias=a_st[:, n % 2, 1:2],
                       accum_out=a_st[:, n % 2, 2:3]).then_inc(exp_done, 1)

                exps(0)
                for n, (h, qt) in enumerate(units):
                    if n + 1 < len(units):
                        exps(n + 1)
                    nk = 1 if qt == 0 else 3
                    act.wait_ge(pt_mm, a0 + n + 1)
                    if a0 + n >= 2:
                        act.wait_ge(pv_mm, a0 + n - 1)
                    copy(a_pt[:, n % 2, 0:nk, :].rearrange("p t c -> p (t c)"),
                         ps[:, 2 + n % 2, 0:P * nk]).then_inc(pt_ev, 1)
                    if qt == TT - 1:
                        act.wait_ge(pv_mm, a0 + n + 1)
                        copy(bufo[:, h, :], ps[:, 4 + (n // TT) % 2, 0:T]).then_inc(oh_ev, 1)

            def gqa(l):
                for t in range(12):
                    tile_done(act, "in", l, t)
                    copy(q_qkv[:, t, :], ps[:, t % 2, 0:T]).then_inc(raw_ev, 1)
                    if t < 10:
                        act.wait_ge(raw_ev, t + 1)
                        op(q_sq[:, t, :], q_qkv[:, t, :], ACT.Square).then_inc(at_sq, 1)
                for n in range(10):
                    act.wait_ge(at_nmm, n + 1)
                    op(q_sq[:, n, :], ps[:, 2 + n % 2, 0:T], ACT.Sqrt, bias=C("eps"), scale=1.0 / P).then_inc(at_dev, 1)
                act.wait_ge(own_ready, 2)
                for kv in range(2):
                    act.wait_ge(vt_mm, kv + 1)
                    src = ps[:, kv, 0:T].rearrange("p (t c) -> p t c", t=TT)
                    copy(q_vall[:, kv, 0, :], src[:, 0, :])
                    copy(q_vall[:, kv, 2:4, :], src[:, 1:3, :]).then_inc(vt_ev, 1)
                attention(l, range(H), 0, QK_SCALE)

            def mla(l):
                for t in range(6):
                    tile_done(act, "in", l, t)
                    copy(m_c[:, t, :], ps[:, t % 2, 0:T]).then_inc(raw_ev, 1)
                    act.wait_ge(raw_ev, 12 + t + 1)
                    op(m_sq[:, t, :], m_c[:, t, :], ACT.Square).then_inc(at_sq, 1)
                used(act, unit_at["mix", l] + 3)
                copy(m_kr[0:64, :], ps[0:64, 0, 0:T]).then_inc(raw_ev, 1)
                for m, n in enumerate((512, 256)):
                    act.wait_ge(at_nmm, 10 + m + 1)
                    op(m_sq[:, m, :], ps[:, 2 + m, 0:T], ACT.Sqrt, bias=C("eps"), scale=1.0 / n).then_inc(at_dev, 1)
                for half in range(2):
                    job = 0
                    ups = 13 * half
                    for k in range(2):
                        for hd in range(2):
                            for rows, dst in ((P, m_qn), (64, m_qr)):
                                if hd == 1 and rows == 64:
                                    used(act, unit_at["mix", l] + 4 + 3 * half + k)
                                else:
                                    ups += 1
                                    act.wait_ge(up_mm, ups)
                                copy(dst[0:rows, 2 * k + hd, :], ps[0:rows, (job + 1) % 2, 0:T]).then_inc(up_ev, 1)
                                job += 1
                    for n in range(8):
                        if n < 7:
                            ups += 1
                            act.wait_ge(up_mm, ups)
                        else:
                            used(act, unit_at["mix", l] + 6 + 3 * half)
                        dst = m_kn[:, n, :] if n < 4 else m_v[:, n - 4, :]
                        copy(dst, ps[:, (job + 1) % 2, 0:512]).then_inc(up_ev, 1)
                        job += 1
                    attention(l, range(4 * half, 4 * half + 4), 4 * half, MLA_SCALE)

            def gathered(S, n, j):
                for q in range(2):
                    act.wait_ge(S["ga"], n * 3 + q + 1)
                    copy(e_hs[:, j, 4 * q:4 * q + 4, :].rearrange("p k c -> p (k c)"),
                         ps[:, 5 + q, :]).then_inc(S["ga_ev"], 1)

            def gate_silu(S, e):
                op(e_sg[:, e % 2, :], ps[:, e % 2, 0:DE], ACT.Silu).then_inc(S["sg"], 1)

            def hidden_t(S, n, e):
                act.wait_ge(S["tr"], n + 1)
                b = e % 2
                copy(e_hidT[:, b, :, :].rearrange("p f c -> p (f c)"),
                     ps[:, 2, 256 * b:256 * b + 256]).then_inc(S["trv"], 1)

            def y_high(S):
                copy(e_yhi[:, :].rearrange("p (y c) -> p y c", y=2), ps[:, 3:5, :]).then_inc(S["yhi"], 1)

            def moe(l):
                act.wait_ge(rt_mm, l + 1)
                op(e_rt[:, 0, :], ps[:, 2, 0:TT * NE], ACT.Sigmoid).then_inc(score_ready, 1)
                for n in range(2 * TT):
                    act.wait_ge(tk_mm, 2 * TT * l + n + 1)
                    copy(e_hi[:, n // 2, 512 * (n % 2):512 * (n % 2) + 512], ps[:, 5 + n % 2, :]).then_inc(tk_hi, 1)
                act.wait_ge(row2_mm, l + 1)
                copy(e_sidrow[:, :], ps[:, 2, P:P + T]).then_inc(row2_ready, 1)
                u0, per = unit_at["moe", l], len(MOE_UNITS)
                with act.Fori(0, NG // 2) as i:
                    for kind, j, e in MOE_STEPS:
                        gg = i * 2 + (NG * l + j)
                        n = i * (2 * EPG) + (NE * l + EPG * j + e)
                        if kind == "G":
                            gathered(F, gg, j)
                        elif kind == "U":
                            used(act, u0 + MOE_UNIT_OF[j, e, 1], i * per)
                            gate_silu(F, e)
                        elif kind == "T":
                            hidden_t(F, n, e)
                        elif kind == "D" and e == EPG - 1:
                            used(act, u0 + MOE_UNIT_OF[j, e, 2], i * per)
                            y_high(F)
                act.wait_ge(flags_ready, l + 1)
                with act.Fori(0, NG) as g:
                    for b in range(2):
                        n = g * 2 + (2 * NG * l + b)
                        more = act.value_load(flags[0:1, g, b:b + 1], min_val=0, max_val=1)
                        with act.If(more > 0):
                            gathered(X, n, 0)
                            for e in range(EPG):
                                for part in range(PARTS):
                                    k = PARTS * e + part
                                    if k:
                                        act.wait_ge(x_piece, n * (EPG * PARTS) + k)
                                    src = I["moe"][g * EPG + (NE * l + e), :, part * UNIT:(part + 1) * UNIT]
                                    act.dma_start(piece_buf(part), src).then_inc(x_w, 16)
                                gate_silu(X, e)
                                hidden_t(X, n * EPG + e, e)
                            act.wait_ge(x_piece, (n + 1) * (EPG * PARTS))
                            y_high(X)
                            act.wait_ge(X["sc_ev"], n * KT + KT)
                            copy(e_sg[:, 0, 0:1], C("eps"))
                        with act.Else():
                            act.sem_inc(X["ga_ev"], 2)
                            act.sem_inc(X["sg"], EPG)
                            act.sem_inc(X["trv"], EPG)
                            act.sem_inc(X["yhi"], 1)
                            act.sem_inc(x_w, 16 * EPG * PARTS)

            act.wait_ge(params_in, 16)
            op(silc[:, :, :], cond, ACT.Silu).then_inc(cond_ready, 1)
            act.wait_ge(consts_in, 16)
            for l, kind in enumerate(KINDS):
                {"gdn": gdn, "gqa": gqa, "mla": mla}[kind](l)
                layer_norm(2 * l, l, 0, bufh, bufo)
                moe(l)
                layer_norm(2 * l + 1, l, 1, bufo, bufh)

        @block.vector
        def _(dve):
            V = nc.vector
            v = Chain(dve, chain_v)
            tt_, ts_, stt = V.tensor_tensor, V.tensor_scalar, V.scalar_tensor_tensor

            def modulation(l):
                used(dve, unit_at["ada", l] + ADA_UNITS - 1)
                raw = ps[:, 7, 0:96].rearrange("p (m s) -> p m s", s=2)
                tt_(mod[:, l, :, :], raw, wide(b_ada[:, l, :], 2), ALU.add).then_inc(mod_ready, 1)
                dve.wait_ge(mod_ready, 3 * l + 1)
                for s in (1, 4):
                    rows = mod[:, l, KT * s:KT * s + 2 * KT, :]
                    ts_(rows, rows, 1.0, None, ALU.add).then_inc(mod_ready, 1)
                dve.wait_ge(mod_ready, 3 * l + 3)

            def modulate(l, which):
                n = 2 * l + which
                for k in range(KT):
                    if n == 0:
                        dve.wait_ge(x_in, 16)
                    else:
                        dve.wait_ge(x_ready, KT * (n - 1) + k + 1)
                    for seg, cols in enumerate((CTXS, LATS)):
                        last = ts_(bufh[:, k, cols], bufx[:, k, cols], mrow(l, 3 * which + 1, k, seg),
                                   mrow(l, 3 * which, k, seg), ALU.mult, ALU.add)
                    last.then_inc(h_ready, 1)

            def residual(l, which, src, rbuf, ready):
                n = 2 * l + which
                dve.wait_ge(ax_ready, n + 1)
                for k in range(KT):
                    ready(k)
                    for seg, cols in enumerate((CTXS, LATS)):
                        last = stt(rbuf[:, k, cols], src(k)[:, cols], mrow(l, 3 * which + 2, k, seg), bufx[:, k, cols],
                                   ALU.mult, ALU.add)
                    last.then_inc(r_ready, 1)

            def layer_norm(n, l, which, rbuf):
                dve.wait_ge(mean_ready, n + 1)
                dve.wait_ge(r_ready, KT * (n + 1))
                for q in range(4):
                    tiles = rbuf[:, 2 * q:2 * q + 2, :]
                    tt_(tiles, tiles, spread(lnt[:, 0, :], 2), ALU.subtract).then_inc(centred, 1)
                dve.wait_ge(dev_ready, n + 1)
                v.step(V.reciprocal(lnt[:, 1, :], lnt[:, 1, :]))
                v.wait()
                dve.wait_ge(centred, 4 * n + 4)
                for k in range(KT):
                    stt(rbuf[:, k, :], rbuf[:, k, :], ln_g[:, 2 * l + which, k:k + 1], lnt[:, 1, :],
                        ALU.mult, ALU.mult).then_inc(normed, 1)

            def gdn(l):
                li = li_of[l]
                dve.wait_ge(ab_mm, li + 1)
                raw = ps[:, 2, 0:96].rearrange("p (t c) -> p t c", t=TT)
                v.step(tt_(g_tmp[:, 0, :, :], raw[:, :, 0:16], spread(R("dt_bias")[:, 16 * li:16 * li + 16], TT), ALU.add))
                v.wait()
                v.step(ts_(g_tmp[:, 1, :, :], g_tmp[:, 0, :, :], 0.0, None, ALU.max))
                v.wait()
                stt(g_tmp[:, 2, :, :], g_tmp[:, 1, :, :], -2.0, g_tmp[:, 0, :, :], ALU.mult, ALU.add).then_inc(sp_in, 1)
                dve.wait_ge(sp_exp, li + 1)
                v.step(ts_(g_tmp[:, 3, :, :], g_tmp[:, 3, :, :], 1.0, None, ALU.add))
                v.wait()
                v.step(V.reciprocal(g_all[:, 4, :, :], g_tmp[:, 3, :, :]))
                v.wait()
                v.step(ts_(g_all[:, 5, :, :], g_all[:, 4, :, :], -1.0, None, ALU.mult))
                dve.wait_ge(sp_ln, li + 1)
                v.step(tt_(g_tmp[:, 1, :, :], g_tmp[:, 1, :, :], g_tmp[:, 5, :, :], ALU.add))
                v.wait()
                stt(g_all[:, 0, :, :], g_tmp[:, 1, :, :], -1.0, spread(g_tmp[:, 4, 0, :], TT),
                    ALU.mult, ALU.mult).then_inc(g_ready, 1)
                dve.wait_ge(cum_mm, li + 1)
                cum = ps[:, 3, 0:48].rearrange("p (t c) -> p t c", t=TT)
                dve.wait_ge(cum_ready, 2 * li + 1)
                v.step(ts_(g_all[:, 1, :, :], cum, -1.0, None, ALU.mult))
                ts_(g_all[:, 2, :, :], g_tmp[:, 0, :, :], -1.0, None, ALU.mult).then_inc(cum_ready, 1)
                dve.wait_ge(cum_ready, 2 * li + 2)
                dve.wait_ge(pad_zero, li + 1)
                with dve.Fori(0, H // HEADS_PER_ITER) as i:
                    v.enter(i, HEADS_PER_ITER * 16)
                    for j in range(HEADS_PER_ITER):
                        gdn_head(l, i, j)
                    turns = H // HEADS_PER_ITER
                v.leave(turns)
                residual(l, 0, lambda k: ps[:, k % 2, :], bufh, lambda k: tile_done(dve, "out", l, k))

            def gdn_head(l, i, j):
                li = li_of[l]
                h = i * HEADS_PER_ITER + j
                hh = i * HEADS_PER_ITER + (li * H + j)
                cols = g_all.rearrange("p a b (d h) -> p h (a b) d", h=H)
                V.tensor_copy(g_head.rearrange("p a b d -> p (a b) d"), cols[:, h, :, :]).then_inc(head_cols, 1)
                v.step(V.tensor_copy(g_taps.rearrange("p a b -> p (a b)"), conv[:, hh, :]))
                v.wait()
                for m in range(3):
                    dve.wait_ge(raw_in, hh * 3 + m + 1)
                    acc = g_acc[:, m, :]
                    v.step(ts_(acc, g_cin[:, m, 0:CONVW], g_taps[:, m, 0:1], None, ALU.mult))
                    for tap in range(1, TAPS):
                        v.wait()
                        last = stt(acc, g_cin[:, m, tap:tap + CONVW], g_taps[:, m, tap:tap + 1], acc, ALU.mult, ALU.add)
                        if tap < TAPS - 1:
                            v.step(last)
                    last.then_inc(conv_done, 1)
                for d in range(2):
                    dve.wait_ge(row_mm, hh * 2 + d + 1)
                    tt_(g_w[:, d, :, :], ps[:, 4 + d, 0:T].rearrange("p (t c) -> p t c", t=TT),
                        spread(C(f"inv{d}"), TT), ALU.subtract).then_inc(row_masked, 1)
                dve.wait_ge(nrm_dev, hh + 1)
                v.step(V.reciprocal(g_rs, g_rs))
                v.wait()
                dve.wait_ge(silu_done, hh * 3 + 3)
                stt(g_qkv[:, 0, :], g_qkv[:, 0, :], QK_SCALE, g_rs[:, 0, :], ALU.mult, ALU.mult).then_inc(qk_ready, 1)
                tt_(g_qkv[:, 1, :], g_qkv[:, 1, :], g_rs[:, 1, :], ALU.mult).then_inc(qk_ready, 1)
                dve.wait_ge(gram_mm, hh * 2 + 2)
                dve.wait_ge(head_cols, hh + 1)
                for d in range(2):
                    dve.wait_ge(strict_done, hh * 2 + d + 1)
                    for t in range(TT):
                        last = stt(g_n[d][:, t, :], ps[:, 2, P * t:P * t + P], g_head[:, 5, t, d:d + 1], g_n[d][:, t, :],
                                   ALU.mult, ALU.mult)
                    last.then_inc(n_done, 1)
                for d in range(2):
                    wd = g_w[:, d, :, :].rearrange("p t c -> p (t c)")
                    tt_(wd, wd, ps[:, 3, 0:T], ALU.mult).then_inc(w_done, 1)
                for d in range(2):
                    dve.wait_ge(inv_mm[d], hh * 15 + 1)
                    src = ps[:, 4 + d, 0:T].rearrange("p (t c) -> p t c", t=TT)
                    for dst, mask in ((g_t32, "off32"), (g_t64, "off64"), (g_ndt, "diag16")):
                        last = tt_(dst[d], src, spread(C(mask), TT), ALU.mult)
                    last.then_inc(inv_x[d], 1)
                for s, (n, bank) in enumerate(((3, 1), (6, 0), (8, 0), (11, 1), (14, 0))):
                    for d in range(2):
                        dve.wait_ge(inv_mm[d], hh * 15 + n + 1)
                        dve.wait_ge(inv_x[d], hh * 6 + s + 1)
                        x = g_x[d].rearrange("p t c -> p (t c)")
                        tt_(x, x, ps[:, 4 + d + 2 * bank, 0:T], ALU.add).then_inc(inv_x[d], 1)
                for k, steps in enumerate(SCAN_ROUNDS):
                    for n, (ch, d, t, half, c0, first) in steps:
                        rows = slice(64 * half, 64 * half + 64)
                        dve.wait_ge(ks_mm, hh * 12 + n + 1)
                        stt(g_y[rows, ch, :], ps[rows, ch, 0:P], g_head[rows, 2, t, d:d + 1], g_vt[rows, t, :],
                            ALU.mult, ALU.add).then_inc(y_done, 1)
                    for n, (ch, d, t, half, c0, first) in steps:
                        dve.wait_ge(os_mm, hh * 12 + n + 1)
                        if k:
                            dve.wait_ge(s_done, hh * 12 + SCAN_PREV[n] + 1)
                        ck = c0 // CHUNK
                        stt(g_state[:, ch, :], scan_state(ch, d, first, j), g_last[:, d, ck:ck + 1],
                            ps[:, ch, 3 * P:4 * P], ALU.mult, ALU.add).then_inc(s_done, 1)
                dve.wait_ge(o_done, hh + 1)
                tt_(g_o, g_o, ps[:, 5, 0:T], ALU.add).then_inc(o_sum, 1)
                dve.wait_ge(o_dev, hh + 1)
                v.step(V.reciprocal(g_rs[:, 0, :], g_rs[:, 0, :]))
                v.wait()
                v.step(stt(g_o, g_o, R("gdn_g")[:, li:li + 1], g_rs[:, 0, :], ALU.mult, ALU.mult))
                v.wait()
                dve.wait_ge(z_in, hh + 1)
                dve.wait_ge(st_out, hh * 16 + 16)
                tt_(bufo[:, h, :], g_o, g_z[:, j % 2, :], ALU.mult).then_inc(head_done, 1)

            def attention(l, heads, first_head, scale):
                a0 = att_at[l] + TT * first_head
                units = [(h, qt) for h in heads for qt in range(TT)]

                def maximum(n):
                    nk = P if units[n][1] == 0 else T
                    dve.wait_ge(sc_mm, a0 + n + 1)
                    v.step(V.reduce_max(a_st[:, n % 2, 0:1], ps[:, n % 2, 0:nk], AX.X))
                    v.wait()
                    ts_(a_st[:, n % 2, 1:2], a_st[:, n % 2, 0:1], -scale, None, ALU.mult).then_inc(max_done, 1)

                maximum(0)
                for n, (h, qt) in enumerate(units):
                    if n + 1 < len(units):
                        maximum(n + 1)
                    nk = P if qt == 0 else T
                    dve.wait_ge(exp_done, a0 + n + 1)
                    v.step(V.reciprocal(a_st[:, n % 2, 3:4], a_st[:, n % 2, 2:3]))
                    v.wait()
                    pb = a_p[:, n % 2, 0:nk]
                    ts_(pb, pb, a_st[:, n % 2, 3:4], None, ALU.mult).then_inc(p_done, 1)

            def rotate(dst, x, bank, rows, cos, sin, before):
                if before:
                    dve.wait_ge(rot_done, before)
                n = x.shape[1]
                rot = ps[0:rows, bank, 0:n * LAT].rearrange("p (n c) -> p n c", n=n)
                tmp = a_tmp[0:rows, 0:n, :]
                v.step(tt_(tmp, rot, spread(C(sin, rows), n), ALU.mult))
                v.step(tt_(x, x, spread(C(cos, rows), n), ALU.mult))
                v.wait()
                return tt_(dst, x, tmp, ALU.add)

            def gqa(l):
                for n in range(10):
                    dve.wait_ge(at_dev, n + 1)
                    v.step(V.reciprocal(q_sq[:, n, :], q_sq[:, n, :]))
                    v.wait()
                    g = R("gqa_q") if n < H else R("gqa_k")
                    stt(q_qkv[:, n, :], q_qkv[:, n, :], g, q_sq[:, n, :], ALU.mult, ALU.mult).then_inc(at_normed, 1)
                dve.wait_ge(at_normed, 10)
                for kv in range(2):
                    V.tensor_copy(q_kall[:, kv, 0:CTX], q_qkv[:, H + kv, CTXS]).then_inc(own_ready, 1)
                for n in range(5):
                    dve.wait_ge(rot_mm, n + 1)
                    x = q_qkv[:, 2 * n:2 * n + 2, LATS]
                    dst = x if n < 4 else q_kall[:, :, P + PAST:NK]
                    rotate(dst, x, 4 + n % 2, P, "cos128", "sin128", n).then_inc(rot_done, 1)
                attention(l, range(H), 0, QK_SCALE)
                residual(l, 0, lambda k: ps[:, k % 2, :], bufh, lambda k: tile_done(dve, "out", l, k))

            def mla(l):
                dve.wait_ge(at_dev, 10 + 2)
                v.step(V.reciprocal(m_sq[:, 0:2, :], m_sq[:, 0:2, :]))
                v.wait()
                for n in range(6):
                    g = R("mla_q")[:, n:n + 1] if n < 4 else R("mla_kv")[:, n - 4:n - 3]
                    stt(m_c[:, n, :], m_c[:, n, :], g, m_sq[:, 0 if n < 4 else 1, :],
                        ALU.mult, ALU.mult).then_inc(at_normed, 1)
                dve.wait_ge(at_normed, 10 + 6)
                v.step(V.tensor_copy(m_krall[0:64, 0:CTX], m_kr[0:64, CTXS]))
                for n in range(2):
                    V.tensor_copy(m_ckv[:, n, 0:CTX], m_c[:, 4 + n, CTXS]).then_inc(own_ready, 1)
                    V.tensor_copy(m_ckv[:, n, P + PAST:NK], m_c[:, 4 + n, LATS]).then_inc(own_ready, 1)
                dve.wait_ge(rot_mm, 6)
                dve.wait_ge(raw_ev, 12 + 7)
                rotate(m_krall[0:64, P + PAST:NK].rearrange("p (o c) -> p o c", o=1),
                       m_kr[0:64, LATS].rearrange("p (o c) -> p o c", o=1), 4, 64, "cos64", "sin64",
                       5).then_inc(rot_done, 1)
                for half in range(2):
                    for m in range(2):
                        dve.wait_ge(rot_mm, 6 + 2 * half + m + 1)
                        x = m_qr[0:64, 2 * m:2 * m + 2, LATS]
                        rotate(x, x, 4 + m, 64, "cos64", "sin64", 6 + 2 * half + m).then_inc(rot_done, 1)
                        dve.wait_ge(rot_done, 6 + 2 * half + m + 1)
                    attention(l, range(4 * half, 4 * half + 4), 4 * half, MLA_SCALE)
                residual(l, 0, lambda k: ps[:, k % 2, :], bufh, lambda k: tile_done(dve, "out", l, k))

            def route(l):
                e_ = [e_rt[:, n, :] for n in range(10)]
                score, sel, t1, t2, t3, m3, o1, o2, oh, comb = e_
                as16 = lambda x: x.rearrange("p (t e) -> p t e", t=TT)
                dve.wait_ge(score_ready, l + 1)
                v.step(tt_(as16(sel), as16(score), spread(R("router_b"), TT), ALU.add))
                v.wait()
                pair = sel.rearrange("p (g a b) -> p g a b", a=2, b=2)
                hi = t1[:, 0:24].rearrange("p (g a) -> p g a", a=2)
                lo = t2[:, 0:24].rearrange("p (g a) -> p g a", a=2)
                v.step(tt_(hi, pair[:, :, :, 0], pair[:, :, :, 1], ALU.max))
                v.step(tt_(lo, pair[:, :, :, 0], pair[:, :, :, 1], ALU.min))
                v.wait()
                first, second, third = t3[:, 0:12], t3[:, 12:24], t3[:, 24:36]
                v.step(tt_(first, hi[:, :, 0], hi[:, :, 1], ALU.max))
                v.step(tt_(second, hi[:, :, 0], hi[:, :, 1], ALU.min))
                v.step(tt_(third, lo[:, :, 0], lo[:, :, 1], ALU.max))
                v.wait()
                v.step(tt_(second, second, third, ALU.max))
                v.wait()
                v.step(tt_(first, first, second, ALU.add))
                v.wait()

                def one_hot(out, x, n, weights, best):
                    v.step(V.tensor_reduce(best, x, AX.X, ALU.max))
                    v.wait()
                    v.step(tt_(out, x, wide(best, n), ALU.is_equal))
                    v.wait()
                    v.step(tt_(out, out, spread(weights, TT), ALU.mult))
                    v.wait()
                    v.step(V.tensor_reduce(best, out, AX.X, ALU.max))
                    v.wait()
                    return tt_(out, out, wide(best, n), ALU.is_equal)

                gs = first.rearrange("p (t g) -> p t g", t=TT)
                ohg = oh[:, 0:TT * NG].rearrange("p (t g) -> p t g", t=TT)
                one_hot(ohg, gs, NG, C("first4"), m3[:, 0:TT]).then_inc(oh_ready, 1)
                dve.wait_ge(oh_ready, l + 1)
                for n in range(2 * TT):
                    dve.wait_ge(tk_hi, 2 * TT * l + n + 1)
                    cols = slice(512 * (n % 2), 512 * (n % 2) + 512)
                    tt_(e_lo[:, n // 2, cols], ps[:, 5 + n % 2, :], e_hi[:, n // 2, cols].bitcast(F32),
                        ALU.subtract).then_inc(tk_lo, 1)
                dve.wait_ge(rk_mm, l + 1)
                rank = ps[:, 2, 64:76].rearrange("p (t g) -> p t g", t=TT)
                slot = t1[:, 0:12].rearrange("p (t g) -> p t g", t=TT)
                v.step(V.tensor_copy(e_cnt[:, :], ps[:, 2, 80:84]))
                v.step(tt_(slot, rank, spread(C("group_off"), TT), ALU.add))
                v.wait()
                v.step(tt_(slot, slot, ohg, ALU.mult))
                v.wait()
                V.tensor_reduce(e_sid[:, 0, :], slot, AX.X, ALU.add).then_inc(sid_ready, 1)
                for b in range(2):
                    last = ts_(flags[:, :, b], e_cnt[:, :], float(P * (b + 1)), None, ALU.is_gt)
                    if b:
                        last.then_inc(flags_ready, 1)
                sel4, tmp4 = sel.rearrange("p (n e) -> p n e", e=EPG), t2.rearrange("p (n e) -> p n e", e=EPG)
                v.step(tt_(tmp4, sel4, wide(oh[:, 0:TT * NG], EPG), ALU.mult))
                v.step(ts_(m3[:, 16:16 + TT * NG], oh[:, 0:TT * NG], BIG, -BIG, ALU.mult, ALU.add))
                v.wait()
                v.step(tt_(tmp4, tmp4, wide(m3[:, 16:16 + TT * NG], EPG), ALU.add))
                v.wait()
                v.step(one_hot(as16(o1), as16(t2), NE, C("first16"), m3[:, 0:TT]))
                v.wait()
                v.step(stt(t2, o1, -4 * BIG, t2, ALU.mult, ALU.add))
                v.wait()
                v.step(one_hot(as16(o2), as16(t2), NE, C("first16"), m3[:, 0:TT]))
                v.wait()
                v.step(tt_(o1, o1, o2, ALU.add))
                v.wait()
                v.step(tt_(o1, o1, score, ALU.mult))
                v.wait()
                v.step(V.tensor_reduce(m3[:, 0:TT], as16(o1), AX.X, ALU.add))
                v.wait()
                v.step(V.reciprocal(m3[:, 3:3 + TT], m3[:, 0:TT]))
                v.wait()
                v.step(tt_(as16(comb), as16(o1), wide(m3[:, 3:3 + TT], NE), ALU.mult))
                dve.wait_ge(row2_ready, l + 1)
                dve.wait_ge(sid_ready, l + 1)
                v.wait()

            def pick(S, j, column):
                base, slot = C("block_base")[:, bass.ds(column, 1)], C("block_slot")[:, bass.ds(column, 1)]
                v.step(ts_(e_sid[:, 1 + j, :], e_sid[:, 0, :], base, None, ALU.subtract))
                v.step(ts_(e_put[:, j, :], e_sidrow[:, :], slot, None, ALU.is_equal))
                v.wait()
                for t in range(TT):
                    last = ts_(e_pick[:, j, t, :], C("iota"), e_sid[:, 1 + j, t:t + 1], None, ALU.is_equal)
                last.then_inc(S["pick"], 1)

            def weights(S, n, j):
                dve.wait_ge(S["ga"], n * 3 + 3)
                V.tensor_copy(e_cs[:, j, :], ps[:, 7, 96 + 4 * j:100 + 4 * j]).then_inc(S["cs"], 1)
                dve.wait_ge(S["cs"], n + 1)

            def hidden(S, n, j, e):
                dve.wait_ge(S["sg"], n + 1)
                b = e % 2
                stt(e_hid[:, b, :], ps[:, b, DE:2 * DE], e_cs[:, j, e:e + 1], e_sg[:, b, :],
                    ALU.mult, ALU.mult).then_inc(S["hid"], 1)

            def y_low(S, n):
                dve.wait_ge(S["yhi"], n + 1)
                tt_(e_ylo[:, :].rearrange("p (y c) -> p y c", y=2), ps[:, 3:5, :],
                    e_yhi[:, :].bitcast(F32).rearrange("p (y c) -> p y c", y=2), ALU.subtract).then_inc(S["ylo"], 1)

            def scattered(S, n):
                for ft in range(KT):
                    dve.wait_ge(S["sc"], n * KT + ft + 1)
                    tt_(bufo[:, ft, :], bufo[:, ft, :], ps[:, 5 + ft % 2, 0:T], ALU.add).then_inc(S["sc_ev"], 1)

            def moe(l):
                route(l)
                dve.wait_ge(o_zero, l + 1)
                with dve.Fori(0, NG // 2) as i:
                    v.enter(i, 4)
                    for j in range(2):
                        pick(F, j, i * 2 + j)
                    for kind, j, e in MOE_STEPS:
                        gg = i * 2 + (NG * l + j)
                        n = i * (2 * EPG) + (NE * l + EPG * j + e)
                        if kind == "G":
                            weights(F, gg, j)
                        elif kind == "U":
                            hidden(F, n, j, e)
                        elif kind == "D" and e == EPG - 1:
                            y_low(F, gg)
                        elif kind == "S":
                            if j == 1:
                                dve.wait_ge(F["sc_ev"], gg * KT)
                            scattered(F, gg)
                v.leave(NG // 2)
                dve.wait_ge(F["sc_ev"], NG * KT * (l + 1))
                with dve.Fori(0, NG) as g:
                    v.enter(g, 4)
                    for b in range(2):
                        n = g * 2 + (2 * NG * l + b)
                        more = dve.value_load(flags[0:1, g, b:b + 1], min_val=0, max_val=1)
                        before = v.n
                        with dve.If(more > 0):
                            pick(X, 0, g * 2 + (NG + b))
                            weights(X, n, 0)
                            for e in range(EPG):
                                hidden(X, n * EPG + e, 0, e)
                            y_low(X, n)
                            scattered(X, n)
                            dve.wait_ge(X["sc_ev"], n * KT + KT)
                            V.memset(e_cnt[:, 0:1], 0.0)
                        with dve.Else():
                            dve.sem_inc(chain_v, v.n - before)
                            dve.sem_inc(X["pick"], 1)
                            dve.sem_inc(X["cs"], 1)
                            dve.sem_inc(X["hid"], EPG)
                            dve.sem_inc(X["ylo"], 1)
                            dve.sem_inc(X["sc_ev"], KT)
                v.leave(NG)
                residual(l, 1, lambda k: bufo[:, k, :], bufo, lambda k: None)

            dve.wait_ge(params_in, 16)
            dve.wait_ge(consts_in, 16)
            for l, kind in enumerate(KINDS):
                modulation(l)
                modulate(l, 0)
                {"gdn": gdn, "gqa": gqa, "mla": mla}[kind](l)
                layer_norm(2 * l, l, 0, bufh)
                modulate(l, 1)
                moe(l)
                layer_norm(2 * l + 1, l, 1, bufo)

        @block.gpsimd
        def _(pool):
            G = nc.gpsimd

            def scale_residual(n):
                pool.wait_ge(h_ready, KT * (n + 1))
                G.tensor_scalar(bufx[:, :, :], bufx[:, :, :], ALPHA, None, ALU.mult).then_inc(ax_ready, 1)

            def gdn(l):
                li = li_of[l]
                pool.wait_ge(h_ready, KT * (2 * l + 1))
                G.memset(g_cin, 0.0)
                G.memset(g_y, 0.0)
                G.memset(g_zero, 0.0).then_inc(pad_zero, 1)
                scale_residual(2 * l)
                with pool.Fori(0, H // HEADS_PER_ITER) as i:
                    for j in range(HEADS_PER_ITER):
                        hh = i * HEADS_PER_ITER + (li * H + j)
                        for d in range(2):
                            pool.wait_ge(decay_done, hh * 2 + d + 1)
                            G.tensor_tensor(g_n[d], g_w[:, d, :, :], spread(C(f"lt{d}"), TT), ALU.mult)\
                                .then_inc(strict_done, 1)
                        for d in range(2):
                            pool.wait_ge(n_done, hh * 2 + d + 1)
                            G.tensor_tensor(g_nd[d], g_n[d], spread(C("diag16"), TT), ALU.mult).then_inc(nd_done, 1)
                            pool.wait_ge(nd_done, hh * 2 + d + 1)
                            G.tensor_tensor(g_x[d], g_nd[d], spread(ident, TT), ALU.add).then_inc(x1_done, 1)
                        pool.wait_ge(kv_tok, hh * 2 + 2)
                        pool.wait_ge(head_cols, hh + 1)
                        for d in range(2):
                            last = G.tensor_tensor(g_kd[:, d, :, :], g_kt, wide(g_head[:, 3, :, d], P), ALU.mult)
                        last.then_inc(kd_done, 1)
                        pool.wait_ge(qk_ready, hh * 2 + 2)
                        for d in range(2):
                            G.tensor_tensor(g_eq[:, d, :], g_eq[:, d, :], g_qkv[:, 0, :], ALU.mult).then_inc(qe_done, 1)

            def gqa(l):
                pool.wait_ge(h_ready, KT * (2 * l + 1))
                pool.dma_start(q_kall[:, :, P:P + PAST], I["cache_k"]).then_inc(cache_in, 16)
                pool.dma_start(q_vall[:, :, 1, :], I["cache_v"]).then_inc(cache_in, 16)
                scale_residual(2 * l)
                pool.wait_ge(at_normed, 10)
                pool.wait_ge(raw_ev, 12)
                pool.dma_start(O["cache_k"], q_qkv[:, 8:10, CTXS]).then_inc(cache_out, 16)
                pool.dma_start(O["cache_v"], q_qkv[:, 10:12, CTXS]).then_inc(cache_out, 16)
                pool.wait_ge(cache_out, 16 * 2)

            def mla(l):
                pool.wait_ge(h_ready, KT * (2 * l + 1))
                pool.dma_start(m_ckv[:, :, P:P + PAST], I["cache_ckv"]).then_inc(cache_in, 16)
                pool.dma_start(m_krall[0:64, P:P + PAST], I["cache_kr"]).then_inc(cache_in, 16)
                scale_residual(2 * l)
                pool.wait_ge(at_normed, 10 + 6)
                pool.wait_ge(raw_ev, 12 + 7)
                pool.dma_start(O["cache_ckv"], m_c[:, 4:6, CTXS]).then_inc(cache_out, 16)
                pool.dma_start(O["cache_kr"], m_kr[0:64, CTXS]).then_inc(cache_out, 16)
                pool.wait_ge(cache_out, 16 * 4)

            def moe(l):
                pool.wait_ge(h_ready, KT * (2 * l + 2))
                G.memset(bufo[:, :, :], 0.0).then_inc(o_zero, 1)
                scale_residual(2 * l + 1)

            pool.dma_start(con[:, :], I["consts"]).then_inc(consts_in, 16)
            pool.dma_start(bufx[:, :, :], I["x"]).then_inc(x_in, 16)
            for l, kind in enumerate(KINDS):
                {"gdn": gdn, "gqa": gqa, "mla": mla}[kind](l)
                moe(l)


INPUTS = ["x", "state", "cache_k", "cache_v", "cache_ckv", "cache_kr", "params", "consts", "w_ada", "gdn_w_in",
          "gdn_w_out", "gqa_w_in", "gqa_w_out", "mla_w_in", "mla_w_kr", "mla_w_q_up", "mla_w_kv_up", "mla_w_out", "moe"]
OUTPUTS = {"y": (P, KT, T), "state": (2 * H, P, 2, P), "cache_k": (P, 2, P), "cache_v": (P, 2, P),
           "cache_ckv": (P, 2, P), "cache_kr": (P // 2, P)}


def layout(x_prompt, x_sample, state_gdn, cache_gqa_k, cache_gqa_v, cache_mla_ckv, cache_mla_krope,
           c, c_ctx, w_ada, b_ada, ln_mix_g, ln_mix_b, ln_ffn_g, ln_ffn_b,
           gdn_w_in, gdn_conv, gdn_a_log, gdn_dt_bias, gdn_norm_g, gdn_w_out,
           gqa_w_in, gqa_q_norm, gqa_k_norm, gqa_w_out,
           mla_w_in, mla_q_norm, mla_kv_norm, mla_w_q_up, mla_w_kv_up, mla_w_out,
           router_w, router_b, moe_w_gate, moe_w_up, moe_w_down):
    cc = np.ascontiguousarray

    def units(w, width=2 * P):
        w = w.reshape(-1, w.shape[-2] // P, P, w.shape[-1] // width, width // P, P)
        return cc(w.transpose(0, 3, 2, 4, 1, 5)).reshape(w.shape[0] * w.shape[3], P, -1)

    def feat(a):
        return a.reshape(-1, P).T

    x = np.concatenate([x_prompt[0], x_sample[0]], axis=0).T.reshape(KT, P, T).transpose(1, 0, 2)
    hd = H * P
    per_head = [gdn_w_in[:, :, o * hd:(o + 1) * hd].reshape(2, D, H, P) for o in range(4)]
    w_in = np.stack(per_head, axis=3).reshape(2, D, H * 4 * P)
    w_ab = gdn_w_in[:, :, 4 * hd:].reshape(2, KT, P, 32).transpose(2, 0, 1, 3).reshape(P, -1)
    taps = gdn_conv.reshape(2, TAPS, 3, H, P).transpose(4, 0, 3, 2, 1).reshape(P, -1)
    rows = lambda a: np.broadcast_to(a.reshape(1, -1), (P, a.size))
    ln = lambda m, f: feat(np.stack([m, f], axis=1))
    params = np.concatenate([
        np.stack([feat(c_ctx), feat(c[0])], axis=2).reshape(P, -1), feat(b_ada),
        ln(ln_mix_g, ln_ffn_g), ln(ln_mix_b, ln_ffn_b), taps, feat(gdn_norm_g), feat(gqa_q_norm), feat(gqa_k_norm),
        feat(mla_q_norm), feat(mla_kv_norm), router_w.reshape(KT, P, NE).transpose(1, 0, 2).reshape(P, -1),
        rows(router_b), rows(gdn_a_log), rows(gdn_dt_bias), w_ab], axis=1)
    gate = moe_w_gate.reshape(DEPTH * NE, KT, P, DE)
    up = moe_w_up.reshape(DEPTH * NE, KT, P, DE)
    gate_up = np.concatenate([gate, up], axis=3).transpose(0, 2, 1, 3).reshape(DEPTH * NE, P, -1)
    down = moe_w_down.reshape(DEPTH * NE, 2, P, D).transpose(0, 2, 1, 3).reshape(DEPTH * NE, P, -1)
    q_up = mla_w_q_up[0].reshape(4, P, 4, 2, 192).transpose(2, 1, 3, 0, 4).reshape(4, P, -1)
    kv_up = mla_w_kv_up[0].reshape(2, P, 2, 4, 2, P).transpose(2, 1, 0, 4, 3, 5).reshape(2, P, -1)
    return {
        "x": cc(x), "params": cc(params), "consts": const_table(),
        "state": cc(state_gdn[0].transpose(0, 2, 3, 1, 4).reshape(2 * H, P, 2, P)),
        "cache_k": cc(cache_gqa_k[0, 0].transpose(2, 1, 0)), "cache_v": cc(cache_gqa_v[0, 0]),
        "cache_ckv": cc(cache_mla_ckv[0, 0].reshape(PAST, 2, P).transpose(2, 1, 0)),
        "cache_kr": cc(cache_mla_krope[0, 0].T),
        "w_ada": units(w_ada), "gdn_w_in": units(w_in), "gdn_w_out": units(gdn_w_out), "gqa_w_in": units(gqa_w_in),
        "gqa_w_out": units(gqa_w_out), "mla_w_in": units(mla_w_in[:, :, :6 * P]),
        "mla_w_kr": cc(mla_w_in[0, :, 6 * P:].reshape(KT, P, 64).transpose(1, 0, 2).reshape(P, -1)),
        "mla_w_q_up": cc(q_up), "mla_w_kv_up": cc(kv_up), "mla_w_out": units(mla_w_out),
        "moe": cc(np.concatenate([gate_up, down], axis=2)),
    }


def kernel(**inputs):
    from concourse import bacc
    from concourse.bass_utils import run_bass_kernel_spmd

    arrays = layout(**{k: np.asarray(a) for k, a in inputs.items()})
    nc = bacc.Bacc("TRN2", target_bir_lowering=False, num_devices=1)
    given = {n: nc.dram_tensor(f"in_{n}", arrays[n].shape, F32, kind="ExternalInput").ap() for n in INPUTS}
    made = {n: nc.dram_tensor(f"out_{n}", s, F32, kind="ExternalOutput").ap() for n, s in OUTPUTS.items()}
    trunk(nc, given, made)
    r = run_bass_kernel_spmd(nc, [{f"in_{n}": arrays[n] for n in INPUTS}], core_ids=[0]).results[0]
    y = r["out_y"].transpose(1, 0, 2).reshape(D, T).T
    state = r["out_state"].reshape(2, H, P, 2, P).transpose(0, 3, 1, 2, 4)[None]
    cache_k = r["out_cache_k"].transpose(2, 1, 0)[None, None]
    cache_v = r["out_cache_v"].transpose(2, 1, 0)[None, None]
    ckv = r["out_cache_ckv"].transpose(2, 1, 0).reshape(P, 2 * P)[None, None]
    kr = r["out_cache_kr"].T[None, None]
    return y[None, :CTX], y[None, CTX:], state, cache_k, cache_v, ckv, kr
```

```python
from contextlib import ExitStack

import numpy as np

import concourse.bass as bass
from concourse import mybir

F32 = mybir.dt.float32
F32R = mybir.dt.float32r
I32 = mybir.dt.int32
ALU = mybir.AluOpType
ACT = mybir.ActivationFunctionType
AX = mybir.AxisListType

P = 128
D = 1024
KT = D // P
CTX, LAT = 128, 256
T = CTX + LAT
TT = T // P
PAST = 128
NK = T + PAST
DEPTH = 4
KINDS = ["gdn", "gqa", "mla", "gdn"]
H = 8
CHUNK = 64
TAPS = 5
PADW = 2 + CTX + 2 + LAT + 2
CONVW = PADW - (TAPS - 1)
NE, NG, EPG = 16, 4, 4
DE = 256
GRID_W = 64
THETA = 10000.0
ALPHA = (2 * DEPTH) ** 0.25
EPS = 1e-6
BIG = 1e30
RING = 8
UNIT = 2 * KT * P
ADA_UNITS = 6 * D * KT // UNIT
EXPERT = 3 * KT * DE
PARTS = EXPERT // UNIT
HEADS_PER_ITER = RING // 2
BLOCKS = 2 * NG
CTXS, LATS = slice(0, CTX), slice(CTX, T)
QK_SCALE = P ** -0.5
MLA_SCALE = (P + P // 2) ** -0.5

OUT_UNITS = [UNIT] * 4
MIX_UNITS = {
    "gdn": [UNIT] * (2 * H) + OUT_UNITS,
    "gqa": [UNIT] * 6 + OUT_UNITS,
    "mla": [UNIT] * 3 + [KT * 64] + [4 * 2 * 192] * 4 + [UNIT] * 2 + OUT_UNITS,
}

MOE_STEPS = [("G", 0, 0), ("U", 0, 0), ("U", 0, 1), ("T", 0, 0), ("U", 0, 2), ("D", 0, 0), ("T", 0, 1),
             ("U", 0, 3), ("D", 0, 1), ("T", 0, 2), ("G", 1, 0), ("D", 0, 2), ("T", 0, 3), ("U", 1, 0),
             ("D", 0, 3), ("U", 1, 1), ("S", 0, 0), ("T", 1, 0), ("U", 1, 2), ("D", 1, 0), ("T", 1, 1),
             ("U", 1, 3), ("D", 1, 1), ("T", 1, 2), ("D", 1, 2), ("T", 1, 3), ("D", 1, 3), ("S", 1, 0)]
MOE_UNITS = [(j, e, part) for kind, j, e in MOE_STEPS if kind in "UD" for part in ((0, 1) if kind == "U" else (2,))]
PIECE = UNIT // 2
PIECES = EXPERT // PIECE
SPLITS = 3
MOE_FOLLOW, MOE_PIECE_OF = [], {}
_open, _p = [], 0
for _kind, _j, _e in MOE_STEPS:
    if _kind in "UD":
        for _k in range(4 if _kind == "U" else 2):
            MOE_FOLLOW.append(("P", _j, _e, _p))
            MOE_PIECE_OF[_kind, _j, _e, _k] = _p
            _p += 1
            if _k == 1:
                MOE_FOLLOW += _open
                _open = []
    if _kind != "D":
        _open.append((_kind.lower(), _j, _e, None))
    elif _e == EPG - 1:
        _open.append(("y", _j, _e, None))
MOE_FOLLOW += _open


ADA_PAIRS = DEPTH * ADA_UNITS // 2
ADA_PLAN = [(("start", 0), 4), (("head", 0), 2 * H)]
for _l in range(DEPTH - 1):
    if _l:
        ADA_PLAN += [(("before", _l), 1), (("mixer", _l), 1)]
    ADA_PLAN += [(("router", _l), 2), (("route", _l), 4), (("tail", _l), 2)]
ADA_AT = {}
_q = 0
for _key, _n in ADA_PLAN:
    ADA_AT[_key] = _q
    _q += _n
assert _q == ADA_PAIRS


def gdn_order(l):
    order = [("w", 0, 0), ("w", 0, 1)]
    for j in range(HEADS_PER_ITER):
        ada = [[("ada", j, n)] if l == 0 else [] for n in range(4)]
        w = [[("w", j + 1, half)] if j + 1 < HEADS_PER_ITER else [] for half in range(2)]
        order += ada[0] + w[0] + ada[1] + w[1] + ada[2] + ada[3]
    return order


def unit_plan():
    at, u = {}, 0

    def stage(key, n):
        nonlocal u
        at[key] = u
        u += n

    stage(("start", 0), 2 * 4)
    for l, kind in enumerate(KINDS):
        ada = l < DEPTH - 1
        if kind == "gdn":
            stage(("mix", l), len(gdn_order(l)) * (H // HEADS_PER_ITER))
        else:
            first = 6 if kind == "gqa" else 4
            stage(("before", l), 2)
            stage(("mix", l), first)
            stage(("mixer", l), 2)
            stage(("mix2", l), len(MIX_UNITS[kind]) - first - len(OUT_UNITS))
        stage(("out", l), len(OUT_UNITS))
        if ada:
            stage(("router", l), 4)
            stage(("route", l), 8)
        stage(("moe", l), PARTS * NE)
        if ada:
            stage(("tail", l), 4)
    return at, u


CONSTS = {}
CONST_COLS = 0
for _name, _n in [("ident", P), ("ones", P), ("le0", P), ("le1", P), ("lt0", P), ("lt1", P), ("inv0", P), ("inv1", P),
                  ("diag16", P), ("off32", P), ("off64", P), ("before", P), ("rot128", P), ("rot64", P),
                  ("cos128", LAT), ("sin128", LAT), ("cos64", LAT), ("sin64", LAT), ("iota", P),
                  ("block_base", 12), ("block_slot", 12), ("first4", 4), ("first16", 16), ("group_off", 4), ("eps", 1)]:
    CONSTS[_name] = (CONST_COLS, _n)
    CONST_COLS += _n

PARAMS = {}
PARAM_COLS = 0
for _name, _n in [("cond", KT * 2), ("b_ada", DEPTH * 48), ("ln_g", DEPTH * 2 * KT), ("ln_b", DEPTH * 2 * KT),
                  ("conv", 2 * H * 3 * TAPS), ("gdn_g", 2), ("gqa_q", 1), ("gqa_k", 1), ("mla_q", 4), ("mla_kv", 2),
                  ("router_w", KT * NE), ("router_b", NE), ("a_log", 2 * 16), ("dt_bias", 2 * 16),
                  ("w_ab", 2 * KT * 32)]:
    PARAMS[_name] = (PARAM_COLS, _n)
    PARAM_COLS += _n


def const_table():
    c = np.zeros((P, CONST_COLS), np.float32)

    def put(name, a):
        o, n = CONSTS[name]
        c[:a.shape[0], o:o + n] = a

    j, i = np.arange(P)[:, None], np.arange(P)[None, :]
    same = (j // CHUNK) == (i // CHUNK)
    put("ident", np.eye(P))
    put("ones", np.ones((P, P)))
    for d, (le, lt) in enumerate([(j <= i, j < i), (j >= i, j > i)]):
        put(f"le{d}", (same & le) * 1.0)
        put(f"lt{d}", (same & lt) * 1.0)
        put(f"inv{d}", (1.0 - (same & le)) * BIG)
    put("diag16", (j // 16 == i // 16) * 1.0)
    put("off32", ((j // 32 == i // 32) & (j // 16 != i // 16)) * 1.0)
    put("off64", ((j // 64 == i // 64) & (j // 32 != i // 32)) * 1.0)
    put("before", (j < i) * 1.0)
    for n in (P, P // 2):
        rot, q = np.zeros((n, n), np.float32), n // 4
        for o in (0, 2 * q):
            for m in range(q):
                rot[o + q + m, o + m] = -1.0
                rot[o + m, o + q + m] = 1.0
        full = np.zeros((n, P), np.float32)
        full[:, :n] = rot
        put(f"rot{n}", full)
        inv = (np.float32(THETA) ** (-np.arange(q, dtype=np.float32) / np.float32(q))).astype(np.float32)
        t = np.arange(LAT)
        row = (t // GRID_W).astype(np.float32)[None, :] * inv[:, None]
        col = (t % GRID_W).astype(np.float32)[None, :] * inv[:, None]
        ang = np.concatenate([row, row, col, col], axis=0)
        put(f"cos{n}", np.cos(ang))
        put(f"sin{n}", np.sin(ang))
    put("iota", np.broadcast_to(i.astype(np.float32), (P, P)))
    base = np.array([T * g for g in range(NG)] + [T * g + P * b for g in range(NG) for b in (1, 2)], np.float32)[None]
    put("block_base", np.broadcast_to(base, (P, 12)))
    put("block_slot", base + np.arange(P)[:, None])
    put("first4", np.broadcast_to(np.arange(4, 0, -1.0)[None, :], (P, 4)))
    put("first16", np.broadcast_to(np.arange(16, 0, -1.0)[None, :], (P, 16)))
    put("group_off", np.broadcast_to(T * np.arange(NG, dtype=np.float32)[None, :], (P, NG)))
    put("eps", np.full((P, 1), EPS))
    return c

def scan_plan():
    rounds, prev, last, n = [], {}, {}, 0
    for k in range(LAT // CHUNK):
        steps = []
        for ch, (base, size) in enumerate([(CTX, LAT), (CTX, LAT), (0, CTX), (0, CTX)]):
            if k < size // CHUNK:
                d = ch % 2
                c0 = base + CHUNK * (k if d == 0 else size // CHUNK - 1 - k)
                steps.append((n, (ch, d, c0 // P, c0 % P // CHUNK, c0, k == 0)))
                prev[n] = last.get(ch)
                last[ch] = n
                n += 1
        rounds.append(steps)
    return rounds, prev


SCAN_ROUNDS, SCAN_PREV = scan_plan()


class Chain:

    def __init__(self, eng, sem):
        self.eng, self.sem, self.base, self.n = eng, sem, 0, 0

    def step(self, ins):
        ins.then_inc(self.sem, 1)
        self.n += 1

    def wait(self):
        self.eng.wait_ge(self.sem, self.base + self.n)

    def enter(self, i, per_turn):
        self.outer = (self.base, self.n)
        self.per_turn = per_turn
        self.base, self.n = i * per_turn + self.base + self.n, 0

    def leave(self, turns):
        assert self.n == self.per_turn, (self.n, self.per_turn)
        self.base, self.n = self.outer[0], self.outer[1] + turns * self.per_turn


def trunk(nc, I, O):
    unit_at, n_units = unit_plan()
    with ExitStack() as ctx:
        def sb(name, shape, dt=F32):
            return ctx.enter_context(nc.sbuf_tensor(name, shape, dt))

        def sem(name):
            return ctx.enter_context(nc.semaphore(name))

        def sems(names):
            return [sem(n) for n in names.split()]

        ring = sb("ring", [P, RING, UNIT])
        bufx = sb("bufx", [P, KT, T])
        bufh = sb("bufh", [P, KT, T])
        bufo = sb("bufo", [P, KT, T])
        con = sb("con", [P, CONST_COLS])
        par = sb("par", [P, PARAM_COLS])
        silc = sb("silc", [P, KT, 2])
        ada_row = sb("ada_row", [2, 2 * 2 * P])
        mod = sb("mod", [P, DEPTH, 6 * KT, 2])
        lnt = sb("lnt", [P, 2, T])
        flags = sb("flags", [P, NG, 3], I32)
        SCRATCH = 21600
        with nc.sbuf_tensor("scratch", [P, SCRATCH], F32) as scratch:
            pass
        ps = ctx.enter_context(nc.psum_tensor("ps", [P, 8, 512], F32))

        def C(name, rows=P):
            o, n = CONSTS[name]
            return con[0:rows, o:o + n]

        def R(name):
            o, n = PARAMS[name]
            return par[:, o:o + n]

        def spread(ap, n):
            return ap.rearrange("p (o m) -> p o m", o=1).to_broadcast([ap.shape[0], n, ap.shape[1]])

        def wide(ap, n):
            return ap.rearrange("p (m o) -> p m o", o=1).to_broadcast([ap.shape[0], ap.shape[1], n])

        class Carve:

            def __init__(self):
                self.at = 0

            def __call__(self, *dims):
                n = int(np.prod(dims))
                v = scratch[:, self.at:self.at + n]
                self.at += n
                assert self.at <= SCRATCH, self.at
                if len(dims) == 1:
                    return v
                names = "abcd"[:len(dims)]
                return v.rearrange(f"p ({' '.join(names)}) -> p {' '.join(names)}", **dict(zip(names, dims)))

        ones, ident = C("ones"), C("ident")
        cond = R("cond").rearrange("p (k s) -> p k s", s=2)
        b_ada = R("b_ada").rearrange("p (l m) -> p l m", l=DEPTH)
        b_pairs = R("b_ada")
        mod_pairs = mod.rearrange("p l m s -> p (l m s)").rearrange("p (q r) -> p q r", r=8)
        ln_g = R("ln_g").rearrange("p (l k) -> p l k", k=KT)
        ln_b = R("ln_b").rearrange("p (l k) -> p l k", k=KT)
        conv = R("conv").rearrange("p (n m) -> p n m", m=3 * TAPS)
        router_w = R("router_w").rearrange("p (k e) -> p k e", k=KT)
        w_ab = R("w_ab").rearrange("p (l k c) -> p l k c", l=2, k=KT)

        def mrow(l, s, k, seg):
            return mod[:, l, s * KT + k, seg:seg + 1]

        c = Carve()
        g_all = c(6, TT, 16)
        g_tmp = c(6, TT, 16)
        g_head2 = c(2, 6, TT, 2)
        g_taps = c(3, TAPS)
        g_cin = c(3, PADW)
        g_acc = c(3, CONVW)
        g_z = c(2, T)
        g_sq = c(2, T)
        g_rs = c(2, T)
        g_ro = c(T)
        g_qkv2 = c(2, 3, T)
        g_kt = c(TT, P)
        g_vt = c(TT, P)
        g_kd = c(2, TT, P)
        g_w = c(2, TT, P)
        g_eq = c(2, T)
        g_last = c(2, T // CHUNK)
        g_n, g_nd, g_ndt, g_t32, g_t64, g_pa, g_pb, g_x = ([c(TT, P), c(TT, P)] for _ in range(8))
        g_s0 = c(2, 2, P)
        g_zero = c(P)
        g_state = c(4, P)
        g_y = c(4, P)
        g_v = c(4, P)
        g_o = c(T)
        g_osq = c(T)
        c = Carve()
        a_p = c(2, T)
        a_pt = c(2, 3, P)
        a_st = c(2, 4)
        a_tmp = c(2, LAT)
        shared = c.at
        q_qkv = c(12, T)
        q_sq = c(10, T)
        q_kall = c(2, NK)
        q_vall = c(2, NK // P, P)
        c = Carve()
        c(shared)
        m_c = c(6, T)
        m_sq = c(6, T)
        m_kr = c(T)
        m_ckv = c(2, NK)
        m_krall = c(NK)
        m_qn = c(4, T)
        m_qr = c(4, T)
        m_kn = c(4, NK)
        m_v = c(NK // P, 4 * P)
        e_hi, e_lo = sb("e_hi", [P, TT, D], F32R), sb("e_lo", [P, TT, D], F32R)
        e_pick = sb("e_pick", [P, 2, TT, P], F32R)
        e_put = sb("e_put", [P, 2, T], F32R)
        spare = bufh[:, :, :].rearrange("p k t -> p (k t)")
        e_sg, e_hid = (spare[:, o:o + 2 * DE].rearrange("p (b c) -> p b c", b=2) for o in (PIECE, PIECE + 2 * DE))
        e_yhi, e_ylo = sb("e_yhi", [P, D], F32R), sb("e_ylo", [P, D], F32R)
        e_hs = sb("e_hs", [P, 2, 2, KT, P], F32R)
        e_whi, e_wlo = sb("e_whi", [P, SPLITS, PIECE], F32R), sb("e_wlo", [P, SPLITS, PIECE], F32R)
        e_hidT = sb("e_hidT", [P, 2, 2, 2, P], F32R)
        e_cs = sb("e_cs", [P, 2, EPG])
        e_sidrow = lnt[:, 0, :]
        e_rt = sb("e_rt", [P, 10, TT * NE])
        e_sid = sb("e_sid", [P, 3, TT])
        e_cnt = sb("e_cnt", [P, NG])

        params_in, consts_in, x_in = sems("params_in consts_in x_in")
        ring_full = [sem(f"ring_full{i}") for i in range(RING)]
        ring_free = sem("ring_free")
        cond_ready, bias_ready, h_ready, ax_ready = sems("cond_ready bias_ready h_ready ax_ready")
        ada_row_ready, ada_tr, mod_ready = sems("ada_row_ready ada_tr mod_ready")
        (r_ready, mean_mm, mean_ready, centred, squared, var_mm, dev_ready, normed, x_ready) = sems(
            "r_ready mean_mm mean_ready centred squared var_mm dev_ready normed x_ready")
        tile_mm, y_out = sems("tile_mm y_out")
        chain_v, chain_a = sems("chain_v chain_a")
        (ab_mm, sp_in, sp_exp, sp_ln, g_ready, cum_mm, cum_ready) = sems(
            "ab_mm sp_in sp_exp sp_ln g_ready cum_mm cum_ready")
        pad_zero, s0_in, st_out = sems("pad_zero s0_in st_out")
        (raw_in, z_in, conv_done, head_cols, silu_done, qk_sq, nrm_mm, nrm_dev, qk_ready, kv_tr, kv_tok,
         kd_done, gram_mm, row_mm, row_masked, decay_done, strict_done, n_done, w_done, nd_done, x1_done,
         qe_done) = sems(
            "raw_in z_in conv_done head_cols silu_done qk_sq nrm_mm nrm_dev qk_ready kv_tr kv_tok kd_done "
            "gram_mm row_mm row_masked decay_done strict_done n_done w_done nd_done x1_done qe_done")
        inv_mm, inv_cp, inv_x = ([sem(f"{n}{d}") for d in range(2)] for n in ("inv_mm", "inv_cp", "inv_x"))
        (ks_mm, y_done, vn_mm, v_done, os_mm, s_done, o_done, o_sum, o_sq, o_nrm_mm, o_dev, head_done) = sems(
            "ks_mm y_done vn_mm v_done os_mm s_done o_done o_sum o_sq o_nrm_mm o_dev head_done")
        (raw_ev, at_sq, at_nmm, at_dev, at_normed, rot_mm, rot_done, own_ready, vt_mm, vt_ev, cache_in, cache_out,
         up_mm, up_ev) = sems(
            "raw_ev at_sq at_nmm at_dev at_normed rot_mm rot_done own_ready vt_mm vt_ev cache_in cache_out "
            "up_mm up_ev")
        (sc_mm, max_done, exp_done, p_done, pt_mm, pt_ev, pv_mm, oh_ev) = sems(
            "sc_mm max_done exp_done p_done pt_mm pt_ev pv_mm oh_ev")
        (o_zero, rt_mm, score_ready, oh_ready, rk_mm, sid_ready, row2_mm, row2_ready, tk_mm, tk_hi, tk_lo,
         flags_ready) = sems(
            "o_zero rt_mm score_ready oh_ready rk_mm sid_ready row2_mm row2_ready tk_mm tk_hi tk_lo flags_ready")

        def moe_sems(pre):
            names = "pick ga ga_ev cs whi wlo wfree up sg hid tr thi tlo dn yhi ylo sc sc_ev".split()
            return dict(zip(names, sems(" ".join(pre + n for n in names))))

        F = moe_sems("f_")
        X = moe_sems("x_")
        x_w = sem("x_w")

        tiles_at, n_tiles = {}, 0
        for l, kind in enumerate(KINDS):
            tiles_at["in", l] = n_tiles
            n_tiles += {"gdn": 2 * H, "gqa": 6, "mla": 3}[kind]
            tiles_at["out", l] = n_tiles
            n_tiles += 4
        att_at = {1: 0, 2: H * TT}
        li_of = {0: 0, 3: 1}

        def unit(u):
            return ring[:, u % RING, :]

        def landed(eng, u, turn=0):
            eng.wait_ge(ring_full[u % RING], turn * 16 + 16 * (u // RING + 1))

        def used(eng, u, shift=0):
            eng.wait_ge(ring_free, shift + (u + 1))

        def tile_done(eng, stage, l, n):
            if n % 2 == 0:
                eng.wait_ge(tile_mm, tiles_at[stage, l] + n // 2 + 1)
            else:
                used(eng, unit_at["mix" if stage == "in" else "out", l] + n // 2)

        def head_unit(l, what, j, n):
            return unit_at["mix", l] + gdn_order(l).index((what, j, n))

        def scan_state(ch, d, first, j):
            if not first:
                return g_state[:, ch, :]
            return g_s0[:, j % 2, d, :] if ch < 2 else g_zero

        block = ctx.enter_context(nc.Block())

        @block.sync
        def _(sp):
            sp.dma_start(par[:, :], I["params"]).then_inc(params_in, 16)

            def load(src, u, cols=UNIT):
                if u >= RING:
                    used(sp, u - RING)
                sp.dma_start(unit(u)[:, 0:cols], src).then_inc(ring_full[u % RING], 16)

            def ada_stage(stage, l):
                for k in range(2 * dict(ADA_PLAN)[stage, l]):
                    load(I["w_ada"][2 * ADA_AT[stage, l] + k], unit_at[stage, l] + k)

            ada_stage("start", 0)
            for l, kind in enumerate(KINDS):
                u0, u2, uo = unit_at["mix", l], unit_at.get(("mix2", l)), unit_at["out", l]
                if kind == "gdn":
                    order = gdn_order(l)
                    with sp.Fori(0, H // HEADS_PER_ITER) as i:
                        for n, (what, j, k) in enumerate(order):
                            if what == "w":
                                src = I["gdn_w_in"][i * (2 * HEADS_PER_ITER) + (li_of[l] * 2 * H + 2 * j + k)]
                            else:
                                src = I["w_ada"][i * (4 * HEADS_PER_ITER) + (2 * ADA_AT["head", l] + 4 * j + k)]
                            used(sp, u0 + n - RING, i * len(order))
                            sp.dma_start(unit(u0 + n), src).then_inc(ring_full[(u0 + n) % RING], 16)
                    for k in range(4):
                        load(I["gdn_w_out"][4 * li_of[l] + k], uo + k)
                elif kind == "gqa":
                    ada_stage("before", l)
                    for k in range(6):
                        load(I["gqa_w_in"][k], u0 + k)
                    ada_stage("mixer", l)
                    for k in range(4):
                        load(I["gqa_w_out"][k], uo + k)
                else:
                    ada_stage("before", l)
                    for k in range(3):
                        load(I["mla_w_in"][k], u0 + k)
                    load(I["mla_w_kr"], u0 + 3, KT * 64)
                    ada_stage("mixer", l)
                    for half in range(2):
                        for k in range(2):
                            load(I["mla_w_q_up"][2 * half + k], u2 + 3 * half + k, 4 * 2 * 192)
                        load(I["mla_w_kv_up"][half], u2 + 2 + 3 * half)
                    for k in range(4):
                        load(I["mla_w_out"][k], uo + k)
                if l < DEPTH - 1:
                    ada_stage("router", l)
                    ada_stage("route", l)
                u0, per = unit_at["moe", l], len(MOE_UNITS)

                def expert_part(turn, n):
                    j, e, part = MOE_UNITS[n]
                    return I["moe"][turn * (2 * EPG) + (l * NE + j * EPG + e), :, part * UNIT:(part + 1) * UNIT]

                with sp.Fori(0, NG // 2) as i:
                    for n in range(per):
                        used(sp, u0 + n - RING, i * per)
                        sp.dma_start(unit(u0 + n), expert_part(i, n)).then_inc(ring_full[(u0 + n) % RING], 16)
                if l < DEPTH - 1:
                    ada_stage("tail", l)
            sp.wait_ge(x_ready, KT * 2 * DEPTH)
            sp.dma_start(O["y"], bufx[:, :, :]).then_inc(y_out, 16)
            sp.wait_ge(y_out, 16)
            sp.wait_ge(st_out, 16 * 2 * H)
            sp.wait_ge(cache_out, 16 * 4)

        @block.tensor
        def _(pe):
            mm = nc.tensor.matmul

            def ada_unit(q, u, x, part=None, turn=0):
                if part != 1:
                    landed(pe, u, turn)
                    if x == 0 and not (isinstance(q, int) and q == 0):
                        pe.wait_ge(mod_ready, q)
                w = unit(u).rearrange("p (k c) -> p k c", k=KT)
                for kt in range(KT) if part is None else range(4 * part, 4 * part + 4):
                    last = mm(ps[0:2, 7, 2 * P * x:2 * P * x + 2 * P], silc[:, kt, :], w[:, kt, :],
                              start=(kt == 0), stop=(kt == KT - 1))
                if part != 0:
                    last.then_inc(ring_free, 1)

            def ada_turn(q):
                pe.wait_ge(ada_row_ready, q + 1)
                for m in range(4):
                    last = mm(ps[:, 7, 2 * m:2 * m + 2], ada_row[:, P * m:P * m + P], ident[0:2, 0:2],
                              start=True, stop=True)
                last.then_inc(ada_tr, 1)

            def ada_pair(stage, l, n):
                for x in range(2):
                    ada_unit(ADA_AT[stage, l] + n, unit_at[stage, l] + 2 * n + x, x)

            def project(l, stage, first, n, rhs, banks, wait_bank, tiles=None):
                u0 = unit_at["mix" if stage == "in" else "out", l]
                for t in range(first, first + n):
                    if t % 2 == 0:
                        landed(pe, u0 + t // 2)
                    w = unit(u0 + t // 2).rearrange("p (m k c) -> p m k c", m=2, k=KT)
                    wait_bank(t)
                    for kt in range(KT):
                        if stage == "in" and t == 0:
                            pe.wait_ge(h_ready, KT * 2 * l + kt + 1)
                        last = mm(ps[:, banks[t % len(banks)], 0:T], w[:, t % 2, kt, :], rhs[:, kt, :],
                                  start=(kt == 0), stop=(kt == KT - 1))
                    last.then_inc(tile_mm if t % 2 == 0 else ring_free, 1)

            def project_out(l, ready, n_ready):
                pe.wait_ge(ready, n_ready)
                project(l, "out", 0, KT, bufo, (0, 1),
                        lambda t: pe.wait_ge(r_ready, KT * 2 * l + t - 1) if t >= 2 else None)

            def layer_norm(n, rbuf, sqbuf, between=lambda: None):
                for k in range(KT):
                    pe.wait_ge(r_ready, KT * n + k + 1)
                    last = mm(ps[:, 5, 0:T], ones, rbuf[:, k, :], start=(k == 0), stop=(k == KT - 1))
                last.then_inc(mean_mm, 1)
                between()
                for k in range(KT):
                    if k % 2 == 0:
                        pe.wait_ge(squared, 4 * n + k // 2 + 1)
                    last = mm(ps[:, 6, 0:T], ones, sqbuf[:, k, :], start=(k == 0), stop=(k == KT - 1))
                last.then_inc(var_mm, 1)

            def head_proj(l, j, m, i, part=None):
                u = head_unit(l, "w", j, m // 2)
                hh = i * HEADS_PER_ITER + (li_of[l] * H + j)
                if part != 1:
                    landed(pe, u, i * (len(gdn_order(l)) // RING))
                    if m:
                        pe.wait_ge(raw_in, hh * 3 + m)
                    elif j:
                        pe.wait_ge(z_in, hh)
                w = unit(u).rearrange("p (m k c) -> p m k c", m=2, k=KT)
                for kt in range(KT) if part is None else range(4 * part, 4 * part + 4):
                    last = mm(ps[:, 6, 0:T], w[:, m % 2, kt, :], bufh[:, kt, :], start=(kt == 0), stop=(kt == KT - 1))
                if part != 0:
                    last.then_inc(tile_mm if m % 2 == 0 else ring_free, 1)

            def head_ada(l, j, n, i, part=None):
                if l == 0:
                    q = i * (2 * HEADS_PER_ITER) + (ADA_AT["head", l] + 2 * j + n // 2)
                    ada_unit(q, head_unit(l, "ada", j, n), n % 2, part, i * (len(gdn_order(l)) // RING))

            def head_ada_turn(l, j, n, i):
                if l == 0:
                    ada_turn(i * (2 * HEADS_PER_ITER) + (ADA_AT["head", l] + 2 * j + n))

            def gdn(l):
                li = li_of[l]
                for kt in range(KT):
                    pe.wait_ge(h_ready, KT * 2 * l + kt + 1)
                for t in range(TT):
                    for kt in range(KT):
                        last = mm(ps[:, 2, 32 * t:32 * t + 32], bufh[:, kt, P * t:P * t + P], w_ab[:, li, kt, :],
                                  start=(kt == 0), stop=(kt == KT - 1))
                last.then_inc(ab_mm, 1)
                pe.wait_ge(g_ready, li + 1)
                for what, mats in enumerate((("le0", "le1"), ("lt1", "lt0"))):
                    for t in range(TT):
                        for d in range(2):
                            o = 48 * what + 16 * t + 8 * d
                            last = mm(ps[:, 3, o:o + 8], C(mats[d]), g_all[:, 0, t, 8 * d:8 * d + 8],
                                      start=True, stop=True)
                last.then_inc(cum_mm, 1)
                pe.wait_ge(cum_ready, 2 * (li + 1))
                with pe.Fori(0, H // HEADS_PER_ITER) as i:
                    for j in range(HEADS_PER_ITER):
                        gdn_head(l, i, j)
                project_out(l, head_done, H * (li + 1))

            def qk_norms(hh):
                pe.wait_ge(qk_sq, hh + 1)
                for m in range(2):
                    last = mm(ps[:, 2 + m, 0:T], ones, g_sq[:, m, :], start=True, stop=True)
                last.then_inc(nrm_mm, 1)

            def decay_rows(hh, j):
                pe.wait_ge(head_cols, hh + 1)
                if j:
                    pe.wait_ge(o_sum, hh)
                for d in range(2):
                    for t in range(TT):
                        last = mm(ps[:, 4 + d, P * t:P * t + P],
                                  g_head2[:, j % 2, 0, t, d:d + 1].to_broadcast([P, P]), C(f"le{d}"),
                                  start=True, stop=True)
                    last.then_inc(row_mm, 1)

            def gdn_head(l, i, j):
                hh = i * HEADS_PER_ITER + (li_of[l] * H + j)
                more = j + 1 < HEADS_PER_ITER
                qkv = g_qkv2[:, j % 2, :, :]
                if j == 0:
                    for m in range(4):
                        head_proj(l, j, m, i)
                    qk_norms(hh)
                    decay_rows(hh, j)
                pe.wait_ge(silu_done, hh * 3 + 3)
                if j:
                    pe.wait_ge(o_dev, hh)
                for t in range(TT):
                    last = nc.tensor.transpose(ps[:, 0, P * t:P * t + P], qkv[:, 2, P * t:P * t + P], ident)
                last.then_inc(kv_tr, 1)
                if more:
                    head_proj(l, j + 1, 0, i)
                pe.wait_ge(qk_ready, hh * 2 + 1)
                for t in range(TT):
                    last = nc.tensor.transpose(ps[:, 1, P * t:P * t + P], qkv[:, 1, P * t:P * t + P], ident)
                last.then_inc(kv_tr, 1)
                pe.wait_ge(qk_ready, hh * 2 + 2)
                for m, rhs in ((0, 1), (1, 0)):
                    for t in range(TT):
                        cols = slice(P * t, P * t + P)
                        last = mm(ps[:, 2 + m, cols], qkv[:, 1, cols], qkv[:, rhs, cols], start=True, stop=True)
                    last.then_inc(gram_mm, 1)
                head_ada(l, j, 0, i)
                inverse(l, i, j, hh)
                scan(l, i, j, hh)

            def inverse(l, i, j, hh):
                jobs = [
                    ("T", g_n, None, 0, 0, 0), ("M", g_ndt, g_nd, 1, 0, 1), ("M", g_nd, g_ndt, 0, 0, 1),
                    ("M", g_pb, g_x, 1, 2, 1), ("M", g_pb, g_pa, 0, 2, 1), ("M", g_pa, g_pb, 1, 2, 2),
                    ("M", g_ndt, g_x, 0, 4, 2), ("M", g_nd, g_ndt, 1, 4, 2), ("M", g_pa, g_x, 0, 5, 3),
                    ("T", g_x, None, 1, 5, 4), ("M", g_t32, g_x, 0, 5, 4), ("M", g_pb, g_nd, 1, 7, 4),
                    ("T", g_x, None, 0, 7, 5), ("M", g_t64, g_x, 1, 7, 5), ("M", g_pb, g_nd, 0, 9, 5)]
                for n, (kind, a, b, bank, copies, sums) in enumerate(jobs):
                    for d in range(2):
                        if n == 0:
                            pe.wait_ge(n_done, hh * 2 + d + 1)
                            pe.wait_ge(decay_done, hh * 2 + d + 1)
                        if n == 1:
                            pe.wait_ge(n_done, hh * 2 + 2)
                            pe.wait_ge(w_done, hh * 2 + 2)
                            pe.wait_ge(nd_done, hh * 2 + d + 1)
                        if n == 3:
                            pe.wait_ge(x1_done, hh * 2 + d + 1)
                        if copies:
                            pe.wait_ge(inv_cp[d], hh * 9 + copies)
                        if sums:
                            pe.wait_ge(inv_x[d], hh * 6 + sums)
                        for t in range(TT):
                            out = ps[:, 4 + d - 2 * bank, P * t:P * t + P]
                            if kind == "T":
                                last = nc.tensor.transpose(out, a[d][:, t, :], ident)
                            else:
                                last = mm(out, a[d][:, t, :], b[d][:, t, :], start=True, stop=True)
                        last.then_inc(inv_mm[d], 1)
                    if n == 0 and j + 1 < HEADS_PER_ITER:
                        head_proj(l, j + 1, 1, i)
                    if n == 2:
                        head_ada(l, j, 1, i)

            def scan(l, i, j, hh):
                pe.wait_ge(kd_done, hh + 1)
                pe.wait_ge(qe_done, hh * 2 + 2)
                pe.wait_ge(w_done, hh * 2 + 2)
                for d in range(2):
                    pe.wait_ge(inv_x[d], hh * 6 + 6)
                pe.wait_ge(s0_in, hh * 16 + 16)
                more = j + 1 < HEADS_PER_ITER
                qkv = g_qkv2[:, j % 2, :, :]

                def meanwhile(k, part):
                    if k < 2 and more:
                        head_proj(l, j + 1, 2 + k, i, part)
                    if k >= 2:
                        head_ada(l, j, k, i, part)

                for k, steps in enumerate(SCAN_ROUNDS):
                    for n, (ch, d, t, half, c0, first) in steps:
                        if k == 0:
                            if n == 0:
                                pe.wait_ge(kv_tok, hh * 2 + 2)
                        else:
                            pe.wait_ge(s_done, hh * 12 + SCAN_PREV[n] + 1)
                        rows = slice(64 * half, 64 * half + 64)
                        mm(ps[rows, ch, 0:P], qkv[:, 1, c0:c0 + CHUNK], scan_state(ch, d, first, j),
                           start=True, stop=True).then_inc(ks_mm, 1)
                    if k == 0:
                        head_ada_turn(l, j, 0, i)
                    meanwhile(k, 0)
                    for n, (ch, d, t, half, c0, first) in steps:
                        rows = slice(64 * half, 64 * half + 64)
                        pe.wait_ge(y_done, hh * 12 + n + 1)
                        mm(ps[rows, ch, P:2 * P], g_x[d][:, t, rows], g_y[:, ch, :],
                           start=True, stop=True).then_inc(vn_mm, 1)
                    meanwhile(k, 1)
                    for n, (ch, d, t, half, c0, first) in steps:
                        rows = slice(64 * half, 64 * half + 64)
                        pe.wait_ge(v_done, hh * 12 + n + 1)
                        out = ps[:, 4 + d, c0:c0 + CHUNK]
                        mm(out, scan_state(ch, d, first, j), g_eq[:, d, c0:c0 + CHUNK], start=True, stop=False)
                        mm(out, g_v[rows, ch, :], g_w[rows, d, t, rows], start=False, stop=True)
                        mm(ps[:, ch, 3 * P:4 * P], g_kd[rows, d, t, :], g_v[rows, ch, :],
                           start=True, stop=True).then_inc(os_mm, 1)
                head_ada_turn(l, j, 1, i)
                if more:
                    pe.wait_ge(s_done, hh * 12 + 12)
                    qk_norms(hh + 1)
                    decay_rows(hh + 1, j + 1)
                pe.wait_ge(o_sq, hh + 1)
                mm(ps[:, 0, 0:T], ones, g_osq[:, :], start=True, stop=True).then_inc(o_nrm_mm, 1)

            def attention(l, heads, first_head, scores, values):
                a0 = att_at[l] + TT * first_head
                units = [(h, qt) for h in heads for qt in range(TT)]

                def score(n):
                    h, qt = units[n]
                    nk = P if qt == 0 else T
                    k0 = 0 if qt == 0 else P
                    if a0 + n >= 2:
                        pe.wait_ge(exp_done, a0 + n - 1)
                    scores(ps[:, n % 2, 0:nk], h, slice(P * qt, P * qt + P), slice(k0, k0 + nk)).then_inc(sc_mm, 1)

                score(0)
                for n, (h, qt) in enumerate(units):
                    if n + 1 < len(units):
                        score(n + 1)
                    tiles = [0] if qt == 0 else [1, 2, 3]
                    pe.wait_ge(p_done, a0 + n + 1)
                    if a0 + n >= 2:
                        pe.wait_ge(pt_ev, a0 + n - 1)
                    for m in range(len(tiles)):
                        last = nc.tensor.transpose(ps[:, 2 + n % 2, P * m:P * m + P], a_p[:, n % 2, P * m:P * m + P],
                                                   ident)
                    last.then_inc(pt_mm, 1)
                    pe.wait_ge(pt_ev, a0 + n + 1)
                    hn = a0 // TT + n // TT
                    if qt == 0 and hn >= 2:
                        pe.wait_ge(oh_ev, hn - 1)
                    for m, kt in enumerate(tiles):
                        last = mm(ps[:, 4 + (n // TT) % 2, P * qt:P * qt + P], values(h, kt), a_pt[:, n % 2, m, :],
                                  start=(m == 0), stop=(m == len(tiles) - 1))
                    last.then_inc(pv_mm, 1)

            def gqa(l):
                ada_pair("before", l, 0)
                ada_turn(ADA_AT["before", l])
                project(l, "in", 0, 12, bufh, (0, 1), lambda t: pe.wait_ge(raw_ev, t - 1) if t >= 2 else None)
                for n in range(10):
                    pe.wait_ge(at_sq, n + 1)
                    if n >= 2:
                        pe.wait_ge(at_dev, n - 1)
                    mm(ps[:, 2 + n % 2, 0:T], ones, q_sq[:, n, :], start=True, stop=True).then_inc(at_nmm, 1)
                pe.wait_ge(raw_ev, 12)
                for kv in range(2):
                    for t in range(TT):
                        last = nc.tensor.transpose(ps[:, kv, P * t:P * t + P], q_qkv[:, 10 + kv, P * t:P * t + P], ident)
                    last.then_inc(vt_mm, 1)
                ada_pair("mixer", l, 0)
                ada_turn(ADA_AT["mixer", l])
                for n in range(5):
                    pe.wait_ge(at_normed, 2 * n + 2)
                    if n >= 2:
                        pe.wait_ge(rot_done, n - 1)
                    for m in range(2):
                        last = mm(ps[:, 4 + n % 2, LAT * m:LAT * m + LAT], C("rot128"), q_qkv[:, 2 * n + m, LATS],
                                  start=True, stop=True)
                    last.then_inc(rot_mm, 1)
                pe.wait_ge(rot_done, 5)
                pe.wait_ge(own_ready, 2)
                pe.wait_ge(vt_ev, 2)
                pe.wait_ge(cache_in, 16 * 2)

                def scores(out, h, q, keys):
                    return mm(out, q_qkv[:, h, q], q_kall[:, h // 4, keys], start=True, stop=True)

                attention(l, range(H), 0, scores, lambda h, kt: q_vall[:, h // 4, kt, :])
                project_out(l, oh_ev, H)

            def mla(l):
                ada_pair("before", l, 0)
                ada_turn(ADA_AT["before", l])
                project(l, "in", 0, 6, bufh, (0, 1), lambda t: pe.wait_ge(raw_ev, 12 + t - 1) if t >= 2 else None)
                u = unit_at["mix", l] + 3
                landed(pe, u)
                w = unit(u)[:, 0:KT * 64].rearrange("p (k c) -> p k c", k=KT)
                pe.wait_ge(raw_ev, 12 + 5)
                for kt in range(KT):
                    last = mm(ps[0:64, 0, 0:T], w[:, kt, :], bufh[:, kt, :], start=(kt == 0), stop=(kt == KT - 1))
                last.then_inc(ring_free, 1)
                ada_pair("mixer", l, 0)
                for m, tiles in enumerate((range(4), range(4, 6))):
                    for n in tiles:
                        pe.wait_ge(at_sq, 10 + n + 1)
                        last = mm(ps[:, 2 + m, 0:T], ones, m_sq[:, n, :], start=(n == tiles[0]), stop=(n == tiles[-1]))
                    last.then_inc(at_nmm, 1)
                ada_turn(ADA_AT["mixer", l])
                pe.wait_ge(raw_ev, 12 + 7)
                mm(ps[0:64, 4, 0:LAT], C("rot64", 64)[:, 0:64], m_kr[0:64, LATS],
                   start=True, stop=True).then_inc(rot_mm, 1)
                pe.wait_ge(at_normed, 10 + 6)
                pe.wait_ge(cache_in, 16 * 4)
                pe.wait_ge(own_ready, 2 + 4)
                pe.wait_ge(rot_done, 6)
                for half in range(2):
                    mla_half(l, half)
                project_out(l, oh_ev, 2 * H)

            def mla_half(l, half):
                n_up = 16 * half
                job = [n_up]

                def free_bank():
                    if job[0] - n_up >= 2:
                        pe.wait_ge(up_ev, job[0] - 1)
                    elif half:
                        pe.wait_ge(up_ev, n_up)
                    job[0] += 1
                    return job[0] % 2

                if half:
                    pe.wait_ge(oh_ev, H + 4)
                for k in range(2):
                    u = unit_at["mix2", l] + 3 * half + k
                    landed(pe, u)
                    w = unit(u)[:, 0:4 * 2 * 192].rearrange("p (h k c) -> p h k c", h=2, k=4)
                    for hd in range(2):
                        for cols in (slice(0, P), slice(P, 192)):
                            rows = cols.stop - cols.start
                            b = free_bank()
                            for kt in range(4):
                                last = mm(ps[0:rows, b, 0:T], w[:, hd, kt, cols], m_c[:, kt, :],
                                          start=(kt == 0), stop=(kt == 3))
                            if hd == 1 and rows == 64:
                                last.then_inc(ring_free, 1)
                            else:
                                last.then_inc(up_mm, 1)
                u = unit_at["mix2", l] + 2 + 3 * half
                landed(pe, u)
                w = unit(u).rearrange("p (k c) -> p k c", k=2)
                for hd in range(4):
                    b = free_bank()
                    for kt in range(2):
                        last = mm(ps[:, b, 0:NK], w[:, kt, P * hd:P * hd + P], m_ckv[:, kt, :],
                                  start=(kt == 0), stop=(kt == 1))
                    last.then_inc(up_mm, 1)
                for tile in range(NK // P):
                    b = free_bank()
                    for kt in range(2):
                        last = mm(ps[:, b, 0:512], m_ckv[:, kt, P * tile:P * tile + P], w[:, kt, 512:1024],
                                  start=(kt == 0), stop=(kt == 1))
                    last.then_inc(up_mm if tile < 3 else ring_free, 1)
                pe.wait_ge(up_ev, 16 * half + 16)
                for m in range(2):
                    for hd in range(2):
                        last = mm(ps[0:64, 4 + m, LAT * hd:LAT * hd + LAT], C("rot64", 64)[:, 0:64],
                                  m_qr[0:64, 2 * m + hd, LATS], start=True, stop=True)
                    last.then_inc(rot_mm, 1)
                pe.wait_ge(rot_done, 6 + 2 * half + 2)

                def scores(out, h, q, keys):
                    mm(out, m_qn[:, h % 4, q], m_kn[:, h % 4, keys], start=True, stop=False)
                    return mm(out, m_qr[0:64, h % 4, q], m_krall[0:64, keys], start=False, stop=True)

                attention(l, range(4 * half, 4 * half + 4), 4 * half, scores,
                          lambda h, kt: m_v[:, kt, P * (h % 4):P * (h % 4) + P])

            def gather(S, n, j, comb_cols):
                pe.wait_ge(S["pick"], n + 1)
                for half, part in enumerate((e_hi, e_lo)):
                    for q in range(2):
                        if half:
                            pe.wait_ge(S["ga_ev"], n * 4 + q + 1)
                        for ft in range(4 * q, 4 * q + 4):
                            for t in range(TT):
                                last = mm(ps[:, 5 + q, P * (ft % 4):P * (ft % 4) + P],
                                          part[:, t, P * ft:P * ft + P], e_pick[:, j, t, :],
                                          start=(t == 0), stop=(t == TT - 1))
                        last.then_inc(S["ga"], 1)
                for t in range(TT):
                    last = mm(ps[:, 7, 96 + 4 * j:100 + 4 * j], e_pick[:, j, t, :].bitcast(F32), comb_cols(t),
                              start=(t == 0), stop=(t == TT - 1))
                last.then_inc(S["ga"], 1)

            def transpose_hidden(S, n, b):
                pe.wait_ge(S["hid"], n + 1)
                for m in range(2):
                    last = nc.tensor.transpose(ps[:, 2, 256 * b + P * m:256 * b + P * m + P],
                                               e_hid[:, b, P * m:P * m + P], ident)
                last.then_inc(S["tr"], 1)

            def split_products(out, parts, whi, wlo, start, stop, frees=False):
                first = mm(out, parts[0], whi, start=start, stop=False)
                if frees:
                    first.then_inc(ring_free, 1)
                mm(out, parts[0], wlo, start=False, stop=False)
                return mm(out, parts[1], whi, start=False, stop=stop)

            def down(S, n, p, e, k):
                b = p % SPLITS
                pe.wait_ge(S["whi"], n + 1)
                pe.wait_ge(S["wlo"], n + 1)
                for y in range(2):
                    cols = slice(512 * y, 512 * y + 512)
                    last = split_products(ps[:, 3 + y, :], [e_hidT[:, e % 2, part, k, :] for part in range(2)],
                                          e_whi[:, b, cols], e_wlo[:, b, cols],
                                          e == 0 and k == 0, e == EPG - 1 and k == 1, S is F and p % 2 == 1 and y == 0)
                last.then_inc(S["wfree"], 1)

            def scatter(S, n, j):
                pe.wait_ge(S["yhi"], n + 1)
                pe.wait_ge(S["ylo"], n + 1)
                for ft in range(KT):
                    if ft >= 2:
                        pe.wait_ge(S["sc_ev"], n * KT + (ft - 1))
                    b = 5 + ft % 2
                    mm(ps[:, b, 0:T], e_yhi[:, P * ft:P * ft + P], e_put[:, j, :], start=True, stop=False)
                    mm(ps[:, b, 0:T], e_ylo[:, P * ft:P * ft + P], e_put[:, j, :],
                       start=False, stop=True).then_inc(S["sc"], 1)

            def gate_up(S, n, p, j, e, k):
                b = p % SPLITS
                pe.wait_ge(S["whi"], n + 1)
                pe.wait_ge(S["wlo"], n + 1)
                for m in range(2):
                    kt, cols = 2 * k + m, slice(512 * m, 512 * m + 512)
                    last = split_products(ps[:, e % 2, :], [e_hs[:, j, part, kt, :] for part in range(2)],
                                          e_whi[:, b, cols], e_wlo[:, b, cols], kt == 0, kt == KT - 1,
                                          S is F and p % 2 == 1 and m == 0)
                last.then_inc(S["wfree"], 1)

            def moe(l):
                ada = l < DEPTH - 1
                if ada:
                    for n in range(2):
                        ada_pair("router", l, n)
                        ada_turn(ADA_AT["router", l] + n)
                for kt in range(KT):
                    pe.wait_ge(h_ready, KT * (2 * l + 1) + kt + 1)
                for t in range(TT):
                    for kt in range(KT):
                        last = mm(ps[:, 2, NE * t:NE * t + NE], bufh[:, kt, P * t:P * t + P], router_w[:, kt, :],
                                  start=(kt == 0), stop=(kt == KT - 1))
                last.then_inc(rt_mm, 1)
                pe.wait_ge(o_zero, l + 1)

                def token_tile(n):
                    if n >= 2:
                        pe.wait_ge(tk_hi, 2 * TT * l + n - 1)
                        pe.wait_ge(tk_lo, 2 * TT * l + n - 1)
                    for m in range(4):
                        last = nc.tensor.transpose(ps[:, 5 + n % 2, P * m:P * m + P],
                                                   bufh[:, 4 * (n % 2) + m, P * (n // 2):P * (n // 2) + P], ident)
                    last.then_inc(tk_mm, 1)

                token_tile(0)
                token_tile(1)
                if ada:
                    ada_pair("route", l, 0)
                oh = e_rt[:, 8, 0:TT * NG].rearrange("p (t g) -> p t g", t=TT)
                pe.wait_ge(oh_ready, l + 1)
                for t in range(TT):
                    for t2 in range(t + 1):
                        mm(ps[:, 2, 64 + 4 * t:68 + 4 * t], C("before") if t2 == t else ones, oh[:, t2, :],
                           start=(t2 == 0), stop=(t2 == t))
                for t in range(TT):
                    last = mm(ps[:, 2, 80:84], ones, oh[:, t, :], start=(t == 0), stop=(t == TT - 1))
                last.then_inc(rk_mm, 1)
                if ada:
                    ada_turn(ADA_AT["route", l])
                pe.wait_ge(sid_ready, l + 1)
                for t in range(TT):
                    last = mm(ps[:, 2, P + P * t:2 * P + P * t], e_sid[:, 0, t:t + 1].to_broadcast([P, P]), ident,
                              start=True, stop=True)
                last.then_inc(row2_mm, 1)
                if ada:
                    ada_pair("route", l, 1)
                token_tile(2)
                token_tile(3)
                if ada:
                    ada_turn(ADA_AT["route", l] + 1)
                    ada_pair("route", l, 2)
                token_tile(4)
                token_tile(5)
                if ada:
                    ada_turn(ADA_AT["route", l] + 2)
                    ada_pair("route", l, 3)
                    ada_turn(ADA_AT["route", l] + 3)
                    pe.wait_ge(mod_ready, ADA_AT["route", l] + 4)
                pe.wait_ge(row2_ready, l + 1)
                pe.wait_ge(tk_hi, 2 * TT * (l + 1))
                pe.wait_ge(tk_lo, 2 * TT * (l + 1))

                u0, per = unit_at["moe", l], len(MOE_UNITS)
                comb = e_rt[:, 9, :].rearrange("p (t e) -> p t e", t=TT)
                with pe.Fori(0, NG // 2) as i:
                    for kind, j, e in MOE_STEPS:
                        gg = i * 2 + (NG * l + j)
                        n = i * (2 * EPG) + (NE * l + EPG * j + e)
                        if kind == "G":
                            gather(F, gg, j, lambda t: comb[:, t, bass.ds(i * (2 * EPG) + EPG * j, EPG)])
                        elif kind == "U":
                            if e == 0:
                                pe.wait_ge(F["ga_ev"], gg * 4 + 4)
                            for k in range(4):
                                p = MOE_PIECE_OF["U", j, e, k]
                                gate_up(F, i * (2 * per) + (2 * per * (NG // 2) * l + p), p, j, e, k)
                        elif kind == "T":
                            transpose_hidden(F, n, e % 2)
                        elif kind == "D":
                            pe.wait_ge(F["thi"], n + 1)
                            pe.wait_ge(F["tlo"], n + 1)
                            for k in range(2):
                                p = MOE_PIECE_OF["D", j, e, k]
                                down(F, i * (2 * per) + (2 * per * (NG // 2) * l + p), p, e, k)
                        else:
                            scatter(F, gg, j)
                pe.wait_ge(F["sc_ev"], KT * NG * (l + 1))
                pe.wait_ge(flags_ready, l + 1)
                crowded = pe.value_load(flags[0:1, 0, 2:3], min_val=0, max_val=1)
                with pe.If(crowded > 0):
                    with pe.Fori(0, NG) as g:
                        for b in range(2):
                            n = g * 2 + (2 * NG * l + b)
                            more = pe.value_load(flags[0:1, g, b:b + 1], min_val=0, max_val=1)
                            with pe.If(more > 0):
                                gather(X, n, 0, lambda t: comb[:, t, bass.ds(g * EPG, EPG)])
                                pe.wait_ge(X["ga_ev"], n * 4 + 4)
                                for e in range(EPG):
                                    for k in range(PIECES):
                                        p = PIECES * e + k
                                        if k < 4:
                                            gate_up(X, n * (EPG * PIECES) + p, p, 0, e, k)
                                        else:
                                            if k == 4:
                                                transpose_hidden(X, n * EPG + e, e % 2)
                                                pe.wait_ge(X["thi"], n * EPG + (e + 1))
                                                pe.wait_ge(X["tlo"], n * EPG + (e + 1))
                                            down(X, n * (EPG * PIECES) + p, p, e, k - 4)
                                scatter(X, n, 0)
                                pe.wait_ge(X["sc_ev"], n * KT + KT)
                                pe.nop()
                            with pe.Else():
                                pe.sem_inc(X["ga"], 5)
                                pe.sem_inc(X["tr"], EPG)
                                pe.sem_inc(X["wfree"], EPG * PIECES)
                                pe.sem_inc(X["sc"], KT)
                with pe.Else():
                    pe.sem_inc(X["ga"], BLOCKS * 5)
                    pe.sem_inc(X["tr"], BLOCKS * EPG)
                    pe.sem_inc(X["wfree"], BLOCKS * EPG * PIECES)
                    pe.sem_inc(X["sc"], BLOCKS * KT)

            for S in (F, X):
                pe.sem_inc(S["wfree"], SPLITS)
            pe.wait_ge(consts_in, 16)
            pe.wait_ge(params_in, 16)
            pe.wait_ge(cond_ready, 1)
            for n in range(4):
                ada_pair("start", 0, n)
                ada_turn(n)
            for l, kind in enumerate(KINDS):
                {"gdn": gdn, "gqa": gqa, "mla": mla}[kind](l)
                layer_norm(2 * l, bufh, bufo)
                moe(l)
                if l + 1 < DEPTH:
                    def last_pair():
                        ada_pair("tail", l, 1)
                        ada_turn(ADA_AT["tail", l] + 1)

                    ada_pair("tail", l, 0)
                    ada_turn(ADA_AT["tail", l])
                    layer_norm(2 * l + 1, bufo, bufh, last_pair)
                else:
                    layer_norm(2 * l + 1, bufo, bufh)

        @block.scalar
        def _(act):
            op = nc.scalar.activation
            a = Chain(act, chain_a)

            def copy(out, in_, **kw):
                return op(out, in_, ACT.Copy, **kw)

            def ada_copy(q, u, shift=0):
                used(act, u, shift)
                copy(ada_row[:, :], ps[0:2, 7, :]).then_inc(ada_row_ready, 1)

            def ada_stage(stage, l, n):
                ada_copy(ADA_AT[stage, l] + n, unit_at[stage, l] + 2 * n + 1)

            def layer_norm(n, l, which, rbuf, sqbuf, between=lambda: None):
                act.wait_ge(mean_mm, n + 1)
                copy(lnt[:, 0, :], ps[:, 5, 0:T], scale=1.0 / D).then_inc(mean_ready, 1)
                for q in range(4):
                    act.wait_ge(centred, 4 * n + q + 1)
                    op(sqbuf[:, 2 * q:2 * q + 2, :], rbuf[:, 2 * q:2 * q + 2, :], ACT.Square).then_inc(squared, 1)
                between()
                act.wait_ge(var_mm, n + 1)
                op(lnt[:, 1, :], ps[:, 6, 0:T], ACT.Sqrt, bias=C("eps"), scale=1.0 / D).then_inc(dev_ready, 1)
                for k in range(KT):
                    act.wait_ge(normed, KT * n + k + 1)
                    op(bufx[:, k, :], rbuf[:, k, :], ACT.Identity,
                       bias=ln_b[:, 2 * l + which, k:k + 1]).then_inc(x_ready, 1)

            def head_raw(l, i, j, m):
                if m % 2 == 0:
                    act.wait_ge(tile_mm, i * (2 * HEADS_PER_ITER) + (tiles_at["in", l] + 2 * j + m // 2 + 1))
                else:
                    used(act, head_unit(l, "w", j, m // 2), i * len(gdn_order(l)))
                if m < 3:
                    copy(g_cin[:, m, 2:2 + CTX], ps[:, 6, CTXS])
                    copy(g_cin[:, m, 4 + CTX:4 + T], ps[:, 6, LATS]).then_inc(raw_in, 1)
                else:
                    op(g_z[:, j % 2, :], ps[:, 6, 0:T], ACT.Silu).then_inc(z_in, 1)

            def head_silu(hh, j, m):
                qkv = g_qkv2[:, j % 2, :, :]
                act.wait_ge(conv_done, hh * 3 + m + 1)
                op(qkv[:, m, CTXS], g_acc[:, m, 0:CTX], ACT.Silu)
                op(qkv[:, m, LATS], g_acc[:, m, 2 + CTX:CONVW], ACT.Silu).then_inc(silu_done, 1)

            def head_squares(hh, j):
                act.wait_ge(silu_done, hh * 3 + 2)
                op(g_sq, g_qkv2[:, j % 2, 0:2, :], ACT.Square).then_inc(qk_sq, 1)

            def head_decays(hh, j):
                for d in range(2):
                    act.wait_ge(row_masked, hh * 2 + d + 1)
                    op(g_eq[:, d, :], ps[:, 4 + d, 0:T], ACT.Exp)
                    at = CHUNK - 1 if d == 0 else 0
                    rows = ps[:, 4 + d, 0:T].rearrange("p (n c) -> p n c", c=CHUNK)
                    op(g_last[:, d, :], rows[:, :, at], ACT.Exp)
                    for t in range(TT):
                        last = op(g_w[:, d, t, :], g_w[:, d, t, :], ACT.Exp, bias=g_head2[:, j % 2, 1, t, d:d + 1])
                    last.then_inc(decay_done, 1)

            def head_norms(hh):
                act.wait_ge(nrm_mm, hh + 1)
                op(g_rs, ps[:, 2:4, 0:T], ACT.Sqrt, bias=C("eps")).then_inc(nrm_dev, 1)

            def head_ada(l, i, j, n):
                if l == 0:
                    ada_copy(None, head_unit(l, "ada", j, 2 * n + 1), i * len(gdn_order(l)))

            def gdn(l):
                li = li_of[l]
                act.wait_ge(sp_in, li + 1)
                op(g_tmp[:, 4, 0, :], R("a_log")[:, 16 * li:16 * li + 16], ACT.Exp)
                raw = ps[:, 2, 0:96].rearrange("p (t c) -> p t c", t=TT)
                op(g_tmp[:, 3, :, :], raw[:, :, 16:32], ACT.Exp, scale=-1.0)
                op(g_tmp[:, 2, :, :], g_tmp[:, 2, :, :], ACT.Exp).then_inc(sp_exp, 1)
                act.wait_ge(sp_exp, li + 1)
                op(g_tmp[:, 5, :, :], g_tmp[:, 2, :, :], ACT.Ln, bias=1.0).then_inc(sp_ln, 1)
                act.wait_ge(cum_mm, li + 1)
                cum = ps[:, 3, 0:96].rearrange("p (w t c) -> p w t c", w=2, t=TT)
                a.step(op(g_tmp[:, 0, :, :], cum[:, 0, :, :], ACT.Exp))
                op(g_all[:, 3, :, :], cum[:, 1, :, :], ACT.Exp).then_inc(cum_ready, 1)
                act.wait_ge(pad_zero, li + 1)
                with act.Fori(0, H // HEADS_PER_ITER) as i:
                    for j in range(HEADS_PER_ITER):
                        gdn_head(l, i, j)

            def gdn_head(l, i, j):
                hh = i * HEADS_PER_ITER + (li_of[l] * H + j)
                more = j + 1 < HEADS_PER_ITER
                g_head = g_head2[:, j % 2, :, :, :]
                act.dma_start(g_s0[:, j % 2, :, :], I["state"][hh]).then_inc(s0_in, 16)
                if j == 0:
                    for m in range(4):
                        head_raw(l, i, j, m)
                    for m in range(3):
                        head_silu(hh, j, m)
                    head_squares(hh, j)
                    head_norms(hh)
                if j == 0:
                    head_decays(hh, j)
                act.wait_ge(kv_tr, hh * 2 + 1)
                copy(g_vt.rearrange("p t c -> p (t c)"), ps[:, 0, 0:T]).then_inc(kv_tok, 1)
                if more:
                    head_raw(l, i, j + 1, 0)
                act.wait_ge(kv_tr, hh * 2 + 2)
                copy(g_kt.rearrange("p t c -> p (t c)"), ps[:, 1, 0:T]).then_inc(kv_tok, 1)
                if more:
                    head_raw(l, i, j + 1, 1)
                for n, dst, bank in ((1, g_pa, 1), (2, g_pb, 0), (4, g_nd, 0), (5, g_ndt, 1), (7, g_pa, 1),
                                     (9, g_pb, 1), (10, g_nd, 0), (12, g_pb, 0), (13, g_nd, 1)):
                    for d in range(2):
                        act.wait_ge(inv_mm[d], hh * 15 + n + 1)
                        copy(dst[d].rearrange("p t c -> p (t c)"), ps[:, 4 + d - 2 * bank, 0:T]).then_inc(inv_cp[d], 1)
                    if n == 4:
                        head_ada(l, i, j, 0)
                for k, steps in enumerate(SCAN_ROUNDS):
                    for n, (ch, d, t, half, c0, first) in steps:
                        rows = slice(64 * half, 64 * half + 64)
                        act.wait_ge(vn_mm, hh * 12 + n + 1)
                        copy(g_v[rows, ch, :], ps[rows, ch, P:2 * P],
                             scale=g_head[rows, 4, t, d:d + 1]).then_inc(v_done, 1)
                    if more:
                        if k < 2:
                            head_raw(l, i, j + 1, 2 + k)
                        if k:
                            head_silu(hh + 1, j + 1, k - 1)
                        if k == 3:
                            head_squares(hh + 1, j + 1)
                    if k == 1:
                        act.wait_ge(s_done, hh * 12 + 8)
                        act.dma_start(O["state"][hh], g_state[:, 2:4, :]).then_inc(st_out, 16)
                head_ada(l, i, j, 1)
                act.wait_ge(os_mm, hh * 12 + 12)
                copy(g_o, ps[:, 4, 0:T]).then_inc(o_done, 1)
                if more:
                    head_norms(hh + 1)
                act.wait_ge(o_sum, hh + 1)
                op(g_osq, g_o, ACT.Square).then_inc(o_sq, 1)
                act.wait_ge(o_nrm_mm, hh + 1)
                op(g_ro, ps[:, 0, 0:T], ACT.Sqrt, bias=C("eps"), scale=1.0 / P).then_inc(o_dev, 1)
                if more:
                    head_decays(hh + 1, j + 1)

            def attention(l, heads, first_head, scale):
                a0 = att_at[l] + TT * first_head
                units = [(h, qt) for h in heads for qt in range(TT)]

                def exps(n):
                    nk = P if units[n][1] == 0 else T
                    act.wait_ge(max_done, a0 + n + 1)
                    if a0 + n >= 2:
                        act.wait_ge(pt_mm, a0 + n - 1)
                    op(a_p[:, n % 2, 0:nk], ps[:, n % 2, 0:nk], ACT.Exp, scale=scale, bias=a_st[:, n % 2, 1:2],
                       accum_out=a_st[:, n % 2, 2:3]).then_inc(exp_done, 1)

                exps(0)
                for n, (h, qt) in enumerate(units):
                    if n + 1 < len(units):
                        exps(n + 1)
                    nk = 1 if qt == 0 else 3
                    act.wait_ge(pt_mm, a0 + n + 1)
                    if a0 + n >= 2:
                        act.wait_ge(pv_mm, a0 + n - 1)
                    copy(a_pt[:, n % 2, 0:nk, :].rearrange("p t c -> p (t c)"),
                         ps[:, 2 + n % 2, 0:P * nk]).then_inc(pt_ev, 1)
                    if qt == TT - 1:
                        act.wait_ge(pv_mm, a0 + n + 1)
                        copy(bufo[:, h, :], ps[:, 4 + (n // TT) % 2, 0:T]).then_inc(oh_ev, 1)

            def gqa(l):
                ada_stage("before", l, 0)
                for t in range(12):
                    tile_done(act, "in", l, t)
                    copy(q_qkv[:, t, :], ps[:, t % 2, 0:T]).then_inc(raw_ev, 1)
                    if t < 10:
                        act.wait_ge(raw_ev, t + 1)
                        op(q_sq[:, t, :], q_qkv[:, t, :], ACT.Square).then_inc(at_sq, 1)
                for n in range(10):
                    act.wait_ge(at_nmm, n + 1)
                    op(q_sq[:, n, :], ps[:, 2 + n % 2, 0:T], ACT.Sqrt, bias=C("eps"), scale=1.0 / P).then_inc(at_dev, 1)
                ada_stage("mixer", l, 0)
                act.wait_ge(own_ready, 2)
                for kv in range(2):
                    act.wait_ge(vt_mm, kv + 1)
                    src = ps[:, kv, 0:T].rearrange("p (t c) -> p t c", t=TT)
                    copy(q_vall[:, kv, 0, :], src[:, 0, :])
                    copy(q_vall[:, kv, 2:4, :], src[:, 1:3, :]).then_inc(vt_ev, 1)
                attention(l, range(H), 0, QK_SCALE)

            def mla(l):
                ada_stage("before", l, 0)
                for t in range(6):
                    tile_done(act, "in", l, t)
                    copy(m_c[:, t, :], ps[:, t % 2, 0:T]).then_inc(raw_ev, 1)
                    act.wait_ge(raw_ev, 12 + t + 1)
                    op(m_sq[:, t, :], m_c[:, t, :], ACT.Square).then_inc(at_sq, 1)
                used(act, unit_at["mix", l] + 3)
                copy(m_kr[0:64, :], ps[0:64, 0, 0:T]).then_inc(raw_ev, 1)
                ada_stage("mixer", l, 0)
                for m, n in enumerate((512, 256)):
                    act.wait_ge(at_nmm, 10 + m + 1)
                    op(m_sq[:, m, :], ps[:, 2 + m, 0:T], ACT.Sqrt, bias=C("eps"), scale=1.0 / n).then_inc(at_dev, 1)
                for half in range(2):
                    job = 0
                    ups = 13 * half
                    for k in range(2):
                        for hd in range(2):
                            for rows, dst in ((P, m_qn), (64, m_qr)):
                                if hd == 1 and rows == 64:
                                    used(act, unit_at["mix2", l] + 3 * half + k)
                                else:
                                    ups += 1
                                    act.wait_ge(up_mm, ups)
                                copy(dst[0:rows, 2 * k + hd, :], ps[0:rows, (job + 1) % 2, 0:T]).then_inc(up_ev, 1)
                                job += 1
                    for n in range(8):
                        if n < 7:
                            ups += 1
                            act.wait_ge(up_mm, ups)
                        else:
                            used(act, unit_at["mix2", l] + 2 + 3 * half)
                        dst = m_kn[:, n, :] if n < 4 else m_v[:, n - 4, :]
                        copy(dst, ps[:, (job + 1) % 2, 0:512]).then_inc(up_ev, 1)
                        job += 1
                    attention(l, range(4 * half, 4 * half + 4), 4 * half, MLA_SCALE)

            def gathered(S, n, j):
                for half in range(2):
                    for q in range(2):
                        act.wait_ge(S["ga"], n * 5 + 2 * half + q + 1)
                        copy(e_hs[:, j, half, 4 * q:4 * q + 4, :].rearrange("p k c -> p (k c)"),
                             ps[:, 5 + q, :]).then_inc(S["ga_ev"], 1)

            def split_high(S, n, p, w):
                act.wait_ge(S["wfree"], n + 1)
                copy(e_whi[:, p % SPLITS, :], w).then_inc(S["whi"], 1)

            def gate_silu(S, used_pieces, e):
                act.wait_ge(S["wfree"], used_pieces)
                op(e_sg[:, e % 2, :], ps[:, e % 2, 0:DE], ACT.Silu).then_inc(S["sg"], 1)

            def hidden_t(S, n, e):
                act.wait_ge(S["tr"], n + 1)
                b = e % 2
                copy(e_hidT[:, b, 0, :, :].rearrange("p f c -> p (f c)"),
                     ps[:, 2, 256 * b:256 * b + 256]).then_inc(S["thi"], 1)

            def y_high(S, used_pieces):
                act.wait_ge(S["wfree"], used_pieces)
                copy(e_yhi[:, :].rearrange("p (y c) -> p y c", y=2), ps[:, 3:5, :]).then_inc(S["yhi"], 1)

            def moe(l):
                ada = l < DEPTH - 1
                if ada:
                    ada_stage("router", l, 0)
                    ada_stage("router", l, 1)
                act.wait_ge(rt_mm, l + 1)
                op(e_rt[:, 0, :], ps[:, 2, 0:TT * NE], ACT.Sigmoid).then_inc(score_ready, 1)
                for n in range(2 * TT):
                    act.wait_ge(tk_mm, 2 * TT * l + n + 1)
                    copy(e_hi[:, n // 2, 512 * (n % 2):512 * (n % 2) + 512], ps[:, 5 + n % 2, :]).then_inc(tk_hi, 1)
                    if n == 1:
                        if ada:
                            ada_stage("route", l, 0)
                        act.wait_ge(row2_mm, l + 1)
                        copy(e_sidrow, ps[:, 2, P:P + T]).then_inc(row2_ready, 1)
                    if ada and n % 2:
                        ada_stage("route", l, n // 2 + 1)
                u0, per = unit_at["moe", l], len(MOE_UNITS)
                with act.Fori(0, NG // 2) as i:
                    for kind, j, e, p in MOE_FOLLOW:
                        gg = i * 2 + (NG * l + j)
                        n = i * (2 * EPG) + (NE * l + EPG * j + e)
                        before = i * (2 * per) + (2 * per * (NG // 2) * l + SPLITS)
                        if kind == "P":
                            u = u0 + p // 2
                            if p % 2 == 0:
                                landed(act, u, i * (per // RING))
                            split_high(F, i * (2 * per) + (2 * per * (NG // 2) * l + p), p,
                                       unit(u)[:, PIECE * (p % 2):PIECE * (p % 2) + PIECE])
                        elif kind == "g":
                            gathered(F, gg, j)
                        elif kind == "u":
                            gate_silu(F, before + MOE_PIECE_OF["U", j, e, 3] + 1, e)
                        elif kind == "t":
                            hidden_t(F, n, e)
                        elif kind == "y":
                            y_high(F, before + MOE_PIECE_OF["D", j, e, 1] + 1)
                act.wait_ge(flags_ready, l + 1)
                crowded = act.value_load(flags[0:1, 0, 2:3], min_val=0, max_val=1)
                with act.If(crowded > 0):
                    with act.Fori(0, NG) as g:
                        for b in range(2):
                            n = g * 2 + (2 * NG * l + b)
                            more = act.value_load(flags[0:1, g, b:b + 1], min_val=0, max_val=1)
                            with act.If(more > 0):
                                gathered(X, n, 0)
                                for e in range(EPG):
                                    before = n * (EPG * PIECES) + SPLITS
                                    for k in range(PIECES):
                                        p = PIECES * e + k
                                        if k == 4:
                                            gate_silu(X, before + p, e)
                                            hidden_t(X, n * EPG + e, e)
                                        if p:
                                            act.wait_ge(X["wlo"], n * (EPG * PIECES) + p)
                                        src = I["moe"][g * EPG + (NE * l + e), :, k * PIECE:(k + 1) * PIECE]
                                        act.dma_start(spare[:, 0:PIECE], src).then_inc(x_w, 16)
                                        act.wait_ge(x_w, (n * (EPG * PIECES) + (p + 1)) * 16)
                                        split_high(X, n * (EPG * PIECES) + p, p, spare[:, 0:PIECE])
                                y_high(X, n * (EPG * PIECES) + (SPLITS + EPG * PIECES))
                                act.wait_ge(X["sc_ev"], n * KT + KT)
                                copy(e_sg[:, 0, 0:1], C("eps"))
                            with act.Else():
                                act.sem_inc(X["ga_ev"], 4)
                                act.sem_inc(X["whi"], EPG * PIECES)
                                act.sem_inc(X["sg"], EPG)
                                act.sem_inc(X["thi"], EPG)
                                act.sem_inc(X["yhi"], 1)
                                act.sem_inc(x_w, 16 * EPG * PIECES)
                with act.Else():
                    act.sem_inc(X["ga_ev"], BLOCKS * 4)
                    act.sem_inc(X["whi"], BLOCKS * EPG * PIECES)
                    act.sem_inc(X["sg"], BLOCKS * EPG)
                    act.sem_inc(X["thi"], BLOCKS * EPG)
                    act.sem_inc(X["yhi"], BLOCKS)
                    act.sem_inc(x_w, BLOCKS * 16 * EPG * PIECES)

            act.wait_ge(params_in, 16)
            op(silc[:, :, :], cond, ACT.Silu).then_inc(cond_ready, 1)
            act.wait_ge(consts_in, 16)
            for n in range(4):
                ada_stage("start", 0, n)
            for l, kind in enumerate(KINDS):
                {"gdn": gdn, "gqa": gqa, "mla": mla}[kind](l)
                layer_norm(2 * l, l, 0, bufh, bufo)
                moe(l)
                if l + 1 < DEPTH:
                    ada_stage("tail", l, 0)
                    layer_norm(2 * l + 1, l, 1, bufo, bufh, lambda: ada_stage("tail", l, 1))
                else:
                    layer_norm(2 * l + 1, l, 1, bufo, bufh)

        @block.vector
        def _(dve):
            V = nc.vector
            v = Chain(dve, chain_v)
            tt_, ts_, stt = V.tensor_tensor, V.tensor_scalar, V.scalar_tensor_tensor

            def ada_add(q):
                dve.wait_ge(ada_tr, q + 1)
                at = q * 4
                if isinstance(q, int):
                    rows, bias = mod_pairs[:, q, :], b_pairs[:, 4 * q:4 * q + 4]
                else:
                    rows, bias = mod_pairs[:, q, :], b_pairs[:, bass.ds(at, 4)]
                tt_(rows.rearrange("p (m s) -> p m s", s=2), ps[:, 7, 0:8].rearrange("p (m s) -> p m s", s=2),
                    wide(bias, 2), ALU.add).then_inc(mod_ready, 1)

            def modulate(l, which):
                n = 2 * l + which
                for k in range(KT):
                    if n == 0:
                        dve.wait_ge(x_in, 16)
                    else:
                        dve.wait_ge(x_ready, KT * (n - 1) + k + 1)
                    for seg, cols in enumerate((CTXS, LATS)):
                        last = ts_(bufh[:, k, cols], bufx[:, k, cols], mrow(l, 3 * which + 1, k, seg),
                                   mrow(l, 3 * which, k, seg), ALU.mult, ALU.add)
                    last.then_inc(h_ready, 1)

            def residual(l, which, src, rbuf, ready):
                n = 2 * l + which
                dve.wait_ge(ax_ready, n + 1)
                for k in range(KT):
                    ready(k)
                    for seg, cols in enumerate((CTXS, LATS)):
                        last = stt(rbuf[:, k, cols], src(k)[:, cols], mrow(l, 3 * which + 2, k, seg), bufx[:, k, cols],
                                   ALU.mult, ALU.add)
                    last.then_inc(r_ready, 1)

            def layer_norm(n, l, which, rbuf, between=lambda: None):
                dve.wait_ge(mean_ready, n + 1)
                dve.wait_ge(r_ready, KT * (n + 1))
                for q in range(4):
                    tiles = rbuf[:, 2 * q:2 * q + 2, :]
                    tt_(tiles, tiles, spread(lnt[:, 0, :], 2), ALU.subtract).then_inc(centred, 1)
                between()
                dve.wait_ge(dev_ready, n + 1)
                v.step(V.reciprocal(lnt[:, 1, :], lnt[:, 1, :]))
                v.wait()
                dve.wait_ge(centred, 4 * n + 4)
                for k in range(KT):
                    stt(rbuf[:, k, :], rbuf[:, k, :], ln_g[:, 2 * l + which, k:k + 1], lnt[:, 1, :],
                        ALU.mult, ALU.mult).then_inc(normed, 1)

            def gdn(l):
                li = li_of[l]
                dve.wait_ge(ab_mm, li + 1)
                raw = ps[:, 2, 0:96].rearrange("p (t c) -> p t c", t=TT)
                v.step(tt_(g_tmp[:, 0, :, :], raw[:, :, 0:16], spread(R("dt_bias")[:, 16 * li:16 * li + 16], TT), ALU.add))
                v.wait()
                v.step(ts_(g_tmp[:, 1, :, :], g_tmp[:, 0, :, :], 0.0, None, ALU.max))
                v.wait()
                stt(g_tmp[:, 2, :, :], g_tmp[:, 1, :, :], -2.0, g_tmp[:, 0, :, :], ALU.mult, ALU.add).then_inc(sp_in, 1)
                dve.wait_ge(sp_exp, li + 1)
                v.step(ts_(g_tmp[:, 3, :, :], g_tmp[:, 3, :, :], 1.0, None, ALU.add))
                v.wait()
                v.step(V.reciprocal(g_all[:, 4, :, :], g_tmp[:, 3, :, :]))
                v.wait()
                v.step(ts_(g_all[:, 5, :, :], g_all[:, 4, :, :], -1.0, None, ALU.mult))
                dve.wait_ge(sp_ln, li + 1)
                v.step(tt_(g_tmp[:, 1, :, :], g_tmp[:, 1, :, :], g_tmp[:, 5, :, :], ALU.add))
                v.wait()
                stt(g_all[:, 0, :, :], g_tmp[:, 1, :, :], -1.0, spread(g_tmp[:, 4, 0, :], TT),
                    ALU.mult, ALU.mult).then_inc(g_ready, 1)
                dve.wait_ge(cum_mm, li + 1)
                cum = ps[:, 3, 0:48].rearrange("p (t c) -> p t c", t=TT)
                dve.wait_ge(cum_ready, 2 * li + 1)
                v.step(ts_(g_all[:, 1, :, :], cum, -1.0, None, ALU.mult))
                ts_(g_all[:, 2, :, :], g_tmp[:, 0, :, :], -1.0, None, ALU.mult).then_inc(cum_ready, 1)
                dve.wait_ge(cum_ready, 2 * li + 2)
                dve.wait_ge(pad_zero, li + 1)
                with dve.Fori(0, H // HEADS_PER_ITER) as i:
                    v.enter(i, HEADS_PER_ITER * 16)
                    for j in range(HEADS_PER_ITER):
                        gdn_head(l, i, j)
                    turns = H // HEADS_PER_ITER
                v.leave(turns)
                if l == 0:
                    dve.wait_ge(mod_ready, ADA_UNITS // 2)
                residual(l, 0, lambda k: ps[:, k % 2, :], bufh, lambda k: tile_done(dve, "out", l, k))

            def head_columns(l, i, j):
                hh = i * HEADS_PER_ITER + (li_of[l] * H + j)
                cols = g_all.rearrange("p a b (d h) -> p h (a b) d", h=H)
                V.tensor_copy(g_head2[:, j % 2, :, :, :].rearrange("p a b d -> p (a b) d"),
                              cols[:, i * HEADS_PER_ITER + j, :, :]).then_inc(head_cols, 1)
                v.step(V.tensor_copy(g_taps.rearrange("p a b -> p (a b)"), conv[:, hh, :]))

            def convolve(hh, m):
                dve.wait_ge(raw_in, hh * 3 + m + 1)
                v.wait()
                acc = g_acc[:, m, :]
                v.step(ts_(acc, g_cin[:, m, 0:CONVW], g_taps[:, m, 0:1], None, ALU.mult))
                for tap in range(1, TAPS):
                    v.wait()
                    last = stt(acc, g_cin[:, m, tap:tap + CONVW], g_taps[:, m, tap:tap + 1], acc, ALU.mult, ALU.add)
                    if tap < TAPS - 1:
                        v.step(last)
                last.then_inc(conv_done, 1)

            def mask_rows(hh):
                for d in range(2):
                    dve.wait_ge(row_mm, hh * 2 + d + 1)
                    tt_(g_w[:, d, :, :], ps[:, 4 + d, 0:T].rearrange("p (t c) -> p t c", t=TT),
                        spread(C(f"inv{d}"), TT), ALU.subtract).then_inc(row_masked, 1)

            def normalize(hh, j):
                qkv = g_qkv2[:, j % 2, :, :]
                dve.wait_ge(nrm_dev, hh + 1)
                v.step(V.reciprocal(g_rs, g_rs))
                v.wait()
                dve.wait_ge(silu_done, hh * 3 + 3)
                tt_(qkv[:, 1, :], qkv[:, 1, :], g_rs[:, 1, :], ALU.mult).then_inc(qk_ready, 1)
                stt(qkv[:, 0, :], qkv[:, 0, :], QK_SCALE, g_rs[:, 0, :], ALU.mult, ALU.mult).then_inc(qk_ready, 1)

            def gdn_head(l, i, j):
                li = li_of[l]
                h = i * HEADS_PER_ITER + j
                hh = i * HEADS_PER_ITER + (li * H + j)
                more = j + 1 < HEADS_PER_ITER
                g_head = g_head2[:, j % 2, :, :, :]
                if j == 0:
                    head_columns(l, i, j)
                    for m in range(3):
                        convolve(hh, m)
                if j == 0:
                    mask_rows(hh)
                    normalize(hh, j)
                dve.wait_ge(gram_mm, hh * 2 + 2)
                dve.wait_ge(head_cols, hh + 1)
                for d in range(2):
                    dve.wait_ge(strict_done, hh * 2 + d + 1)
                    for t in range(TT):
                        last = stt(g_n[d][:, t, :], ps[:, 2, P * t:P * t + P], g_head[:, 5, t, d:d + 1], g_n[d][:, t, :],
                                   ALU.mult, ALU.mult)
                    last.then_inc(n_done, 1)
                for d in range(2):
                    wd = g_w[:, d, :, :].rearrange("p t c -> p (t c)")
                    tt_(wd, wd, ps[:, 3, 0:T], ALU.mult).then_inc(w_done, 1)
                for d in range(2):
                    dve.wait_ge(inv_mm[d], hh * 15 + 1)
                    src = ps[:, 4 + d, 0:T].rearrange("p (t c) -> p t c", t=TT)
                    for dst, mask in ((g_ndt, "diag16"), (g_t32, "off32"), (g_t64, "off64")):
                        last = tt_(dst[d], src, spread(C(mask), TT), ALU.mult)
                    last.then_inc(inv_x[d], 1)
                for s, (n, bank) in enumerate(((3, 1), (6, 0), (8, 0), (11, 1), (14, 0))):
                    for d in range(2):
                        dve.wait_ge(inv_mm[d], hh * 15 + n + 1)
                        dve.wait_ge(inv_x[d], hh * 6 + s + 1)
                        x = g_x[d].rearrange("p t c -> p (t c)")
                        tt_(x, x, ps[:, 4 + d - 2 * bank, 0:T], ALU.add).then_inc(inv_x[d], 1)
                for k, steps in enumerate(SCAN_ROUNDS):
                    for n, (ch, d, t, half, c0, first) in steps:
                        rows = slice(64 * half, 64 * half + 64)
                        dve.wait_ge(ks_mm, hh * 12 + n + 1)
                        stt(g_y[rows, ch, :], ps[rows, ch, 0:P], g_head[rows, 2, t, d:d + 1], g_vt[rows, t, :],
                            ALU.mult, ALU.add).then_inc(y_done, 1)
                    if k == 0:
                        if l == 0:
                            ada_add(i * (2 * HEADS_PER_ITER) + (ADA_AT["head", l] + 2 * j))
                        if more:
                            head_columns(l, i, j + 1)
                    if more and k < 3:
                        convolve(hh + 1, k)
                    for n, (ch, d, t, half, c0, first) in steps:
                        dve.wait_ge(os_mm, hh * 12 + n + 1)
                        if k:
                            dve.wait_ge(s_done, hh * 12 + SCAN_PREV[n] + 1)
                        ck = c0 // CHUNK
                        stt(g_state[:, ch, :], scan_state(ch, d, first, j), g_last[:, d, ck:ck + 1],
                            ps[:, ch, 3 * P:4 * P], ALU.mult, ALU.add).then_inc(s_done, 1)
                if l == 0:
                    ada_add(i * (2 * HEADS_PER_ITER) + (ADA_AT["head", l] + 2 * j + 1))
                dve.wait_ge(o_done, hh + 1)
                tt_(g_o, g_o, ps[:, 5, 0:T], ALU.add).then_inc(o_sum, 1)
                if more:
                    mask_rows(hh + 1)
                    normalize(hh + 1, j + 1)
                dve.wait_ge(o_dev, hh + 1)
                v.step(V.reciprocal(g_ro, g_ro))
                v.wait()
                v.step(stt(g_o, g_o, R("gdn_g")[:, li:li + 1], g_ro, ALU.mult, ALU.mult))
                v.wait()
                dve.wait_ge(z_in, hh + 1)
                dve.wait_ge(st_out, hh * 16 + 16)
                tt_(bufo[:, h, :], g_o, g_z[:, j % 2, :], ALU.mult).then_inc(head_done, 1)

            def attention(l, heads, first_head, scale):
                a0 = att_at[l] + TT * first_head
                units = [(h, qt) for h in heads for qt in range(TT)]

                def maximum(n):
                    nk = P if units[n][1] == 0 else T
                    dve.wait_ge(sc_mm, a0 + n + 1)
                    v.step(V.reduce_max(a_st[:, n % 2, 0:1], ps[:, n % 2, 0:nk], AX.X))
                    v.wait()
                    ts_(a_st[:, n % 2, 1:2], a_st[:, n % 2, 0:1], -scale, None, ALU.mult).then_inc(max_done, 1)

                maximum(0)
                for n, (h, qt) in enumerate(units):
                    if n + 1 < len(units):
                        maximum(n + 1)
                    nk = P if qt == 0 else T
                    dve.wait_ge(exp_done, a0 + n + 1)
                    v.step(V.reciprocal(a_st[:, n % 2, 3:4], a_st[:, n % 2, 2:3]))
                    v.wait()
                    pb = a_p[:, n % 2, 0:nk]
                    ts_(pb, pb, a_st[:, n % 2, 3:4], None, ALU.mult).then_inc(p_done, 1)

            def rotate(dst, x, bank, rows, cos, sin, before):
                if before:
                    dve.wait_ge(rot_done, before)
                n = x.shape[1]
                rot = ps[0:rows, bank, 0:n * LAT].rearrange("p (n c) -> p n c", n=n)
                tmp = a_tmp[0:rows, 0:n, :]
                v.step(tt_(tmp, rot, spread(C(sin, rows), n), ALU.mult))
                v.step(tt_(x, x, spread(C(cos, rows), n), ALU.mult))
                v.wait()
                return tt_(dst, x, tmp, ALU.add)

            def gqa(l):
                ada_add(ADA_AT["before", l])
                for n in range(10):
                    dve.wait_ge(at_dev, n + 1)
                    v.step(V.reciprocal(q_sq[:, n, :], q_sq[:, n, :]))
                    v.wait()
                    g = R("gqa_q") if n < H else R("gqa_k")
                    stt(q_qkv[:, n, :], q_qkv[:, n, :], g, q_sq[:, n, :], ALU.mult, ALU.mult).then_inc(at_normed, 1)
                ada_add(ADA_AT["mixer", l])
                dve.wait_ge(at_normed, 10)
                for kv in range(2):
                    V.tensor_copy(q_kall[:, kv, 0:CTX], q_qkv[:, H + kv, CTXS]).then_inc(own_ready, 1)
                for n in range(5):
                    dve.wait_ge(rot_mm, n + 1)
                    x = q_qkv[:, 2 * n:2 * n + 2, LATS]
                    dst = x if n < 4 else q_kall[:, :, P + PAST:NK]
                    rotate(dst, x, 4 + n % 2, P, "cos128", "sin128", n).then_inc(rot_done, 1)
                attention(l, range(H), 0, QK_SCALE)
                residual(l, 0, lambda k: ps[:, k % 2, :], bufh, lambda k: tile_done(dve, "out", l, k))

            def mla(l):
                ada_add(ADA_AT["before", l])
                dve.wait_ge(at_dev, 10 + 2)
                v.step(V.reciprocal(m_sq[:, 0:2, :], m_sq[:, 0:2, :]))
                ada_add(ADA_AT["mixer", l])
                v.wait()
                for n in range(6):
                    g = R("mla_q")[:, n:n + 1] if n < 4 else R("mla_kv")[:, n - 4:n - 3]
                    stt(m_c[:, n, :], m_c[:, n, :], g, m_sq[:, 0 if n < 4 else 1, :],
                        ALU.mult, ALU.mult).then_inc(at_normed, 1)
                dve.wait_ge(at_normed, 10 + 6)
                v.step(V.tensor_copy(m_krall[0:64, 0:CTX], m_kr[0:64, CTXS]))
                for n in range(2):
                    V.tensor_copy(m_ckv[:, n, 0:CTX], m_c[:, 4 + n, CTXS]).then_inc(own_ready, 1)
                    V.tensor_copy(m_ckv[:, n, P + PAST:NK], m_c[:, 4 + n, LATS]).then_inc(own_ready, 1)
                dve.wait_ge(rot_mm, 6)
                dve.wait_ge(raw_ev, 12 + 7)
                rotate(m_krall[0:64, P + PAST:NK].rearrange("p (o c) -> p o c", o=1),
                       m_kr[0:64, LATS].rearrange("p (o c) -> p o c", o=1), 4, 64, "cos64", "sin64",
                       5).then_inc(rot_done, 1)
                for half in range(2):
                    for m in range(2):
                        dve.wait_ge(rot_mm, 6 + 2 * half + m + 1)
                        x = m_qr[0:64, 2 * m:2 * m + 2, LATS]
                        rotate(x, x, 4 + m, 64, "cos64", "sin64", 6 + 2 * half + m).then_inc(rot_done, 1)
                        dve.wait_ge(rot_done, 6 + 2 * half + m + 1)
                    attention(l, range(4 * half, 4 * half + 4), 4 * half, MLA_SCALE)
                residual(l, 0, lambda k: ps[:, k % 2, :], bufh, lambda k: tile_done(dve, "out", l, k))

            def route(l):
                ada = l < DEPTH - 1
                if ada:
                    ada_add(ADA_AT["router", l])
                    ada_add(ADA_AT["router", l] + 1)
                e_ = [e_rt[:, n, :] for n in range(10)]
                score, sel, t1, t2, t3, m3, o1, o2, oh, comb = e_
                as16 = lambda x: x.rearrange("p (t e) -> p t e", t=TT)
                dve.wait_ge(score_ready, l + 1)
                v.step(tt_(as16(sel), as16(score), spread(R("router_b"), TT), ALU.add))
                v.wait()
                pair = sel.rearrange("p (g a b) -> p g a b", a=2, b=2)
                hi = t1[:, 0:24].rearrange("p (g a) -> p g a", a=2)
                lo = t2[:, 0:24].rearrange("p (g a) -> p g a", a=2)
                v.step(tt_(hi, pair[:, :, :, 0], pair[:, :, :, 1], ALU.max))
                v.step(tt_(lo, pair[:, :, :, 0], pair[:, :, :, 1], ALU.min))
                v.wait()
                first, second, third = t3[:, 0:12], t3[:, 12:24], t3[:, 24:36]
                v.step(tt_(first, hi[:, :, 0], hi[:, :, 1], ALU.max))
                v.step(tt_(second, hi[:, :, 0], hi[:, :, 1], ALU.min))
                v.step(tt_(third, lo[:, :, 0], lo[:, :, 1], ALU.max))
                v.wait()
                v.step(tt_(second, second, third, ALU.max))
                v.wait()
                v.step(tt_(first, first, second, ALU.add))
                v.wait()

                def one_hot(out, x, n, weights, best):
                    v.step(V.tensor_reduce(best, x, AX.X, ALU.max))
                    v.wait()
                    v.step(tt_(out, x, wide(best, n), ALU.is_equal))
                    v.wait()
                    v.step(tt_(out, out, spread(weights, TT), ALU.mult))
                    v.wait()
                    v.step(V.tensor_reduce(best, out, AX.X, ALU.max))
                    v.wait()
                    return tt_(out, out, wide(best, n), ALU.is_equal)

                gs = first.rearrange("p (t g) -> p t g", t=TT)
                ohg = oh[:, 0:TT * NG].rearrange("p (t g) -> p t g", t=TT)
                one_hot(ohg, gs, NG, C("first4"), m3[:, 0:TT]).then_inc(oh_ready, 1)
                dve.wait_ge(oh_ready, l + 1)

                def low_parts(first):
                    for n in (first, first + 1):
                        dve.wait_ge(tk_hi, 2 * TT * l + n + 1)
                        cols = slice(512 * (n % 2), 512 * (n % 2) + 512)
                        tt_(e_lo[:, n // 2, cols], ps[:, 5 + n % 2, :], e_hi[:, n // 2, cols].bitcast(F32),
                            ALU.subtract).then_inc(tk_lo, 1)

                dve.wait_ge(rk_mm, l + 1)
                rank = ps[:, 2, 64:76].rearrange("p (t g) -> p t g", t=TT)
                slot = t1[:, 0:12].rearrange("p (t g) -> p t g", t=TT)
                v.step(V.tensor_copy(e_cnt[:, :], ps[:, 2, 80:84]))
                v.step(tt_(slot, rank, spread(C("group_off"), TT), ALU.add))
                v.wait()
                v.step(tt_(slot, slot, ohg, ALU.mult))
                v.wait()
                V.tensor_reduce(e_sid[:, 0, :], slot, AX.X, ALU.add).then_inc(sid_ready, 1)
                for b in range(2):
                    ts_(flags[:, :, b], e_cnt[:, :], float(P * (b + 1)), None, ALU.is_gt)
                v.step(V.tensor_reduce(m3[:, 46:47], e_cnt[:, :], AX.X, ALU.max))
                v.wait()
                ts_(flags[:, 0, 2:3], m3[:, 46:47], float(P), None, ALU.is_gt).then_inc(flags_ready, 1)
                if ada:
                    ada_add(ADA_AT["route", l])
                low_parts(0)
                sel4, tmp4 = sel.rearrange("p (n e) -> p n e", e=EPG), t2.rearrange("p (n e) -> p n e", e=EPG)
                v.step(tt_(tmp4, sel4, wide(oh[:, 0:TT * NG], EPG), ALU.mult))
                v.step(ts_(m3[:, 16:16 + TT * NG], oh[:, 0:TT * NG], BIG, -BIG, ALU.mult, ALU.add))
                v.wait()
                v.step(tt_(tmp4, tmp4, wide(m3[:, 16:16 + TT * NG], EPG), ALU.add))
                v.wait()
                v.step(one_hot(as16(o1), as16(t2), NE, C("first16"), m3[:, 0:TT]))
                v.wait()
                v.step(stt(t2, o1, -4 * BIG, t2, ALU.mult, ALU.add))
                v.wait()
                v.step(one_hot(as16(o2), as16(t2), NE, C("first16"), m3[:, 0:TT]))
                v.wait()
                v.step(tt_(o1, o1, o2, ALU.add))
                v.wait()
                v.step(tt_(o1, o1, score, ALU.mult))
                v.wait()
                v.step(V.tensor_reduce(m3[:, 0:TT], as16(o1), AX.X, ALU.add))
                v.wait()
                v.step(V.reciprocal(m3[:, 3:3 + TT], m3[:, 0:TT]))
                v.wait()
                v.step(tt_(as16(comb), as16(o1), wide(m3[:, 3:3 + TT], NE), ALU.mult))
                for n in (1, 2):
                    low_parts(2 * n)
                    if ada:
                        ada_add(ADA_AT["route", l] + n)
                if ada:
                    ada_add(ADA_AT["route", l] + 3)
                dve.wait_ge(row2_ready, l + 1)
                dve.wait_ge(sid_ready, l + 1)
                v.wait()

            def pick(S, j, column):
                base, slot = C("block_base")[:, bass.ds(column, 1)], C("block_slot")[:, bass.ds(column, 1)]
                v.step(ts_(e_sid[:, 1 + j, :], e_sid[:, 0, :], base, None, ALU.subtract))
                v.step(ts_(e_put[:, j, :], e_sidrow, slot, None, ALU.is_equal))
                v.wait()
                for t in range(TT):
                    last = ts_(e_pick[:, j, t, :], C("iota"), e_sid[:, 1 + j, t:t + 1], None, ALU.is_equal)
                last.then_inc(S["pick"], 1)

            def weights(S, n, j):
                dve.wait_ge(S["ga"], n * 5 + 5)
                V.tensor_copy(e_cs[:, j, :], ps[:, 7, 96 + 4 * j:100 + 4 * j]).then_inc(S["cs"], 1)
                dve.wait_ge(S["cs"], n + 1)

            def hidden(S, n, j, e):
                dve.wait_ge(S["sg"], n + 1)
                b = e % 2
                stt(e_hid[:, b, :], ps[:, b, DE:2 * DE], e_cs[:, j, e:e + 1], e_sg[:, b, :],
                    ALU.mult, ALU.mult).then_inc(S["hid"], 1)

            def split_low(S, n, p, w):
                b = p % SPLITS
                dve.wait_ge(S["whi"], n + 1)
                return tt_(e_wlo[:, b, :], w, e_whi[:, b, :].bitcast(F32), ALU.subtract)

            def hidden_low(S, n, e):
                dve.wait_ge(S["thi"], n + 1)
                b = e % 2
                tt_(e_hidT[:, b, 1, :, :], ps[:, 2, 256 * b:256 * b + 256].rearrange("p (f c) -> p f c", f=2),
                    e_hidT[:, b, 0, :, :].bitcast(F32), ALU.subtract).then_inc(S["tlo"], 1)

            def y_low(S, n):
                dve.wait_ge(S["yhi"], n + 1)
                tt_(e_ylo[:, :].rearrange("p (y c) -> p y c", y=2), ps[:, 3:5, :],
                    e_yhi[:, :].bitcast(F32).rearrange("p (y c) -> p y c", y=2), ALU.subtract).then_inc(S["ylo"], 1)

            def scattered(S, n):
                for ft in range(KT):
                    dve.wait_ge(S["sc"], n * KT + ft + 1)
                    tt_(bufo[:, ft, :], bufo[:, ft, :], ps[:, 5 + ft % 2, 0:T], ALU.add).then_inc(S["sc_ev"], 1)

            def moe(l):
                route(l)
                dve.wait_ge(o_zero, l + 1)
                per = len(MOE_UNITS)
                with dve.Fori(0, NG // 2) as i:
                    v.enter(i, 4)
                    for j in range(2):
                        pick(F, j, i * 2 + j)
                    for kind, j, e, p in MOE_FOLLOW:
                        gg = i * 2 + (NG * l + j)
                        n = i * (2 * EPG) + (NE * l + EPG * j + e)
                        if kind == "P":
                            w = unit(unit_at["moe", l] + p // 2)[:, PIECE * (p % 2):PIECE * (p % 2) + PIECE]
                            last = split_low(F, i * (2 * per) + (2 * per * (NG // 2) * l + p), p, w)
                            last.then_inc(F["wlo"], 1)
                        elif kind == "g":
                            weights(F, gg, j)
                        elif kind == "u":
                            hidden(F, n, j, e)
                        elif kind == "t":
                            hidden_low(F, n, e)
                        elif kind == "y":
                            y_low(F, gg)
                        elif kind == "s":
                            if j == 1:
                                dve.wait_ge(F["sc_ev"], gg * KT)
                            scattered(F, gg)
                v.leave(NG // 2)
                dve.wait_ge(F["sc_ev"], NG * KT * (l + 1))
                crowded = dve.value_load(flags[0:1, 0, 2:3], min_val=0, max_val=1)
                before_all = (v.base, v.n)
                with dve.If(crowded > 0):
                    with dve.Fori(0, NG) as g:
                        v.enter(g, 4)
                        for b in range(2):
                            n = g * 2 + (2 * NG * l + b)
                            more = dve.value_load(flags[0:1, g, b:b + 1], min_val=0, max_val=1)
                            before = v.n
                            with dve.If(more > 0):
                                pick(X, 0, g * 2 + (NG + b))
                                weights(X, n, 0)
                                for e in range(EPG):
                                    for k in range(PIECES):
                                        if k == 4:
                                            hidden(X, n * EPG + e, 0, e)
                                            hidden_low(X, n * EPG + e, e)
                                        p = PIECES * e + k
                                        split_low(X, n * (EPG * PIECES) + p, p, spare[:, 0:PIECE]).then_inc(X["wlo"], 1)
                                y_low(X, n)
                                scattered(X, n)
                                dve.wait_ge(X["sc_ev"], n * KT + KT)
                                V.memset(e_cnt[:, 0:1], 0.0)
                            with dve.Else():
                                dve.sem_inc(chain_v, v.n - before)
                                dve.sem_inc(X["pick"], 1)
                                dve.sem_inc(X["cs"], 1)
                                dve.sem_inc(X["wlo"], EPG * PIECES)
                                dve.sem_inc(X["tlo"], EPG)
                                dve.sem_inc(X["hid"], EPG)
                                dve.sem_inc(X["ylo"], 1)
                                dve.sem_inc(X["sc_ev"], KT)
                    v.leave(NG)
                with dve.Else():
                    dve.sem_inc(chain_v, v.n - before_all[1])
                    dve.sem_inc(X["pick"], BLOCKS)
                    dve.sem_inc(X["cs"], BLOCKS)
                    dve.sem_inc(X["wlo"], BLOCKS * EPG * PIECES)
                    dve.sem_inc(X["tlo"], BLOCKS * EPG)
                    dve.sem_inc(X["hid"], BLOCKS * EPG)
                    dve.sem_inc(X["ylo"], BLOCKS)
                    dve.sem_inc(X["sc_ev"], BLOCKS * KT)
                residual(l, 1, lambda k: bufo[:, k, :], bufo, lambda k: None)

            dve.wait_ge(params_in, 16)
            dve.wait_ge(consts_in, 16)
            for s in (1, 4):
                rows = b_ada[:, :, KT * s:KT * s + 2 * KT]
                ts_(rows, rows, 1.0, None, ALU.add).then_inc(bias_ready, 1)
            dve.wait_ge(bias_ready, 2)
            for n in range(4):
                ada_add(n)
            for l, kind in enumerate(KINDS):
                dve.wait_ge(mod_ready, l * (ADA_UNITS // 2) + (ADA_UNITS // 2 if l else 4))
                modulate(l, 0)
                {"gdn": gdn, "gqa": gqa, "mla": mla}[kind](l)
                layer_norm(2 * l, l, 0, bufh)
                modulate(l, 1)
                moe(l)
                if l + 1 < DEPTH:
                    ada_add(ADA_AT["tail", l])
                    layer_norm(2 * l + 1, l, 1, bufo, lambda: ada_add(ADA_AT["tail", l] + 1))
                else:
                    layer_norm(2 * l + 1, l, 1, bufo)

        @block.gpsimd
        def _(pool):
            G = nc.gpsimd

            def scale_residual(n):
                pool.wait_ge(h_ready, KT * (n + 1))
                G.tensor_scalar(bufx[:, :, :], bufx[:, :, :], ALPHA, None, ALU.mult).then_inc(ax_ready, 1)

            def gdn(l):
                li = li_of[l]
                pool.wait_ge(h_ready, KT * (2 * l + 1))
                G.memset(g_cin, 0.0)
                G.memset(g_y, 0.0)
                G.memset(g_zero, 0.0).then_inc(pad_zero, 1)
                scale_residual(2 * l)
                with pool.Fori(0, H // HEADS_PER_ITER) as i:
                    for j in range(HEADS_PER_ITER):
                        hh = i * HEADS_PER_ITER + (li * H + j)
                        g_head = g_head2[:, j % 2, :, :, :]
                        for d in range(2):
                            pool.wait_ge(decay_done, hh * 2 + d + 1)
                            G.tensor_tensor(g_n[d], g_w[:, d, :, :], spread(C(f"lt{d}"), TT), ALU.mult)\
                                .then_inc(strict_done, 1)
                        for d in range(2):
                            pool.wait_ge(n_done, hh * 2 + d + 1)
                            G.tensor_tensor(g_nd[d], g_n[d], spread(C("diag16"), TT), ALU.mult).then_inc(nd_done, 1)
                            pool.wait_ge(nd_done, hh * 2 + d + 1)
                            G.tensor_tensor(g_x[d], g_nd[d], spread(ident, TT), ALU.add).then_inc(x1_done, 1)
                        pool.wait_ge(kv_tok, hh * 2 + 2)
                        pool.wait_ge(head_cols, hh + 1)
                        for d in range(2):
                            last = G.tensor_tensor(g_kd[:, d, :, :], g_kt, wide(g_head[:, 3, :, d], P), ALU.mult)
                        last.then_inc(kd_done, 1)
                        pool.wait_ge(qk_ready, hh * 2 + 2)
                        for d in range(2):
                            G.tensor_tensor(g_eq[:, d, :], g_eq[:, d, :], g_qkv2[:, j % 2, 0, :], ALU.mult).then_inc(qe_done, 1)

            def gqa(l):
                pool.wait_ge(h_ready, KT * (2 * l + 1))
                pool.dma_start(q_kall[:, :, P:P + PAST], I["cache_k"]).then_inc(cache_in, 16)
                pool.dma_start(q_vall[:, :, 1, :], I["cache_v"]).then_inc(cache_in, 16)
                scale_residual(2 * l)
                pool.wait_ge(at_normed, 10)
                pool.wait_ge(raw_ev, 12)
                pool.dma_start(O["cache_k"], q_qkv[:, 8:10, CTXS]).then_inc(cache_out, 16)
                pool.dma_start(O["cache_v"], q_qkv[:, 10:12, CTXS]).then_inc(cache_out, 16)
                pool.wait_ge(cache_out, 16 * 2)

            def mla(l):
                pool.wait_ge(h_ready, KT * (2 * l + 1))
                pool.dma_start(m_ckv[:, :, P:P + PAST], I["cache_ckv"]).then_inc(cache_in, 16)
                pool.dma_start(m_krall[0:64, P:P + PAST], I["cache_kr"]).then_inc(cache_in, 16)
                scale_residual(2 * l)
                pool.wait_ge(at_normed, 10 + 6)
                pool.wait_ge(raw_ev, 12 + 7)
                pool.dma_start(O["cache_ckv"], m_c[:, 4:6, CTXS]).then_inc(cache_out, 16)
                pool.dma_start(O["cache_kr"], m_kr[0:64, CTXS]).then_inc(cache_out, 16)
                pool.wait_ge(cache_out, 16 * 4)

            def moe(l):
                pool.wait_ge(h_ready, KT * (2 * l + 2))
                G.memset(bufo[:, :, :], 0.0).then_inc(o_zero, 1)
                scale_residual(2 * l + 1)

            pool.dma_start(con[:, :], I["consts"]).then_inc(consts_in, 16)
            pool.dma_start(bufx[:, :, :], I["x"]).then_inc(x_in, 16)
            for l, kind in enumerate(KINDS):
                {"gdn": gdn, "gqa": gqa, "mla": mla}[kind](l)
                moe(l)


INPUTS = ["x", "state", "cache_k", "cache_v", "cache_ckv", "cache_kr", "params", "consts", "w_ada", "gdn_w_in",
          "gdn_w_out", "gqa_w_in", "gqa_w_out", "mla_w_in", "mla_w_kr", "mla_w_q_up", "mla_w_kv_up", "mla_w_out", "moe"]
OUTPUTS = {"y": (P, KT, T), "state": (2 * H, P, 2, P), "cache_k": (P, 2, P), "cache_v": (P, 2, P),
           "cache_ckv": (P, 2, P), "cache_kr": (P // 2, P)}


def layout(x_prompt, x_sample, state_gdn, cache_gqa_k, cache_gqa_v, cache_mla_ckv, cache_mla_krope,
           c, c_ctx, w_ada, b_ada, ln_mix_g, ln_mix_b, ln_ffn_g, ln_ffn_b,
           gdn_w_in, gdn_conv, gdn_a_log, gdn_dt_bias, gdn_norm_g, gdn_w_out,
           gqa_w_in, gqa_q_norm, gqa_k_norm, gqa_w_out,
           mla_w_in, mla_q_norm, mla_kv_norm, mla_w_q_up, mla_w_kv_up, mla_w_out,
           router_w, router_b, moe_w_gate, moe_w_up, moe_w_down):
    cc = np.ascontiguousarray

    def units(w, width=2 * P):
        w = w.reshape(-1, w.shape[-2] // P, P, w.shape[-1] // width, width // P, P)
        return cc(w.transpose(0, 3, 2, 4, 1, 5)).reshape(w.shape[0] * w.shape[3], P, -1)

    def feat(a):
        return a.reshape(-1, P).T

    x = np.concatenate([x_prompt[0], x_sample[0]], axis=0).T.reshape(KT, P, T).transpose(1, 0, 2)
    hd = H * P
    per_head = [gdn_w_in[:, :, o * hd:(o + 1) * hd].reshape(2, D, H, P) for o in range(4)]
    w_in = np.stack(per_head, axis=3).reshape(2, D, H * 4 * P)
    w_ab = gdn_w_in[:, :, 4 * hd:].reshape(2, KT, P, 32).transpose(2, 0, 1, 3).reshape(P, -1)
    taps = gdn_conv.reshape(2, TAPS, 3, H, P).transpose(4, 0, 3, 2, 1).reshape(P, -1)
    rows = lambda a: np.broadcast_to(a.reshape(1, -1), (P, a.size))
    ln = lambda m, f: feat(np.stack([m, f], axis=1))
    params = np.concatenate([
        np.stack([feat(c_ctx), feat(c[0])], axis=2).reshape(P, -1), feat(b_ada),
        ln(ln_mix_g, ln_ffn_g), ln(ln_mix_b, ln_ffn_b), taps, feat(gdn_norm_g), feat(gqa_q_norm), feat(gqa_k_norm),
        feat(mla_q_norm), feat(mla_kv_norm), router_w.reshape(KT, P, NE).transpose(1, 0, 2).reshape(P, -1),
        rows(router_b), rows(gdn_a_log), rows(gdn_dt_bias), w_ab], axis=1)
    gate = moe_w_gate.reshape(DEPTH * NE, KT, P, DE)
    up = moe_w_up.reshape(DEPTH * NE, KT, P, DE)
    gate_up = np.concatenate([gate, up], axis=3).transpose(0, 2, 1, 3).reshape(DEPTH * NE, P, -1)
    down = moe_w_down.reshape(DEPTH * NE, 2, P, D).transpose(0, 2, 1, 3).reshape(DEPTH * NE, P, -1)
    ada = cc(w_ada.reshape(DEPTH, KT, P, ADA_UNITS, 2 * P).transpose(0, 3, 2, 1, 4)).reshape(DEPTH * ADA_UNITS, P, -1)
    q_up = mla_w_q_up[0].reshape(4, P, 4, 2, 192).transpose(2, 1, 3, 0, 4).reshape(4, P, -1)
    kv_up = mla_w_kv_up[0].reshape(2, P, 2, 4, 2, P).transpose(2, 1, 0, 4, 3, 5).reshape(2, P, -1)
    return {
        "x": cc(x), "params": cc(params), "consts": const_table(),
        "state": cc(state_gdn[0].transpose(0, 2, 3, 1, 4).reshape(2 * H, P, 2, P)),
        "cache_k": cc(cache_gqa_k[0, 0].transpose(2, 1, 0)), "cache_v": cc(cache_gqa_v[0, 0]),
        "cache_ckv": cc(cache_mla_ckv[0, 0].reshape(PAST, 2, P).transpose(2, 1, 0)),
        "cache_kr": cc(cache_mla_krope[0, 0].T),
        "w_ada": ada, "gdn_w_in": units(w_in), "gdn_w_out": units(gdn_w_out), "gqa_w_in": units(gqa_w_in),
        "gqa_w_out": units(gqa_w_out), "mla_w_in": units(mla_w_in[:, :, :6 * P]),
        "mla_w_kr": cc(mla_w_in[0, :, 6 * P:].reshape(KT, P, 64).transpose(1, 0, 2).reshape(P, -1)),
        "mla_w_q_up": cc(q_up), "mla_w_kv_up": cc(kv_up), "mla_w_out": units(mla_w_out),
        "moe": cc(np.concatenate([gate_up, down], axis=2)),
    }


def kernel(**inputs):
    from concourse import bacc
    from concourse.bass_utils import run_bass_kernel_spmd

    arrays = layout(**{k: np.asarray(a) for k, a in inputs.items()})
    nc = bacc.Bacc("TRN2", target_bir_lowering=False, num_devices=1)
    given = {n: nc.dram_tensor(f"in_{n}", arrays[n].shape, F32, kind="ExternalInput").ap() for n in INPUTS}
    made = {n: nc.dram_tensor(f"out_{n}", s, F32, kind="ExternalOutput").ap() for n, s in OUTPUTS.items()}
    trunk(nc, given, made)
    r = run_bass_kernel_spmd(nc, [{f"in_{n}": arrays[n] for n in INPUTS}], core_ids=[0]).results[0]
    y = r["out_y"].transpose(1, 0, 2).reshape(D, T).T
    state = r["out_state"].reshape(2, H, P, 2, P).transpose(0, 3, 1, 2, 4)[None]
    cache_k = r["out_cache_k"].transpose(2, 1, 0)[None, None]
    cache_v = r["out_cache_v"].transpose(2, 1, 0)[None, None]
    ckv = r["out_cache_ckv"].transpose(2, 1, 0).reshape(P, 2 * P)[None, None]
    kr = r["out_cache_kr"].T[None, None]
    return y[None, :CTX], y[None, CTX:], state, cache_k, cache_v, ckv, kr
```
